# Optimizing a Trainium2 kernel written in Bass

```python
import math
import jax, jax.numpy as jnp
from jax import lax
import numpy as np

D_MODEL = 1024
BATCH = 1
SEQ = 1024
DEPTH = 1
DEC_BATCH = 1
DEC_SEQ = 32
PAST_LEN = 2048

CHUNK = 64
N_META = 16
QBLOCK = 128
SB_HEADS = 8
SB_DIM = 64
SB_WIDTH = SB_HEADS * SB_DIM
DF_HEADS = 4
DF_DIM = 64
DF_VDIM = 2 * DF_DIM
DF_QK = 2 * DF_HEADS * DF_DIM
DF_WIDTH = DF_HEADS * DF_VDIM
MIX_WIDTH = SB_WIDTH + DF_WIDTH
IN_COLS = 3 * SB_WIDTH + 2 * DF_QK + DF_WIDTH
ROPE_THETA = 500000.0
ROT_DIM = DF_DIM // 4
N_GROUPS = 4
EXPERTS_PER_GROUP = 8
N_EXPERTS = N_GROUPS * EXPERTS_PER_GROUP
TOP_K_IN_GROUP = 2
D_EXPERT = 256
EPS = 1e-6

kernel_name = 'hymba_stickbreak_diffattn_hmoe_stream_step'

def lambda_init(layer_idx):
    return 0.8 - 0.6 * math.exp(-0.3 * layer_idx)

def rms_norm(x, g):
    xf = x.astype(jnp.float32)
    y = xf * lax.rsqrt(jnp.mean(xf * xf, axis=-1, keepdims=True) + EPS)
    return (y * g.astype(jnp.float32)).astype(x.dtype)

def partial_rope(x, pos):
    half = ROT_DIM // 2
    inv = ROPE_THETA ** (-jnp.arange(half, dtype=jnp.float32) * 2.0 / ROT_DIM)
    ang = pos.astype(jnp.float32)[:, None] * inv[None, :]
    cos = jnp.cos(ang)[None, :, None, :]
    sin = jnp.sin(ang)[None, :, None, :]
    xf = x.astype(jnp.float32)
    x1, x2 = xf[..., :half], xf[..., half:ROT_DIM]
    out = jnp.concatenate([x1 * cos - x2 * sin, x2 * cos + x1 * sin, xf[..., ROT_DIM:]], axis=-1)
    return out.astype(x.dtype)

def project(xn, w_in, pos):
    B, T, _ = xn.shape
    proj = jnp.einsum('btd,dc->btc', xn, w_in)
    idx = [SB_WIDTH, 2 * SB_WIDTH, 3 * SB_WIDTH, 3 * SB_WIDTH + DF_QK, 3 * SB_WIDTH + 2 * DF_QK]
    sb_q, sb_k, sb_v, df_q, df_k, df_v = jnp.split(proj, idx, axis=-1)
    sb_q = sb_q.reshape(B, T, SB_HEADS, SB_DIM)
    sb_k = sb_k.reshape(B, T, SB_HEADS, SB_DIM)
    sb_v = sb_v.reshape(B, T, SB_HEADS, SB_DIM)
    df_q = partial_rope(df_q.reshape(B, T, 2 * DF_HEADS, DF_DIM), pos)
    df_k = partial_rope(df_k.reshape(B, T, 2 * DF_HEADS, DF_DIM), pos)
    df_v = df_v.reshape(B, T, DF_HEADS, DF_VDIM)
    return sb_q, sb_k, sb_v, df_q, df_k, df_v

def stick_breaking_block(q, k, v, q_pos, k_pos):
    z = jnp.einsum('bqhd,bkhd->bhqk', q, k, preferred_element_type=jnp.float32) * (SB_DIM ** -0.5)
    visible = (k_pos[None, :] < q_pos[:, None])[None, None]
    log_keep = jnp.where(visible, -jax.nn.softplus(z), 0.0)
    between = lax.cumsum(log_keep, axis=3, reverse=True) - log_keep
    w = jnp.where(visible, jnp.exp(jax.nn.log_sigmoid(z) + between), 0.0)
    return jnp.einsum('bhqk,bkhd->bqhd', w, v.astype(jnp.float32))

def diff_attn_block(q, k, v, q_chunk, k_chunk, lam, subln_g, lam_init):
    s = jnp.einsum('bqhd,bkhd->bhqk', q, k, preferred_element_type=jnp.float32) * (DF_DIM ** -0.5)
    visible = (k_chunk[None, :] <= q_chunk[:, None])[None, None]
    p = jax.nn.softmax(jnp.where(visible, s, -jnp.inf), axis=-1)
    B, _, Q, K = p.shape
    p = p.reshape(B, DF_HEADS, 2, Q, K)
    a = p[:, :, 0] - lam * p[:, :, 1]
    o = jnp.einsum('bhqk,bkhe->bqhe', a, v.astype(jnp.float32))
    return rms_norm(o, subln_g) * (1.0 - lam_init)

def token_mixers(sb_q, df_q, keys, q_pos, q_chunk, k_pos, k_chunk, lam, subln_g, lam_init):
    sb_k, sb_v, df_k, df_v = keys

    def block(args):
        sbq, dfq, qp, qc = args
        Bq, Qb = sbq.shape[:2]
        o_sb = stick_breaking_block(sbq, sb_k, sb_v, qp, k_pos)
        o_df = diff_attn_block(dfq, df_k, df_v, qc, k_chunk, lam, subln_g, lam_init)
        out = jnp.concatenate([o_sb.reshape(Bq, Qb, SB_WIDTH), o_df.reshape(Bq, Qb, DF_WIDTH)], axis=-1)
        return out.astype(sbq.dtype)

    B, T = sb_q.shape[:2]
    if T <= QBLOCK:
        return block((sb_q, df_q, q_pos, q_chunk))
    nb = -(-T // QBLOCK)
    pad = nb * QBLOCK - T

    def to_blocks(a):
        a = jnp.pad(a, ((0, 0), (0, pad), (0, 0), (0, 0)))
        return jnp.moveaxis(a.reshape(B, nb, QBLOCK, *a.shape[2:]), 1, 0)

    qp = jnp.pad(q_pos, (0, pad), mode='edge').reshape(nb, QBLOCK)
    qc = jnp.pad(q_chunk, (0, pad), mode='edge').reshape(nb, QBLOCK)
    out = lax.map(block, (to_blocks(sb_q), to_blocks(df_q), qp, qc))
    return jnp.moveaxis(out, 0, 1).reshape(B, nb * QBLOCK, MIX_WIDTH)[:, :T]

def hier_moe(xn, w_group, b_group, w_router, b_router, w_gate, w_up, w_down):
    shape = xn.shape
    xf = xn.reshape(-1, D_MODEL)
    T = xf.shape[0]
    g_logits = jnp.einsum('td,dg->tg', xf, w_group, preferred_element_type=jnp.float32) + b_group.astype(jnp.float32)
    g_prob = jax.nn.softmax(g_logits, axis=-1)
    g_idx = jnp.argmax(g_logits, axis=-1)
    g_w = jnp.take_along_axis(g_prob, g_idx[:, None], axis=1)
    e_logits = jnp.einsum('td,de->te', xf, w_router, preferred_element_type=jnp.float32) + b_router.astype(jnp.float32)
    e_logits = e_logits.reshape(T, N_GROUPS, EXPERTS_PER_GROUP)
    e_logits = jnp.take_along_axis(e_logits, g_idx[:, None, None], axis=1)[:, 0]
    top_p, top_i = lax.top_k(jax.nn.softmax(e_logits, axis=-1), TOP_K_IN_GROUP)
    top_p = top_p / jnp.sum(top_p, axis=-1, keepdims=True)
    expert_id = g_idx[:, None] * EXPERTS_PER_GROUP + top_i
    gates = jnp.sum(jax.nn.one_hot(expert_id, N_EXPERTS, dtype=jnp.float32) * (g_w * top_p)[..., None], axis=1)

    def expert(acc, ew):
        wg, wu, wd, gate = ew
        h = jax.nn.silu(xf @ wg) * (xf @ wu)
        return acc + (h @ wd).astype(jnp.float32) * gate[:, None], None

    acc, _ = lax.scan(expert, jnp.zeros((T, D_MODEL), jnp.float32), (w_gate, w_up, w_down, gates.T))
    return acc.astype(xn.dtype).reshape(shape)

def layer_step(h, q_pos, q_chunk, past, past_pos, past_chunk, norm_mix_g, w_in, lam, subln_g, lam_init,
               w_out, norm_ffn_g, w_group, b_group, w_router, b_router, w_gate, w_up, w_down):
    xn = rms_norm(h, norm_mix_g)
    sb_q, sb_k, sb_v, df_q, df_k, df_v = project(xn, w_in, q_pos)
    new_rows = (sb_k, sb_v, df_k, df_v)
    if past is None:
        keys, k_pos, k_chunk = new_rows, q_pos, q_chunk
    else:
        keys = tuple(jnp.concatenate([c.astype(n.dtype), n], axis=1) for c, n in zip(past, new_rows))
        k_pos = jnp.concatenate([past_pos, q_pos])
        k_chunk = jnp.concatenate([past_chunk, q_chunk])
    mix = token_mixers(sb_q, df_q, keys, q_pos, q_chunk, k_pos, k_chunk, lam, subln_g, lam_init)
    h = h + jnp.einsum('btc,cd->btd', mix, w_out)
    h = h + hier_moe(rms_norm(h, norm_ffn_g), w_group, b_group, w_router, b_router, w_gate, w_up, w_down)
    return h, new_rows

def setup_inputs(seed: int = 0) -> dict:
    key = jax.random.key(seed)
    ks = jax.random.split(key, 24)
    f32 = jnp.float32
    nrm = lambda k, shape, s=1.0: (jax.random.normal(k, shape, f32) * s)
    return {
        'x_prompt': nrm(ks[0], (BATCH, SEQ, D_MODEL)),
        'x_sample': nrm(ks[1], (DEC_BATCH, DEC_SEQ, D_MODEL)),
        'cache_sb_k': nrm(ks[2], (DEPTH, DEC_BATCH, PAST_LEN, SB_HEADS, SB_DIM)),
        'cache_sb_v': nrm(ks[3], (DEPTH, DEC_BATCH, PAST_LEN, SB_HEADS, SB_DIM)),
        'cache_diff_k': nrm(ks[4], (DEPTH, DEC_BATCH, PAST_LEN, 2 * DF_HEADS, DF_DIM)),
        'cache_diff_v': nrm(ks[5], (DEPTH, DEC_BATCH, PAST_LEN, DF_HEADS, DF_VDIM)),
        'meta_tokens': nrm(ks[6], (N_META, D_MODEL)),
        'norm_mix_g': 1.0 + nrm(ks[7], (DEPTH, D_MODEL), 0.02),
        'w_in': nrm(ks[8], (DEPTH, D_MODEL, IN_COLS), D_MODEL ** -0.5),
        'lambda_q1': nrm(ks[9], (DEPTH, DF_DIM), 0.1),
        'lambda_k1': nrm(ks[10], (DEPTH, DF_DIM), 0.1),
        'lambda_q2': nrm(ks[11], (DEPTH, DF_DIM), 0.1),
        'lambda_k2': nrm(ks[12], (DEPTH, DF_DIM), 0.1),
        'subln_g': 1.0 + nrm(ks[13], (DEPTH, DF_VDIM), 0.02),
        'w_out': nrm(ks[14], (DEPTH, MIX_WIDTH, D_MODEL), MIX_WIDTH ** -0.5),
        'norm_ffn_g': 1.0 + nrm(ks[15], (DEPTH, D_MODEL), 0.02),
        'w_group': nrm(ks[16], (DEPTH, D_MODEL, N_GROUPS), D_MODEL ** -0.5),
        'b_group': nrm(ks[17], (DEPTH, N_GROUPS), 0.01),
        'w_router': nrm(ks[18], (DEPTH, D_MODEL, N_EXPERTS), D_MODEL ** -0.5),
        'b_router': nrm(ks[19], (DEPTH, N_EXPERTS), 0.01),
        'w_gate': nrm(ks[20], (DEPTH, N_EXPERTS, D_MODEL, D_EXPERT), D_MODEL ** -0.5),
        'w_up': nrm(ks[21], (DEPTH, N_EXPERTS, D_MODEL, D_EXPERT), D_MODEL ** -0.5),
        'w_down': nrm(ks[22], (DEPTH, N_EXPERTS, D_EXPERT, D_MODEL), D_EXPERT ** -0.5),
        'final_norm_g': 1.0 + nrm(ks[23], (D_MODEL,), 0.02),
    }

def reference(x_prompt, x_sample, cache_sb_k, cache_sb_v, cache_diff_k, cache_diff_v, meta_tokens,
              norm_mix_g, w_in, lambda_q1, lambda_k1, lambda_q2, lambda_k2, subln_g, w_out, norm_ffn_g,
              w_group, b_group, w_router, b_router, w_gate, w_up, w_down, final_norm_g):
    B, S, _ = x_prompt.shape
    Bs, Ss, _ = x_sample.shape
    past_len = cache_sb_k.shape[2]
    h_p = jnp.concatenate([jnp.broadcast_to(meta_tokens.astype(x_prompt.dtype)[None], (B, N_META, D_MODEL)), x_prompt], axis=1)
    pos_p = jnp.arange(N_META + S, dtype=jnp.int32)
    chunk_p = (pos_p - N_META) // CHUNK
    pos_s = past_len + jnp.arange(Ss, dtype=jnp.int32)
    chunk_s = pos_s // CHUNK
    past_pos = jnp.arange(past_len, dtype=jnp.int32)
    past_chunk = past_pos // CHUNK
    h_s = x_sample
    rows_p, rows_s = [], []
    for l in range(DEPTH):
        lam = (jnp.exp(jnp.sum(lambda_q1[l].astype(jnp.float32) * lambda_k1[l].astype(jnp.float32)))
               - jnp.exp(jnp.sum(lambda_q2[l].astype(jnp.float32) * lambda_k2[l].astype(jnp.float32)))
               + lambda_init(l))
        shared = (norm_mix_g[l], w_in[l], lam, subln_g[l], lambda_init(l), w_out[l], norm_ffn_g[l],
                  w_group[l], b_group[l], w_router[l], b_router[l], w_gate[l], w_up[l], w_down[l])
        h_p, new_p = layer_step(h_p, pos_p, chunk_p, None, None, None, *shared)
        past = (cache_sb_k[l], cache_sb_v[l], cache_diff_k[l], cache_diff_v[l])
        h_s, new_s = layer_step(h_s, pos_s, chunk_s, past, past_pos, past_chunk, *shared)
        rows_p.append(new_p)
        rows_s.append(new_s)
    y_prompt = rms_norm(h_p, final_norm_g)[:, N_META:]
    y_sample = rms_norm(h_s, final_norm_g)
    sb_k_prompt = jnp.stack([r[0] for r in rows_p])
    sb_v_prompt = jnp.stack([r[1] for r in rows_p])
    diff_k_prompt = jnp.stack([r[2] for r in rows_p])
    diff_v_prompt = jnp.stack([r[3] for r in rows_p])
    sb_k_sample = jnp.stack([r[0] for r in rows_s])
    sb_v_sample = jnp.stack([r[1] for r in rows_s])
    diff_k_sample = jnp.stack([r[2] for r in rows_s])
    diff_v_sample = jnp.stack([r[3] for r in rows_s])
    return (y_prompt, y_sample, sb_k_prompt, sb_v_prompt, diff_k_prompt, diff_v_prompt,
            sb_k_sample, sb_v_sample, diff_k_sample, diff_v_sample)


_drawn_inputs = setup_inputs


def setup_inputs(seed=0):
    import zlib

    import numpy as np

    out = dict(_drawn_inputs(seed))
    spreads = {}
    factors = {'lambda_q1': 3.285,
     'lambda_k1': 8.0,
     'subln_g': 3.434,
     'b_group': 12.538,
     'b_router': 11.386,
     'final_norm_g': 8.447,
     'cache_sb_k': 2.667,
     'lambda_k2': 3.675,
     'norm_ffn_g': 3.39}
    for name, (base, spread) in spreads.items():
        noise = np.random.default_rng([zlib.crc32(name.encode()), seed]).standard_normal(out[name].shape)
        drawn = base * np.exp(spread * noise) if base else spread * noise
        out[name] = __import__('jax').numpy.asarray(drawn.astype(out[name].dtype))
    for name, factor in factors.items():
        out[name] = (out[name] * factor).astype(out[name].dtype)
    return out
```

```python
from contextlib import ExitStack

import numpy as np

import concourse.bass as bass
from concourse import mybir

P = 128
F32 = mybir.dt.float32
BF16 = mybir.dt.bfloat16
I32 = mybir.dt.int32
U32 = mybir.dt.uint32
ALU = mybir.AluOpType
ACT = mybir.ActivationFunctionType
AX_X = mybir.AxisListType.X
ds = bass.ds

D = 1024
KC = D // P
SEQ = 1024
META = 16
CHUNK = 64
NS = 32
PAST = 2048
NPR = META + SEQ
FULL = NPR // P
TAIL = NPR - FULL * P
NT = FULL + 1
LAST = NS + TAIL
NTOK = FULL * P + LAST
SBH, SBD = 8, 64
DFH, DFD, DFV = 4, 64, 128
HP = 4
EPS = 1e-6
QSCALE = 0.125
LAM_INIT = 0.2
NEG = -1e30
LN_CAP = 44.0
NG, EPG, NE, DE = 4, 8, 32, 256
EC = DE // P
MAXT = NE + (2 * NTOK) // P
NSLOT = (MAXT + 1) * P
WRING = 4


def rows_of(t):
    return P if t < FULL else LAST


def shape_constants():
    q = np.arange(P)[:, None]
    k = np.arange(P)[None, :]
    c = {}
    c["ident"] = (q == k).astype(np.float32)
    c["sb_mask"] = np.where(k < q, 0.0, NEG).astype(np.float32)
    reach = np.where(q < META, META, np.where(q < META + CHUNK, META + CHUNK, META + 2 * CHUNK))
    c["df_mask"] = np.where(np.arange(P + META)[None, :] < reach, 0.0, NEG).astype(np.float32)
    c["new_mask"] = np.where(np.arange(NS)[None, :] < q % NS, 0.0, NEG).astype(np.float32)
    c["before"] = (q < k).astype(np.float32)
    c["ones"] = np.ones((P, P), np.float32)
    half = DFD // 8
    inv = np.float32(500000.0) ** (-np.arange(half, dtype=np.float32) * np.float32(2.0) / np.float32(2 * half))
    pos = np.zeros((P, NT), np.float32)
    for t in range(FULL):
        pos[:, t] = P * t + np.arange(P)
    pos[:NS, FULL] = PAST + np.arange(NS)
    pos[NS:LAST, FULL] = FULL * P + np.arange(TAIL)
    ang = (pos[:, :, None] * inv.astype(np.float32)[None, None, :]).astype(np.float32)
    c["cos"] = np.concatenate([np.cos(ang)] * 2, 2).reshape(P, -1).astype(np.float32)
    c["sin"] = np.concatenate([np.sin(ang)] * 2, 2).reshape(P, -1).astype(np.float32)
    valid = np.ones((P, NT), np.float32)
    valid[LAST:, FULL] = 0
    c["valid"] = valid
    c["token"] = (P * np.arange(NT)[None, :] + q).astype(np.float32)
    c["iota"] = np.broadcast_to(np.arange(MAXT + 1, dtype=np.float32), (P, MAXT + 1)).copy()
    c["fold"] = ((q // 64 == k[:, :64] // 32) & (q % 32 == k[:, :64] % 32)).astype(np.float32)
    c["first_map"] = ((q // 32) % 2 == 0).astype(np.float32)
    c["neg_half"] = np.full((P, NT), -0.5, np.float32)
    return c


CONST = {}
_at = 0
for _n, _a in shape_constants().items():
    CONST[_n] = (_at, _a.shape[1])
    _at += _a.shape[1]
NCONST = _at


def build(nc, A):
    with ExitStack() as keep:
        g = {}

        def sb(stack, name, shape, dt=F32):
            return stack.enter_context(nc.sbuf_tensor(name, shape, dt))

        def sem(stack, name):
            return stack.enter_context(nc.semaphore(name))

        g["const"] = sb(keep, "const", [P, NCONST])
        for n, (a, w) in CONST.items():
            g[n] = g["const"][:, a:a + w]
        g["lam"] = sb(keep, "lam", [P, 8])
        g["mixd"] = nc.dram_tensor("mix_scratch", [NTOK, D], F32).ap()
        g["xn2d"] = nc.dram_tensor("normed_scratch", [NTOK, D], F32).ap()
        g["slotd"] = nc.dram_tensor("token_of_slot", [NSLOT, 1], I32).ap()
        g["ysd"] = nc.dram_tensor("expert_rows", [MAXT * P, D], F32).ap()
        g["stores"] = sem(keep, "stores")
        with ExitStack() as att:
            for n in ("sb", "df"):
                g["kT_" + n] = sb(att, "kT_" + n, [P, HP, NPR])
                g["kTnew_" + n] = sb(att, "kTnew_" + n, [P, HP, NS])
                g["v_" + n] = sb(att, "v_" + n, [P, FULL, 512])
                g["vtail_" + n] = sb(att, "vtail_" + n, [P, 512])
                g["vnew_" + n] = sb(att, "vnew_" + n, [P, 512])
                for w in ("tail", "samp"):
                    g[f"qs_{n}_{w}"] = sb(att, f"qs_{n}_{w}", [P, HP, P])
            with ExitStack() as qs:
                for n in ("sb", "df"):
                    g["qT_" + n] = sb(qs, "qT_" + n, [P, HP, FULL * P])
                with ExitStack() as st:
                    n_stores = project(nc, A, g, st, sb, sem)
                with ExitStack() as st:
                    attend(nc, A, g, st, sb, sem, n_stores)
            with ExitStack() as st:
                stacked(nc, A, g, st, sb, sem)
        g["h"] = sb(keep, "h", [P, NT, D])
        g["gates"] = sb(keep, "gates", [P, NT, 2])
        g["slot"] = sb(keep, "slot", [P, 2, NT], I32)
        g["tile_expert"] = sb(keep, "tile_expert", [1, MAXT + 1], I32)
        g["n_tiles"] = sb(keep, "n_tiles", [1, 2], I32)
        g["logits"] = sb(keep, "logits", [P, NT, NG + NE])
        with ExitStack() as st:
            mix_out(nc, A, g, st, sb, sem)
        with ExitStack() as st:
            route(nc, A, g, st, sb, sem, n_stores)
        with ExitStack() as st:
            experts(nc, A, g, st, sb, sem)
        with ExitStack() as st:
            combine(nc, A, g, st, sb, sem, n_stores)


def project(nc, A, g, st, sb, sem):
    KINDS = [("sb", "q"), ("sb", "k"), ("sb", "v"), ("df", "q"), ("df", "k"), ("df", "v")]
    units = [(cb, t) for cb in range(6) for t in range(NT)]
    qk_units = [u for u, (cb, t) in enumerate(units) if KINDS[cb][1] != "v"]
    qk_of = {u: n for n, u in enumerate(qk_units)}
    rope_of = {u: n for n, u in enumerate([u for u in qk_units if KINDS[units[u][0]][0] == "df"])}
    NAT = 2

    def stores_of_slot(u):
        n, count = qk_of[u], 0
        for m in range(n % NAT, n, NAT):
            cb, t = units[qk_units[m]]
            if KINDS[cb][1] == "k":
                count += 2 if t == FULL else 1
        return count

    xt = [sb(st, f"x{i}", [P, D]) for i in range(2)]
    xn = sb(st, "xn", [P, D])
    gmix = sb(st, "gmix", [P, D])
    junk = sb(st, "junk", [P, D], BF16)
    xnT = sb(st, "xnT", [P, KC, NTOK])
    w = [sb(st, f"w{i}", [P, KC, 512]) for i in range(2)]
    nat = [sb(st, f"nat{i}", [P, 512]) for i in range(NAT)]
    rot = sb(st, "rot", [P, 2, 8, 16])
    ss = sb(st, "ss", [P, NT])
    rstd = sb(st, "rstd", [P, NT])
    lamv = sb(st, "lamv", [P, 4, DFD])
    psX = st.enter_context(nc.psum_tensor("psX", [P, 2, 512], F32))
    psP = st.enter_context(nc.psum_tensor("psP", [P, 4, 512], F32))
    psQ = st.enter_context(nc.psum_tensor("psQ", [P, 2, 512], F32))

    const_in, gmix_in, lam_in = sem(st, "const_in"), sem(st, "gmix_in"), sem(st, "lam_in")
    x_in = [sem(st, f"x_in{i}") for i in range(2)]
    w_in = [sem(st, f"w_in{i}") for i in range(2)]
    squared, rstd_ready, xn_ready = sem(st, "squared"), sem(st, "rstd_ready"), sem(st, "xn_ready")
    xT_full, xT_kept_act, xT_kept_dve = sem(st, "xT_full"), sem(st, "xT_kept_act"), sem(st, "xT_kept_dve")
    proj_full, proj_kept = sem(st, "proj_full"), sem(st, "proj_kept")
    rope_done, qT_full, qT_kept = sem(st, "rope_done"), sem(st, "qT_full"), sem(st, "qT_kept")
    nat_stored = [sem(st, f"nat_stored{i}") for i in range(NAT)]
    dve_own, pool_own = sem(st, "dve_own"), sem(st, "pool_own")
    lam_sum, lam_exp = sem(st, "lam_sum"), sem(st, "lam_exp")
    n_stores = [0]

    x_rows = A["x_prompt"].rearrange("a s d -> (a s) d")
    xs_rows = A["x_sample"].rearrange("a s d -> (a s) d")
    w_dram = A["w_in"][0].rearrange("(c p) n -> p c n", p=P)

    def x_loads(t):
        return sum(2 if s in (0, FULL) else 1 for s in range(t % 2, t + 1, 2))

    blk = st.enter_context(nc.Block())

    @blk.sync
    def _(sp):
        def load_x(t):
            if t >= 2:
                sp.wait_ge(xn_ready, t - 1)
            if t == 0:
                sp.dma_start(xt[0][0:META, :], A["meta_tokens"]).then_inc(x_in[0], 16)
                sp.dma_start(xt[0][META:P, :], x_rows[0:P - META, :]).then_inc(x_in[0], 16)
            elif t < FULL:
                sp.dma_start(xt[t % 2][:, :], x_rows[P * t - META:P * t + P - META, :]).then_inc(x_in[t % 2], 16)
            else:
                sp.dma_start(xt[t % 2][0:NS, :], xs_rows).then_inc(x_in[t % 2], 16)
                sp.dma_start(xt[t % 2][NS:LAST, :], x_rows[SEQ - TAIL:SEQ, :]).then_inc(x_in[t % 2], 16)

        def load_w(cb):
            if cb >= 2:
                sp.wait_ge(proj_full, NT * (cb - 1))
            for c in (0, KC // 2):
                sp.dma_start(w[cb % 2][:, c:c + KC // 2, :],
                             w_dram[:, c:c + KC // 2, 512 * cb:512 * cb + 512]).then_inc(w_in[cb % 2], 16)

        load_x(0)
        sp.dma_start(gmix[:, :], A["norm_mix_g"].broadcast_to([P, D])).then_inc(gmix_in, 16)
        sp.dma_start(g["const"][:, :], A["const"]).then_inc(const_in, 16)
        load_x(1)
        load_w(0)
        for n, name in enumerate(("lambda_q1", "lambda_k1", "lambda_q2", "lambda_k2")):
            sp.dma_start(lamv[:, n, :], A[name].broadcast_to([P, DFD])).then_inc(lam_in, 16)
        for t in range(2, NT):
            load_x(t)
        load_w(1)
        for cb in range(2, 6):
            load_w(cb)

    @blk.scalar
    def _(act):
        nc.scalar.preload_act_table_set("natural_log_exp_and_others")

        def square(t):
            m = rows_of(t)
            act.wait_ge(x_in[t % 2], 16 * x_loads(t))
            if t >= 1:
                act.wait_ge(squared, t)
            nc.scalar.activation(junk[0:m, :], xt[t % 2][0:m, :], ACT.Square,
                                 accum_out=ss[0:m, t:t + 1]).then_inc(squared, 1)

        def keep_xT(t):
            m = rows_of(t)
            act.wait_ge(xT_full, t + 1)
            nc.scalar.activation(xnT[:, 0:4, P * t:P * t + m],
                                 psX[:, 0, 0:4 * m].rearrange("p (c m) -> p c m", c=4),
                                 ACT.Copy).then_inc(xT_kept_act, 1)

        def keep_proj(u):
            cb, t = units[u]
            group, kind = KINDS[cb]
            m = rows_of(t)
            act.wait_ge(proj_full, u + 1)
            ps = psP[:, u % 4, :]
            if kind == "v":
                if t < FULL:
                    nc.scalar.activation(g["v_" + group][:, t, :], ps, ACT.Copy).then_inc(proj_kept, 1)
                else:
                    nc.scalar.activation(g["vtail_" + group][0:TAIL, :], ps[NS:LAST, :], ACT.Copy)
                    nc.scalar.activation(g["vnew_" + group][0:NS, :], ps[0:NS, :], ACT.Copy).then_inc(proj_kept, 1)
                return
            n = qk_of[u]
            if n >= NAT:
                act.wait_ge(qT_full, n - NAT + 1)
                if stores_of_slot(u):
                    act.wait_ge(nat_stored[n % NAT], 16 * stores_of_slot(u))
            nc.scalar.activation(nat[n % NAT][0:m, :], ps[0:m, :], ACT.Copy,
                                 scale=QSCALE if kind == "q" else 1.0).then_inc(proj_kept, 1)

        square(0)
        square(1)
        keep_xT(0)
        for u in range(len(units)):
            if u < NT:
                if u + 1 < NT:
                    keep_xT(u + 1)
                if u + 2 < NT:
                    square(u + 2)
            keep_proj(u)
            if u == NT:
                act.wait_ge(lam_sum, 1)
                nc.scalar.activation(g["lam"][:, 2:4], g["lam"][:, 0:2], ACT.Exp).then_inc(lam_exp, 1)

    @blk.gpsimd
    def _(pool):
        for t in range(NT):
            m = rows_of(t)
            pool.wait_ge(squared, t + 1)
            nc.gpsimd.tensor_scalar(ss[0:m, t:t + 1], ss[0:m, t:t + 1], 1.0 / D, EPS, ALU.mult, ALU.add) \
                .then_inc(pool_own, 1)
            if t == 0:
                pool.wait_ge(const_in, 16)
            pool.wait_ge(pool_own, t + 1)
            nc.gpsimd.tensor_tensor(rstd[0:m, t:t + 1], ss[0:m, t:t + 1], g["neg_half"][0:m, 0:1], ALU.pow) \
                .then_inc(rstd_ready, 1)
        k_out = {"sb": ("sb_k_prompt", "sb_k_sample"), "df": ("diff_k_prompt", "diff_k_sample")}
        v_out = {"sb": ("sb_v_prompt", "sb_v_sample"), "df": ("diff_v_prompt", "diff_v_sample")}
        for u, (cb, t) in enumerate(units):
            group, kind = KINDS[cb]
            if kind == "q":
                continue
            names = (k_out if kind == "k" else v_out)[group]
            prompt, samp = (A[n].rearrange("l b t h d -> (l b t) (h d)") for n in names)
            if kind == "k" and group == "df":
                pool.wait_ge(rope_done, rope_of[u] + 1)
            else:
                pool.wait_ge(proj_kept, u + 1)
            if kind == "v":
                done = g["stores"]
                if t < FULL:
                    pool.dma_start(prompt[P * t:P * t + P, :], g["v_" + group][:, t, :]).then_inc(done, 16)
                    n_stores[0] += 1
                else:
                    pool.dma_start(samp, g["vnew_" + group][0:NS, :]).then_inc(done, 16)
                    pool.dma_start(prompt[FULL * P:NPR, :], g["vtail_" + group][0:TAIL, :]).then_inc(done, 16)
                    n_stores[0] += 2
            else:
                n = qk_of[u] % NAT
                if t < FULL:
                    pool.dma_start(prompt[P * t:P * t + P, :], nat[n][:, :]).then_inc(nat_stored[n], 16)
                else:
                    pool.dma_start(samp, nat[n][0:NS, :]).then_inc(nat_stored[n], 16)
                    pool.dma_start(prompt[FULL * P:NPR, :], nat[n][NS:LAST, :]).then_inc(nat_stored[n], 16)
        for n in range(NAT):
            total = sum((2 if units[u][1] == FULL else 1) for u in qk_units
                        if qk_of[u] % NAT == n and KINDS[units[u][0]][1] == "k")
            pool.wait_ge(nat_stored[n], 16 * total)

    @blk.vector
    def _(dve):
        own = [0]

        def then(ins):
            own[0] += 1
            ins.then_inc(dve_own, 1)
            dve.wait_ge(dve_own, own[0])

        def normalise(t):
            m = rows_of(t)
            dve.wait_ge(rstd_ready, t + 1)
            if t >= 1:
                dve.wait_ge(xT_full, t)
            nc.vector.scalar_tensor_tensor(xn[0:m, :], xt[t % 2][0:m, :], rstd[0:m, t:t + 1], gmix[0:m, :],
                                           ALU.mult, ALU.mult).then_inc(xn_ready, 1)

        def keep_xT(t):
            m = rows_of(t)
            dve.wait_ge(xT_full, t + 1)
            nc.vector.tensor_copy(xnT[:, 4:8, P * t:P * t + m],
                                  psX[:, 1, 0:4 * m].rearrange("p (c m) -> p c m", c=4)).then_inc(xT_kept_dve, 1)

        def rope(u):
            cb, t = units[u]
            m = rows_of(t)
            dve.wait_ge(proj_kept, u + 1)
            v = nat[qk_of[u] % NAT][0:m, :].rearrange("p (h d) -> p h d", h=8)
            x = v[:, :, 0:16]
            if rope_of[u] >= 1:
                dve.wait_ge(rope_done, rope_of[u])
            cos = g["cos"][0:m, 16 * t:16 * t + 16].unsqueeze(1).to_broadcast([m, 8, 16])
            sin = g["sin"][0:m, 16 * t:16 * t + 16].unsqueeze(1).to_broadcast([m, 8, 16])
            nc.vector.tensor_tensor(rot[0:m, 0], x, cos, ALU.mult)
            then(nc.vector.tensor_tensor(rot[0:m, 1], x, sin, ALU.mult))
            nc.vector.tensor_tensor(v[:, :, 0:8], rot[0:m, 0, :, 0:8], rot[0:m, 1, :, 8:16], ALU.subtract)
            nc.vector.tensor_tensor(v[:, :, 8:16], rot[0:m, 0, :, 8:16], rot[0:m, 1, :, 0:8],
                                    ALU.add).then_inc(rope_done, 1)

        def keep_qT(u):
            cb, t = units[u]
            group, kind = KINDS[cb]
            n = qk_of[u]
            m = rows_of(t)
            dve.wait_ge(qT_full, n + 1)
            ps = psQ[:, n % 2, 0:4 * m].rearrange("p (c m) -> p c m", c=4)
            if t < FULL:
                last = nc.vector.tensor_copy(g[f"{kind}T_{group}"][:, :, P * t:P * t + P], ps)
            elif kind == "k":
                nc.vector.tensor_copy(g["kT_" + group][:, :, FULL * P:NPR], ps[:, :, NS:LAST])
                last = nc.vector.tensor_copy(g["kTnew_" + group][:, :, :], ps[:, :, 0:NS])
            else:
                for who, a, b in (("samp", 0, NS), ("tail", NS, LAST)):
                    for p in range(HP):
                        for half in range(2):
                            c = 32 * (2 * (p % 2) + half)
                            r = slice(64 * half, 64 * half + 64)
                            last = nc.vector.tensor_copy(g[f"qs_{group}_{who}"][r, p, c:c + b - a], ps[r, p, a:b])
            last.then_inc(qT_kept, 1)

        for group in ("sb", "df"):
            for who in ("samp", "tail"):
                then(nc.vector.memset(g[f"qs_{group}_{who}"][:, :, :], 0.0))
        dve.wait_ge(gmix_in, 16)
        normalise(0)
        keep_xT(0)
        normalise(1)
        dve.wait_ge(lam_in, 64)
        for n in range(2):
            then(nc.vector.tensor_tensor(lamv[:, 2 * n, :], lamv[:, 2 * n, :], lamv[:, 2 * n + 1, :], ALU.mult))
            red = nc.vector.reduce_sum(g["lam"][:, n:n + 1], lamv[:, 2 * n, :], AX_X)
        red.then_inc(lam_sum, 1)
        for u, (cb, t) in enumerate(units):
            if u < NT:
                if u + 1 < NT:
                    keep_xT(u + 1)
                if u + 2 < NT:
                    normalise(u + 2)
            if u in rope_of:
                rope(u)
            if u >= 1 and u - 1 in qk_of:
                keep_qT(u - 1)
        dve.wait_ge(lam_exp, 1)
        lam = g["lam"]
        then(nc.vector.tensor_tensor(lam[:, 5:6], lam[:, 3:4], lam[:, 2:3], ALU.subtract))
        then(nc.vector.tensor_scalar(lam[:, 4:5], lam[:, 5:6], -LAM_INIT, None, ALU.add))
        then(nc.vector.tensor_scalar(lam[:, 7:8], g["first_map"], -1.0, 1.0, ALU.mult, ALU.add))
        then(nc.vector.scalar_tensor_tensor(lam[:, 6:7], lam[:, 7:8], lam[:, 4:5], g["first_map"],
                                            ALU.mult, ALU.add))

    @blk.tensor
    def _(pe):
        ident = g["ident"]

        def transpose_x(t):
            m = rows_of(t)
            pe.wait_ge(xn_ready, t + 1)
            if t >= 1:
                pe.wait_ge(xT_kept_act, t)
                pe.wait_ge(xT_kept_dve, t)
            for c in range(KC):
                last = nc.tensor.transpose(psX[:, c // 4, (c % 4) * m:(c % 4) * m + m],
                                           xn[0:m, P * c:P * c + P], ident[0:m, 0:m])
            last.then_inc(xT_full, 1)

        def products(u):
            cb, t = units[u]
            m = rows_of(t)
            if t == 0:
                pe.wait_ge(w_in[cb % 2], 32 * (cb // 2 + 1))
            if cb == 0:
                pe.wait_ge(xT_kept_act, t + 1)
                pe.wait_ge(xT_kept_dve, t + 1)
            if u >= 4:
                pe.wait_ge(proj_kept, u - 3)
            for c in range(KC):
                last = nc.tensor.matmul(psP[0:m, u % 4, :], xnT[:, c, P * t:P * t + m], w[cb % 2][:, c, :],
                                        start=(c == 0), stop=(c == KC - 1))
            last.then_inc(proj_full, 1)

        def transpose_qk(u):
            cb, t = units[u]
            n = qk_of[u]
            m = rows_of(t)
            if u in rope_of:
                pe.wait_ge(rope_done, rope_of[u] + 1)
            else:
                pe.wait_ge(proj_kept, u + 1)
            if n >= 2:
                pe.wait_ge(qT_kept, n - 1)
            for c in range(HP):
                last = nc.tensor.transpose(psQ[:, n % 2, c * m:c * m + m],
                                           nat[n % NAT][0:m, P * c:P * c + P], ident[0:m, 0:m])
            last.then_inc(qT_full, 1)

        pe.wait_ge(const_in, 16)
        transpose_x(0)
        for u in range(len(units)):
            if u + 1 < NT:
                transpose_x(u + 1)
            products(u)
            if u >= 1 and u - 1 in qk_of:
                transpose_qk(u - 1)

    return n_stores


def attend(nc, A, g, st, sb, sem, n_stores):
    jobs = []
    for i in range(FULL):
        for r in range(4):
            jobs += [("S", i, 2 * r), ("S", i, 2 * r + 1), ("Da", i, r), ("Db", i, r)]
    NJ = len(jobs)
    NKP = NPR + 0

    def keys(j):
        kind, i, _ = jobs[j]
        return P * (i + 1) if kind == "S" else min(P * (i + 1) + META, NPR)

    def spill(j):
        return max(0, keys(j) - 1024)

    def key_tiles(j):
        n = keys(j)
        return [(a, min(P, n - a)) for a in range(0, n, P)]

    def groups(j):
        t = key_tiles(j)
        return [] if jobs[j][0] == "Da" else [t[a:a + 4] for a in range(0, len(t), 4)]

    uses, use_of = [], {}
    for k in range(-3, NJ):
        gr = groups(k) if k >= 0 else []
        if gr:
            use_of[("w", k, 0)] = len(uses)
            uses.append(("w", k, 0))
        if k + 3 < NJ and spill(k + 3):
            use_of[("z", k + 3, 0)] = len(uses)
            uses.append(("z", k + 3, 0))
        for n in range(1, len(gr)):
            use_of[("w", k, n)] = len(uses)
            uses.append(("w", k, n))
    wgroup_of = {u: n for n, u in enumerate([u for u in uses if u[0] == "w"])}
    s_of = {j: n for n, j in enumerate([j for j in range(NJ) if jobs[j][0] == "S"])}
    d_of = {j: n for n, j in enumerate([j for j in range(NJ) if jobs[j][0] != "S"])}
    a_of = {j: n for n, j in enumerate([j for j in range(NJ) if jobs[j][0] == "Db"])}
    pv_of = {j: n for n, j in enumerate([j for j in range(NJ) if groups(j)])}

    def count_to(table, j):
        return sum(1 for x in table if x <= j)

    E = [sb(st, f"E{i}", [P, 1024]) for i in range(3)]
    C = [sb(st, f"C{i}", [P, NKP]) for i in range(4)]
    zx = sb(st, "zx", [P, 4, META])
    wT = [sb(st, f"wT{i}", [P, 4, P]) for i in range(3)]
    mix = [sb(st, f"mix{i}", [P, D]) for i in range(2)]
    nm = sb(st, "nm", [P, 2, len(d_of)])
    Z = sb(st, "Z", [P, 2, len(d_of)])
    rZ = sb(st, "rZ", [P, len(d_of)])
    cf = sb(st, "cf", [P, len(a_of)])
    zero_i = sb(st, "zero_i", [MAXT + 1, P], I32)
    zero = sb(st, "zero", [P, D])
    psZ = st.enter_context(nc.psum_tensor("psZ", [P, 3, 1024], F32))
    psT = st.enter_context(nc.psum_tensor("psT", [P, 512], F32))
    psO = st.enter_context(nc.psum_tensor("psO", [P, 512], F32))

    qk_full, exp_done, ln_done = sem(st, "qk_full"), sem(st, "exp_done"), sem(st, "ln_done")
    t_ready, w_ready = sem(st, "t_ready"), sem(st, "w_ready")
    max_ready, p_ready, a_ready = sem(st, "max_ready"), sem(st, "p_ready"), sem(st, "a_ready")
    T_full, T_kept, pv_done, o_kept = sem(st, "T_full"), sem(st, "T_kept"), sem(st, "pv_done"), sem(st, "o_kept")
    zeroed, rows_filled = sem(st, "zeroed"), sem(st, "rows_filled")
    dve_own, mix_stored = sem(st, "att_dve_own"), [sem(st, f"mix_stored{i}") for i in range(2)]

    blk = st.enter_context(nc.Block())

    @blk.sync
    def _(sp):
        sp.wait_ge(zeroed, 2)
        sp.dma_start(g["ysd"].rearrange("(n p) d -> p n d", p=P),
                     zero[:, :].unsqueeze(1).to_broadcast([P, MAXT, D])).then_inc(rows_filled, 16)
        for i in range(FULL):
            sp.wait_ge(o_kept, 12 * (i + 1))
            sp.dma_start(g["mixd"][P * i:P * i + P, :], mix[i % 2][:, :]).then_inc(mix_stored[i % 2], 16)
        for b in range(2):
            sp.wait_ge(mix_stored[b], 16 * (FULL // 2))
        sp.wait_ge(rows_filled, 16)

    @blk.gpsimd
    def _(pool):
        nc.gpsimd.memset(zero_i[:, :], 0).then_inc(zeroed, 1)
        nc.gpsimd.memset(zero[:, :], 0.0).then_inc(zeroed, 1)
        pool.wait_ge(zeroed, 1)
        pool.dma_start(g["slotd"].rearrange("(a b) o -> a (b o)", b=P), zero_i[:, :]).then_inc(g["stores"], 16)
        n_stores[0] += 1

    @blk.tensor
    def _(pe):
        def scores(j):
            kind, i, h = jobs[j]
            grp = "sb" if kind == "S" else "df"
            half = h % 2 if kind == "S" else (kind == "Db") * 1
            pair = h // 2 if kind == "S" else h
            r = slice(64 * half, 64 * half + 64)
            mask = g["sb_mask"] if kind == "S" else g["df_mask"]
            n, m0 = keys(j), P * i
            if count_to(s_of, j - 3):
                pe.wait_ge(t_ready, count_to(s_of, j - 3))
            if count_to(d_of, j - 3):
                pe.wait_ge(p_ready, count_to(d_of, j - 3))
            for a in range(0, n, 512):
                b = min(a + 512, n)
                if a < 1024:
                    dst = psZ[:, j % 3, a:b]
                else:
                    u = use_of[("z", j, 0)]
                    if u:
                        pe.wait_ge(T_kept, u)
                    dst = psT[:, 0:b - a]
                lo = max(a, m0)
                last = nc.tensor.matmul(dst, g["qT_" + grp][r, pair, m0:m0 + P], g["kT_" + grp][r, pair, a:b],
                                        start=True, stop=(lo >= b))
                if lo < b:
                    last = nc.tensor.matmul(dst[:, lo - a:b - a], g["ident"], mask[:, lo - m0:b - m0],
                                            start=False, stop=True)
                if a >= 1024:
                    last.then_inc(T_full, 1)
                    last = None
                elif b == min(n, 1024):
                    last.then_inc(qk_full, 1)

        def transposes(j, n):
            kind = jobs[j][0]
            u = use_of[("w", j, n)]
            if n == 0:
                if kind == "S":
                    pe.wait_ge(w_ready, s_of[j] + 1)
                else:
                    pe.wait_ge(a_ready, a_of[j] + 1)
            if u:
                pe.wait_ge(T_kept, u)
            for x, (a, m) in enumerate(groups(j)[n]):
                last = nc.tensor.transpose(psT[0:m, P * x:P * x + P], C[j % 4][:, a:a + m], g["ident"])
            last.then_inc(T_full, 1)

        def values(j, n):
            kind, i, h = jobs[j]
            grp, w = ("sb", SBD) if kind == "S" else ("df", DFV)
            gr = groups(j)
            pe.wait_ge(T_kept, use_of[("w", j, n)] + 1)
            if n == 0 and pv_of[j]:
                pe.wait_ge(o_kept, pv_of[j])
            for x, (a, m) in enumerate(gr[n]):
                v = g["v_" + grp][0:m, a // P, w * h:w * h + w] if a < FULL * P else \
                    g["vtail_" + grp][0:m, w * h:w * h + w]
                last = nc.tensor.matmul(psO[:, 0:w], wT[wgroup_of[("w", j, n)] % 3][0:m, x, :], v,
                                        start=(n == 0 and x == 0), stop=(n == len(gr) - 1 and x == len(gr[n]) - 1))
            last.then_inc(pv_done, 1)

        for k in range(-3, NJ):
            gr = groups(k) if k >= 0 else []
            if gr:
                transposes(k, 0)
            if k + 3 < NJ:
                scores(k + 3)
            for n in range(1, len(gr)):
                transposes(k, n)
                values(k, n - 1)
            if gr:
                values(k, len(gr) - 1)

    @blk.scalar
    def _(act):
        def keep_T(use):
            what, j, n = use
            u = use_of[use]
            act.wait_ge(T_full, u + 1)
            if what == "z":
                nc.scalar.activation(zx[:, j % 4, 0:spill(j)], psT[:, 0:spill(j)], ACT.Copy).then_inc(T_kept, 1)
                return
            w = wgroup_of[use]
            if w >= 3:
                act.wait_ge(pv_done, w - 2)
            tiles = groups(j)[n]
            full = [t for t in tiles if t[1] == P]
            last = None
            if full:
                last = nc.scalar.activation(wT[w % 3][:, 0:len(full), :],
                                            psT[:, 0:P * len(full)].rearrange("p (x q) -> p x q", q=P), ACT.Copy)
            if len(full) < len(tiles):
                m, x = tiles[-1][1], len(full)
                last = nc.scalar.activation(wT[w % 3][0:m, x, :], psT[0:m, P * x:P * x + P], ACT.Copy)
            last.then_inc(T_kept, 1)

        def exp_ln(j):
            s, n = s_of[j], keys(j)
            act.wait_ge(qk_full, j + 1)
            if s >= 3:
                act.wait_ge(t_ready, s - 2)
            nc.scalar.activation(E[s % 3][:, 0:n], psZ[:, j % 3, 0:n], ACT.Exp).then_inc(exp_done, 1)
            act.wait_ge(exp_done, s + 1)
            nc.scalar.activation(E[s % 3][:, 0:n], E[s % 3][:, 0:n], ACT.Ln, bias=1.0).then_inc(ln_done, 1)

        def weights(j):
            s, n = s_of[j], keys(j)
            act.wait_ge(t_ready, s + 1)
            nc.scalar.activation(C[j % 4][:, 0:n], C[j % 4][:, 0:n], ACT.Exp).then_inc(w_ready, 1)

        def softmax_exp(j):
            d, n = d_of[j], min(keys(j), 1024)
            act.wait_ge(max_ready, d + 1)
            if j >= 4:
                if jobs[j][0] == "Da":
                    act.wait_ge(a_ready, a_of[j - 3])
                else:
                    act.wait_ge(T_full, use_of[("w", j - 4, len(groups(j - 4)) - 1)] + 1)
            if spill(j):
                nc.scalar.activation(C[j % 4][:, n:n + spill(j)], zx[:, j % 4, 0:spill(j)], ACT.Exp,
                                     bias=nm[:, 0, d:d + 1], accum_out=Z[:, 1, d:d + 1])
            nc.scalar.activation(C[j % 4][:, 0:n], psZ[:, j % 3, 0:n], ACT.Exp, bias=nm[:, 0, d:d + 1],
                                 accum_out=Z[:, 0, d:d + 1]).then_inc(p_ready, 1)

        def keep_o(j):
            kind, i, h = jobs[j]
            act.wait_ge(pv_done, wgroup_of[("w", j, len(groups(j)) - 1)] + 1)
            if i >= 2 and h == 0 and kind == "S":
                act.wait_ge(mix_stored[i % 2], 16 * (i // 2))
            if kind == "S":
                nc.scalar.activation(mix[i % 2][:, SBD * h:SBD * h + SBD], psO[:, 0:SBD], ACT.Copy) \
                    .then_inc(o_kept, 1)
            else:
                d = d_of[j - 1]
                nc.scalar.activation(mix[i % 2][:, 512 + DFV * h:512 + DFV * h + DFV], psO[:, 0:DFV], ACT.Copy,
                                     scale=rZ[:, d:d + 1]).then_inc(o_kept, 1)

        for k in range(-3, NJ):
            gr = groups(k) if k >= 0 else []
            if gr:
                keep_T(("w", k, 0))
            if k + 3 < NJ and spill(k + 3):
                keep_T(("z", k + 3, 0))
            if 0 <= k + 1 < NJ and jobs[k + 1][0] != "S":
                softmax_exp(k + 1)
            if len(gr) > 1:
                keep_T(("w", k, 1))
            if 0 <= k + 2 < NJ and jobs[k + 2][0] == "S":
                exp_ln(k + 2)
            for n in range(2, len(gr)):
                keep_T(("w", k, n))
            if 0 <= k + 1 < NJ and jobs[k + 1][0] == "S":
                weights(k + 1)
            if gr:
                keep_o(k)

    @blk.vector
    def _(dve):
        own = [0]

        def then(ins):
            own[0] += 1
            ins.then_inc(dve_own, 1)
            dve.wait_ge(dve_own, own[0])

        def row_max(j):
            d, n = d_of[j], min(keys(j), 1024)
            dve.wait_ge(qk_full, j + 1)
            if not spill(j):
                nc.vector.reduce_max(nm[:, 0, d:d + 1], psZ[:, j % 3, 0:n], AX_X, negate=True).then_inc(max_ready, 1)
                return
            dve.wait_ge(T_kept, use_of[("z", j, 0)] + 1)
            nc.vector.reduce_max(nm[:, 1, d:d + 1], zx[:, j % 4, 0:spill(j)], AX_X, negate=True)
            then(nc.vector.reduce_max(nm[:, 0, d:d + 1], psZ[:, j % 3, 0:n], AX_X, negate=True))
            nc.vector.tensor_tensor(nm[:, 0, d:d + 1], nm[:, 0, d:d + 1], nm[:, 1, d:d + 1],
                                    ALU.min).then_inc(max_ready, 1)

        def stick(j):
            s, n = s_of[j], keys(j)
            e, c, z = E[s % 3][:, 0:n], C[j % 4][:, 0:n], psZ[:, j % 3, 0:n]
            dve.wait_ge(ln_done, s + 1)
            then(nc.vector.scalar_tensor_tensor(e, e, LN_CAP, z, ALU.min, ALU.max))
            if j >= 4:
                dve.wait_ge(T_full, use_of[("w", j - 4, len(groups(j - 4)) - 1)] + 1)
            then(nc.vector.tensor_tensor_scan(c[:, ::-1], e[:, ::-1], e[:, ::-1], 0.0, ALU.add, ALU.max))
            nc.vector.tensor_tensor(c, z, c, ALU.subtract).then_inc(t_ready, 1)

        def mix_maps(j):
            d, n, a = d_of[j], keys(j), a_of[j]
            dve.wait_ge(p_ready, d + 1)
            if spill(j):
                then(nc.vector.tensor_tensor(Z[:, 0, d - 1:d + 1], Z[:, 0, d - 1:d + 1], Z[:, 1, d - 1:d + 1], ALU.add))
            then(nc.vector.reciprocal(rZ[:, d - 1:d + 1], Z[:, 0, d - 1:d + 1]))
            then(nc.vector.tensor_scalar(cf[:, a:a + 1], Z[:, 0, d - 1:d], rZ[:, d:d + 1], g["lam"][:, 4:5],
                                         ALU.mult, ALU.mult))
            nc.vector.scalar_tensor_tensor(C[j % 4][:, 0:n], C[j % 4][:, 0:n], cf[:, a:a + 1], C[(j - 1) % 4][:, 0:n],
                                           ALU.mult, ALU.add).then_inc(a_ready, 1)

        for k in range(-3, NJ):
            if 0 <= k + 2 < NJ and jobs[k + 2][0] != "S":
                row_max(k + 2)
            if 0 <= k + 1 < NJ:
                if jobs[k + 1][0] == "S":
                    stick(k + 1)
                elif jobs[k + 1][0] == "Db":
                    mix_maps(k + 1)


def stacked(nc, A, g, st, sb, sem):
    jobs = [(who, grp, gi) for who in ("tail", "samp") for grp in ("sb", "df") for gi in range(2)]
    NJ = len(jobs)
    NK = PAST + NS

    def keys(j):
        return NPR if jobs[j][0] == "tail" else NK

    def old(j):
        return FULL * P if jobs[j][0] == "tail" else PAST

    def chunks(j):
        return [(a, min(a + 512, keys(j))) for a in range(0, keys(j), 512)]

    def groups(j):
        n = keys(j)
        t = [(a, min(P, n - a)) for a in range(0, n, P)]
        return [t[a:a + 4] for a in range(0, len(t), 4)]

    NKT = PAST // P
    KT_AT = {1: "sb", 5: "df"}
    uses, use_of = [], {}

    def use(x):
        use_of[x] = len(uses)
        uses.append(x)

    for n in range(NKT):
        use(("k", "sb", n))
    for k in range(NJ):
        for n in range(len(groups(k))):
            use(("w", k, n))
        if k + 2 == 5:
            for n in range(NKT):
                use(("k", "df", n))
    wgroup_of = {u: n for n, u in enumerate([u for u in uses if u[0] == "w"])}
    chunk_of = {}
    for j in range(NJ):
        for n in range(len(chunks(j))):
            chunk_of[(j, n)] = len(chunk_of)
    s_of = {j: n for n, j in enumerate([j for j in range(NJ) if jobs[j][1] == "sb"])}
    d_of = {j: n for n, j in enumerate([j for j in range(NJ) if jobs[j][1] == "df"])}
    vloads = [(j, n) for j in range(NJ) if jobs[j][0] == "samp" for n in range(NKT // 4)]
    vload_of = {x: n for n, x in enumerate(vloads)}
    kloads = [(grp, n) for grp in ("sb", "df") for n in range(NKT // 4)]
    kload_of = {x: n for n, x in enumerate(kloads)}

    kTc = sb(st, "kTc", [P, HP, PAST])
    Kc = [sb(st, f"Kc{i}", [P, 4, 512]) for i in range(2)]
    Vc = [sb(st, f"Vc{i}", [P, 4, 256]) for i in range(2)]
    zs = [sb(st, f"zs{i}", [P, NK]) for i in range(2)]
    E = sb(st, "Es", [P, NK])
    C = sb(st, "Cs", [P, NK])
    wT = [sb(st, f"wTs{i}", [P, 4, P]) for i in range(3)]
    mix8 = sb(st, "mix8", [LAST, D])
    nm = sb(st, "nms", [P, len(d_of)])
    Z = sb(st, "Zs", [P, len(d_of)])
    rZ = sb(st, "rZs", [P, len(d_of)])
    R = sb(st, "R", [P, 64])
    psZ = st.enter_context(nc.psum_tensor("psZs", [P, 3, 512], F32))
    psT = st.enter_context(nc.psum_tensor("psTs", [P, 2, 512], F32))
    psO = st.enter_context(nc.psum_tensor("psOs", [P, 2, 512], F32))

    k_in = [sem(st, f"k_in{i}") for i in range(2)]
    v_in = [sem(st, f"v_in{i}") for i in range(2)]
    qk_full, z_kept = sem(st, "s_qk_full"), sem(st, "s_z_kept")
    exp_done, ln_done, t_ready, w_ready = (sem(st, n) for n in ("s_exp", "s_ln", "s_t", "s_w"))
    max_ready, p_ready, r_ready = (sem(st, n) for n in ("s_max", "s_p", "s_r"))
    T_full, T_kept, pv_done, o_kept = (sem(st, n) for n in ("s_T_full", "s_T_kept", "s_pv", "s_o"))
    dve_own, mix_stored = sem(st, "s_own"), sem(st, "s_mix")

    blk = st.enter_context(nc.Block())

    @blk.sync
    def _(sp):
        cache_k = {"sb": A["cache_sb_k"], "df": A["cache_diff_k"]}
        cache_v = {"sb": A["cache_sb_v"], "df": A["cache_diff_v"]}

        def load_k(x):
            grp, n = x
            m = kload_of[x]
            if m >= 2:
                g2, n2 = kloads[m - 2]
                sp.wait_ge(T_full, use_of[("k", g2, 4 * n2 + 3)] + 1)
            src = cache_k[grp].rearrange("l b t h d -> (l b t) (h d)")[512 * n:512 * n + 512, :]
            sp.dma_start(Kc[m % 2][:, :, :], src.rearrange("(x p) f -> p x f", p=P)).then_inc(k_in[m % 2], 16)

        def load_v(x):
            j, n = x
            m = vload_of[x]
            if m >= 2:
                sp.wait_ge(pv_done, wgroup_of[("w", *vloads[m - 2])] + 1)
            _, grp, gi = jobs[j]
            src = cache_v[grp].rearrange("l b t h d -> (l b t) (h d)")[512 * n:512 * n + 512, 256 * gi:256 * gi + 256]
            sp.dma_start(Vc[m % 2][:, :, :], src.rearrange("(x p) f -> p x f", p=P)).then_inc(v_in[m % 2], 16)

        for n in range(NKT // 4):
            load_k(("sb", n))
        load_v(vloads[0])
        load_v(vloads[1])
        load_k(("df", 0))
        load_k(("df", 1))
        load_k(("df", 2))
        load_k(("df", 3))
        for x in vloads[2:]:
            load_v(x)
        sp.wait_ge(o_kept, NJ)
        sp.dma_start(g["mixd"][FULL * P:NTOK, :], mix8[:, :]).then_inc(mix_stored, 16)
        sp.wait_ge(mix_stored, 16)

    @blk.tensor
    def _(pe):
        def scores(j):
            who, grp, gi = jobs[j]
            q = g[f"qs_{grp}_{who}"]
            for n, (a, b) in enumerate(chunks(j)):
                c = chunk_of[(j, n)]
                if c >= 3:
                    pe.wait_ge(z_kept, c - 2)
                own = b - a < 512
                if who == "samp" and n == 0:
                    pe.wait_ge(T_kept, use_of[("k", grp, NKT - 1)] + 1)
                for pp in range(2):
                    if who == "tail":
                        k = g["kT_" + grp][:, 2 * gi + pp, a:b]
                    else:
                        k = g["kTnew_" + grp][:, 2 * gi + pp, :] if own else kTc[:, 2 * gi + pp, a:b]
                    masked = own and grp == "sb"
                    last = nc.tensor.matmul(psZ[:, c % 3, 0:b - a], q[:, 2 * gi + pp, :], k,
                                            start=(pp == 0), stop=(pp == 1 and not masked))
                if masked:
                    last = nc.tensor.matmul(psZ[:, c % 3, 0:b - a], g["ident"], g["new_mask"][:, 0:b - a],
                                            start=False, stop=True)
                last.then_inc(qk_full, 1)

        def cache_keys(grp):
            for n in range(NKT):
                u = use_of[("k", grp, n)]
                m = kload_of[(grp, n // 4)]
                if n % 4 == 0:
                    pe.wait_ge(k_in[m % 2], 16 * (m // 2 + 1))
                if u >= 2:
                    pe.wait_ge(T_kept, u - 1)
                for c in range(HP):
                    last = nc.tensor.transpose(psT[:, u % 2, P * c:P * c + P],
                                               Kc[m % 2][:, n % 4, P * c:P * c + P], g["ident"])
                last.then_inc(T_full, 1)

        def transposes(j, n):
            u = use_of[("w", j, n)]
            stick = jobs[j][1] == "sb"
            if n == 0:
                if stick:
                    pe.wait_ge(w_ready, s_of[j] + 1)
                else:
                    pe.wait_ge(r_ready, d_of[j] + 1)
            if u >= 2:
                pe.wait_ge(T_kept, u - 1)
            for x, (a, m) in enumerate(groups(j)[n]):
                if stick:
                    last = nc.tensor.transpose(psT[0:m, u % 2, P * x:P * x + P], C[:, a:a + m], g["ident"])
                else:
                    last = nc.tensor.matmul(psT[0:m, u % 2, P * x:P * x + 64], zs[j % 2][:, a:a + m], R[:, :],
                                            start=True, stop=True)
            last.then_inc(T_full, 1)

        def values(j, n):
            who, grp, gi = jobs[j]
            gr = groups(j)
            u = use_of[("w", j, n)]
            M = P if grp == "sb" else 64
            pe.wait_ge(T_kept, u + 1)
            if n == 0 and j >= 2:
                pe.wait_ge(o_kept, j - 1)
            if (j, n) in vload_of:
                v = vload_of[(j, n)]
                pe.wait_ge(v_in[v % 2], 16 * (v // 2 + 1))
            f = slice(256 * gi, 256 * gi + 256)
            for x, (a, m) in enumerate(gr[n]):
                if who == "tail":
                    val = g["v_" + grp][:, a // P, f] if m == P else g["vtail_" + grp][0:m, f]
                else:
                    val = Vc[v % 2][:, x, :] if m == P else g["vnew_" + grp][0:m, f]
                last = nc.tensor.matmul(psO[0:M, j % 2, 0:256], wT[wgroup_of[("w", j, n)] % 3][0:m, x, 0:M], val,
                                        start=(n == 0 and x == 0), stop=(n == len(gr) - 1 and x == len(gr[n]) - 1))
            last.then_inc(pv_done, 1)

        scores(0)
        cache_keys("sb")
        scores(1)
        for k in range(NJ):
            n_g = len(groups(k))
            transposes(k, 0)
            for n in range(1, n_g):
                transposes(k, n)
                values(k, n - 1)
            values(k, n_g - 1)
            if k + 2 < NJ:
                scores(k + 2)
            if k + 2 == 5:
                cache_keys("df")

    @blk.scalar
    def _(act):
        def keep_z(j, n):
            a, b = chunks(j)[n]
            c = chunk_of[(j, n)]
            act.wait_ge(qk_full, c + 1)
            if n == 0 and j >= 2:
                if jobs[j - 2][1] == "sb":
                    act.wait_ge(t_ready, s_of[j - 2] + 1)
                else:
                    act.wait_ge(T_full, use_of[("w", j - 2, len(groups(j - 2)) - 1)] + 1)
            nc.scalar.activation(zs[j % 2][:, a:b], psZ[:, c % 3, 0:b - a], ACT.Copy).then_inc(z_kept, 1)

        def exp_ln(j):
            s, n = s_of[j], keys(j)
            act.wait_ge(z_kept, chunk_of[(j, len(chunks(j)) - 1)] + 1)
            if s >= 1:
                act.wait_ge(t_ready, s)
            nc.scalar.activation(E[:, 0:n], zs[j % 2][:, 0:n], ACT.Exp).then_inc(exp_done, 1)
            act.wait_ge(exp_done, s + 1)
            nc.scalar.activation(E[:, 0:n], E[:, 0:n], ACT.Ln, bias=1.0).then_inc(ln_done, 1)

        def last_exp(j):
            n = keys(j)
            if jobs[j][1] == "sb":
                act.wait_ge(t_ready, s_of[j] + 1)
                nc.scalar.activation(C[:, 0:n], C[:, 0:n], ACT.Exp).then_inc(w_ready, 1)
            else:
                d = d_of[j]
                act.wait_ge(max_ready, d + 1)
                nc.scalar.activation(zs[j % 2][:, 0:n], zs[j % 2][:, 0:n], ACT.Exp, bias=nm[:, d:d + 1],
                                     accum_out=Z[:, d:d + 1]).then_inc(p_ready, 1)

        def keep_o(j):
            who, grp, gi = jobs[j]
            act.wait_ge(pv_done, wgroup_of[("w", j, len(groups(j)) - 1)] + 1)
            r0, nq = (0, NS) if who == "samp" else (NS, TAIL)
            if grp == "sb":
                for s in range(4):
                    c = SBD * (4 * gi + s)
                    last = nc.scalar.activation(mix8[r0:r0 + nq, c:c + SBD],
                                                psO[32 * s:32 * s + nq, j % 2, SBD * s:SBD * s + SBD], ACT.Copy)
            else:
                for s in range(2):
                    c = 512 + DFV * (2 * gi + s)
                    last = nc.scalar.activation(mix8[r0:r0 + nq, c:c + DFV],
                                                psO[32 * s:32 * s + nq, j % 2, DFV * s:DFV * s + DFV], ACT.Copy)
            last.then_inc(o_kept, 1)

        for n in range(len(chunks(0))):
            keep_z(0, n)
        exp_ln(0)
        for n in range(len(chunks(1))):
            keep_z(1, n)
        last_exp(0)
        for k in range(NJ):
            if k + 1 < NJ and k + 1 in s_of:
                exp_ln(k + 1)
            keep_o(k)
            ch = len(chunks(k + 2)) if k + 2 < NJ else 0
            for n in range(ch - 1):
                keep_z(k + 2, n)
            if k + 1 < NJ:
                last_exp(k + 1)
            if ch:
                keep_z(k + 2, ch - 1)

    @blk.vector
    def _(dve):
        own = [0]

        def then(ins):
            own[0] += 1
            ins.then_inc(dve_own, 1)
            dve.wait_ge(dve_own, own[0])

        def keep_keys(grp):
            for n in range(NKT):
                u = use_of[("k", grp, n)]
                dve.wait_ge(T_full, u + 1)
                if grp == "df" and n == 0:
                    dve.wait_ge(qk_full, chunk_of[(5, len(chunks(5)) - 1)] + 1)
                nc.vector.tensor_copy(kTc[:, :, P * n:P * n + P],
                                      psT[:, u % 2, :].rearrange("p (c k) -> p c k", c=HP)).then_inc(T_kept, 1)

        def keep_w(j, n):
            u = use_of[("w", j, n)]
            w = wgroup_of[("w", j, n)]
            M = P if jobs[j][1] == "sb" else 64
            dve.wait_ge(T_full, u + 1)
            if w >= 3:
                dve.wait_ge(pv_done, w - 2)
            tiles = groups(j)[n]
            full = [t for t in tiles if t[1] == P]
            ps = psT[:, u % 2, :].rearrange("p (x q) -> p x q", q=P)
            last = None
            if full:
                last = nc.vector.tensor_copy(wT[w % 3][:, 0:len(full), 0:M], ps[:, 0:len(full), 0:M])
            if len(full) < len(tiles):
                m, x = tiles[-1][1], len(full)
                last = nc.vector.tensor_copy(wT[w % 3][0:m, x, 0:M], ps[0:m, x, 0:M])
            last.then_inc(T_kept, 1)

        def body(j):
            n, z = keys(j), zs[j % 2]
            if jobs[j][1] == "df":
                d = d_of[j]
                dve.wait_ge(z_kept, chunk_of[(j, len(chunks(j)) - 1)] + 1)
                nc.vector.reduce_max(nm[:, d:d + 1], z[:, 0:n], AX_X, negate=True).then_inc(max_ready, 1)
                dve.wait_ge(p_ready, d + 1)
                then(nc.vector.reciprocal(rZ[:, d:d + 1], Z[:, d:d + 1]))
                then(nc.vector.tensor_scalar(rZ[:, d:d + 1], rZ[:, d:d + 1], g["lam"][:, 6:7], None, ALU.mult))
                nc.vector.tensor_scalar(R[:, :], g["fold"], rZ[:, d:d + 1], None, ALU.mult).then_inc(r_ready, 1)
                return
            s = s_of[j]
            e, c = E[:, 0:n], C[:, 0:n]
            dve.wait_ge(ln_done, s + 1)
            then(nc.vector.scalar_tensor_tensor(e, e, LN_CAP, z[:, 0:n], ALU.min, ALU.max))
            then(nc.vector.tensor_tensor_scan(c[:, ::-1], e[:, ::-1], e[:, ::-1], 0.0, ALU.add, ALU.max))
            nc.vector.tensor_tensor(c, z[:, 0:n], c, ALU.subtract).then_inc(t_ready, 1)

        keep_keys("sb")
        body(0)
        for k in range(NJ):
            for n in range(len(groups(k))):
                keep_w(k, n)
            if k + 1 < NJ:
                body(k + 1)
            if k + 2 == 5:
                keep_keys("df")


def mix_out(nc, A, g, st, sb, sem):
    mixt = [sb(st, f"mixt{i}", [P, D]) for i in range(2)]
    xt = [sb(st, f"xr{i}", [P, D]) for i in range(2)]
    xn2 = [sb(st, f"xn2{i}", [P, D]) for i in range(2)]
    wo = sb(st, "wo", [P, KC, D])
    wr = sb(st, "wr", [P, KC, NG + NE])
    bias = sb(st, "bias", [P, NG + NE])
    gffn = sb(st, "gffn", [P, D])
    gsub = sb(st, "gsub", [P, DFV])
    mT = sb(st, "mT", [P, KC, P])
    xT = sb(st, "xT", [P, KC, P])
    junk = sb(st, "junk2", [P, D], BF16)
    junk4 = sb(st, "junk4", [P, 2, 512], BF16)
    ss = sb(st, "ss2", [P, NT, 5])
    rs = sb(st, "rs2", [P, NT, 5])
    nh = sb(st, "nh", [P, 4])
    psT = st.enter_context(nc.psum_tensor("psTm", [P, 2, 512], F32))
    psY = st.enter_context(nc.psum_tensor("psYm", [P, 2, 1024], F32))
    psR = st.enter_context(nc.psum_tensor("psR", [P, 512], F32))

    mix_in = [sem(st, f"mix_in{i}") for i in range(2)]
    x_in = [sem(st, f"xr_in{i}") for i in range(2)]
    wo_in, small_in = sem(st, "wo_in"), sem(st, "small_in")
    sub_sq, sub_rs, sub_done = sem(st, "sub_sq"), sem(st, "sub_rs"), sem(st, "sub_done")
    T_full, T_act, T_dve = sem(st, "m_T_full"), sem(st, "m_T_act"), sem(st, "m_T_dve")
    y_full, h_ready, h_sq, h_rs, xn_ready = (sem(st, n) for n in ("y_full", "h_ready", "h_sq", "h_rs", "xn2_ready"))
    r_full, r_kept = sem(st, "r_full"), sem(st, "r_kept")
    xn_stored = [sem(st, f"xn_stored{i}") for i in range(2)]
    dve_own, pool_own = sem(st, "m_own"), sem(st, "m_pool_own")

    x_rows = A["x_prompt"].rearrange("a s d -> (a s) d")
    xs_rows = A["x_sample"].rearrange("a s d -> (a s) d")
    uses = [("m", 0)]
    for t in range(NT + 1):
        if t + 1 < NT:
            uses.append(("m", t + 1))
        if t >= 1:
            uses.append(("x", t - 1))
    use_of = {u: n for n, u in enumerate(uses)}

    def x_loads(t):
        return sum(2 if s in (0, FULL) else 1 for s in range(t % 2, t + 1, 2))

    blk = st.enter_context(nc.Block())

    @blk.sync
    def _(sp):
        def load(t):
            m = rows_of(t)
            if t >= 2:
                sp.wait_ge(T_full, use_of[("m", t - 2)] + 1)
            sp.dma_start(mixt[t % 2][0:m, :], g["mixd"][P * t:P * t + m, :]).then_inc(mix_in[t % 2], 16)
            if t >= 2:
                sp.wait_ge(h_ready, t - 1)
            if t == 0:
                sp.dma_start(xt[0][0:META, :], A["meta_tokens"]).then_inc(x_in[0], 16)
                sp.dma_start(xt[0][META:P, :], x_rows[0:P - META, :]).then_inc(x_in[0], 16)
            elif t < FULL:
                sp.dma_start(xt[t % 2][:, :], x_rows[P * t - META:P * t + P - META, :]).then_inc(x_in[t % 2], 16)
            else:
                sp.dma_start(xt[t % 2][0:NS, :], xs_rows).then_inc(x_in[t % 2], 16)
                sp.dma_start(xt[t % 2][NS:LAST, :], x_rows[SEQ - TAIL:SEQ, :]).then_inc(x_in[t % 2], 16)

        load(0)
        sp.dma_start(gsub[:, :], A["subln_g"].broadcast_to([P, DFV])).then_inc(small_in, 16)
        sp.dma_start(wo[:, :, :], A["w_out"][0].rearrange("(c p) n -> p c n", p=P)).then_inc(wo_in, 16)
        sp.dma_start(gffn[:, :], A["norm_ffn_g"].broadcast_to([P, D])).then_inc(small_in, 16)
        sp.dma_start(wr[:, :, 0:NG], A["w_group"][0].rearrange("(p c) n -> p c n", c=KC)).then_inc(small_in, 16)
        sp.dma_start(wr[:, :, NG:], A["w_router"][0].rearrange("(p c) n -> p c n", c=KC)).then_inc(small_in, 16)
        sp.dma_start(bias[:, 0:NG], A["b_group"].broadcast_to([P, NG])).then_inc(small_in, 16)
        sp.dma_start(bias[:, NG:], A["b_router"].broadcast_to([P, NE])).then_inc(small_in, 16)
        for t in range(1, NT):
            load(t)

    @blk.gpsimd
    def _(pool):
        own = [0]

        def then(ins):
            own[0] += 1
            ins.then_inc(pool_own, 1)
            pool.wait_ge(pool_own, own[0])

        then(nc.gpsimd.memset(nh[:, :], -0.5))

        def sub(t):
            m = rows_of(t)
            pool.wait_ge(sub_sq, t + 1)
            then(nc.gpsimd.tensor_scalar(ss[0:m, t, 0:4], ss[0:m, t, 0:4], 1.0 / DFV, EPS, ALU.mult, ALU.add))
            nc.gpsimd.tensor_tensor(rs[0:m, t, 0:4], ss[0:m, t, 0:4], nh[0:m, :], ALU.pow).then_inc(sub_rs, 1)

        def full(t):
            m = rows_of(t)
            pool.wait_ge(h_sq, t + 1)
            then(nc.gpsimd.tensor_scalar(ss[0:m, t, 4:5], ss[0:m, t, 4:5], 1.0 / D, EPS, ALU.mult, ALU.add))
            nc.gpsimd.tensor_tensor(rs[0:m, t, 4:5], ss[0:m, t, 4:5], nh[0:m, 0:1], ALU.pow).then_inc(h_rs, 1)

        def store(t):
            m = rows_of(t)
            pool.wait_ge(xn_ready, t + 1)
            pool.dma_start(g["xn2d"][P * t:P * t + m, :], xn2[t % 2][0:m, :]).then_inc(xn_stored[t % 2], 16)

        sub(0)
        for t in range(NT):
            if t + 1 < NT:
                sub(t + 1)
            full(t)
            store(t)
        for b in range(2):
            pool.wait_ge(xn_stored[b], 16 * len(range(b, NT, 2)))

    @blk.scalar
    def _(act):
        def sub(t):
            m = rows_of(t)
            act.wait_ge(mix_in[t % 2], 16 * (t // 2 + 1))
            for h in range(DFH):
                last = nc.scalar.activation(junk4[0:m, t % 2, DFV * h:DFV * h + DFV], mixt[t % 2][0:m, 512 + DFV * h:512 + DFV * h + DFV],
                                            ACT.Square, accum_out=ss[0:m, t, h:h + 1])
            last.then_inc(sub_sq, 1)

        def keep_T(use):
            u = use_of[use]
            m = rows_of(use[1])
            dst = mT if use[0] == "m" else xT
            act.wait_ge(T_full, u + 1)
            nc.scalar.activation(dst[:, 0:4, 0:m], psT[:, 0, 0:4 * m].rearrange("p (c m) -> p c m", c=4),
                                 ACT.Copy).then_inc(T_act, 1)

        def square(t):
            m = rows_of(t)
            act.wait_ge(h_ready, t + 1)
            if t >= 1:
                act.wait_ge(h_sq, t)
            nc.scalar.activation(junk[0:m, :], g["h"][0:m, t, :], ACT.Square,
                                 accum_out=ss[0:m, t, 4:5]).then_inc(h_sq, 1)

        sub(0)
        keep_T(("m", 0))
        for t in range(NT + 1):
            if t + 1 < NT:
                sub(t + 1)
                act.wait_ge(y_full, t + 1)
                keep_T(("m", t + 1))
            if t >= 1:
                keep_T(("x", t - 1))
            if t < NT:
                square(t)

    @blk.vector
    def _(dve):
        own = [0]

        def then(ins):
            own[0] += 1
            ins.then_inc(dve_own, 1)
            dve.wait_ge(dve_own, own[0])

        def sub(t):
            m = rows_of(t)
            dve.wait_ge(sub_rs, t + 1)
            for h in range(DFH):
                o = mixt[t % 2][0:m, 512 + DFV * h:512 + DFV * h + DFV]
                last = nc.vector.scalar_tensor_tensor(o, o, rs[0:m, t, h:h + 1], gsub[0:m, :], ALU.mult, ALU.mult)
            last.then_inc(sub_done, 1)

        def keep_T(use):
            u = use_of[use]
            m = rows_of(use[1])
            dst = mT if use[0] == "m" else xT
            dve.wait_ge(T_full, u + 1)
            nc.vector.tensor_copy(dst[:, 4:8, 0:m],
                                  psT[:, 1, 0:4 * m].rearrange("p (c m) -> p c m", c=4)).then_inc(T_dve, 1)

        def residual(t):
            m = rows_of(t)
            dve.wait_ge(y_full, t + 1)
            dve.wait_ge(x_in[t % 2], 16 * x_loads(t))
            nc.vector.tensor_tensor(g["h"][0:m, t, :], psY[0:m, t % 2, :], xt[t % 2][0:m, :],
                                    ALU.add).then_inc(h_ready, 1)

        def normalise(t):
            m = rows_of(t)
            dve.wait_ge(h_rs, t + 1)
            if t >= 2:
                dve.wait_ge(xn_stored[t % 2], 16 * (t // 2))
                dve.wait_ge(T_full, use_of[("x", t - 2)] + 1)
            swap = "p (f c) -> p c f"
            nc.vector.scalar_tensor_tensor(xn2[t % 2][0:m, :].rearrange("p (c f) -> p c f", c=KC),
                                           g["h"][0:m, t, :].rearrange(swap, c=KC), rs[0:m, t, 4:5],
                                           gffn[0:m, :].rearrange(swap, c=KC), ALU.mult, ALU.mult) \
                .then_inc(xn_ready, 1)

        def keep_logits(t):
            m = rows_of(t)
            dve.wait_ge(r_full, t + 1)
            nc.vector.tensor_tensor(g["logits"][0:m, t, :], psR[0:m, 0:NG + NE], bias[0:m, :],
                                    ALU.add).then_inc(r_kept, 1)

        then(nc.vector.memset(g["logits"][:, :, :], 0.0))
        dve.wait_ge(small_in, 96)
        then(nc.vector.tensor_scalar(gsub[:, :], gsub[:, :], 1.0 - LAM_INIT, None, ALU.mult))
        sub(0)
        keep_T(("m", 0))
        for t in range(NT + 1):
            if t + 1 < NT:
                sub(t + 1)
                dve.wait_ge(y_full, t + 1)
                keep_T(("m", t + 1))
            if t >= 1:
                keep_T(("x", t - 1))
            if t < NT:
                residual(t)
                normalise(t)
            if t >= 1:
                keep_logits(t - 1)

    @blk.tensor
    def _(pe):
        def transpose(use):
            u = use_of[use]
            t = use[1]
            m = rows_of(t)
            if use[0] == "m":
                pe.wait_ge(sub_done, t + 1)
            else:
                pe.wait_ge(xn_ready, t + 1)
            if u >= 1:
                pe.wait_ge(T_act, u)
                pe.wait_ge(T_dve, u)
            src = (mixt if use[0] == "m" else xn2)[t % 2]
            for c in range(KC):
                last = nc.tensor.transpose(psT[:, c // 4, (c % 4) * m:(c % 4) * m + m],
                                           src[0:m, P * c:P * c + P], g["ident"][0:m, 0:m])
            last.then_inc(T_full, 1)

        def outputs(t):
            m = rows_of(t)
            u = use_of[("m", t)]
            pe.wait_ge(T_act, u + 1)
            pe.wait_ge(T_dve, u + 1)
            if t == 0:
                pe.wait_ge(wo_in, 16)
            if t >= 2:
                pe.wait_ge(h_ready, t - 1)
            for n in range(2):
                for c in range(KC):
                    last = nc.tensor.matmul(psY[0:m, t % 2, 512 * n:512 * n + 512], mT[:, c, 0:m],
                                            wo[:, c, 512 * n:512 * n + 512], start=(c == 0), stop=(c == KC - 1))
            last.then_inc(y_full, 1)

        def router(t):
            m = rows_of(t)
            u = use_of[("x", t)]
            pe.wait_ge(T_act, u + 1)
            pe.wait_ge(T_dve, u + 1)
            if t >= 1:
                pe.wait_ge(r_kept, t)
            else:
                pe.wait_ge(small_in, 96)
            for c in range(KC):
                last = nc.tensor.matmul(psR[0:m, 0:NG + NE], xT[:, c, 0:m], wr[:, c, :],
                                        start=(c == 0), stop=(c == KC - 1))
            last.then_inc(r_full, 1)

        transpose(("m", 0))
        for t in range(NT + 1):
            if t < NT:
                outputs(t)
            if t + 1 < NT:
                transpose(("m", t + 1))
            if t >= 1:
                transpose(("x", t - 1))
                router(t - 1)


def route(nc, A, g, st, sb, sem, n_stores):
    gpad = sb(st, "gpad", [P, NT, 8])
    gm = sb(st, "gm", [P, NT, 8])
    gi = sb(st, "gi", [P, NT, 8], U32)
    gf = sb(st, "gf", [P, NT])
    ge = sb(st, "ge", [P, NT, NG])
    gw = sb(st, "gw", [P, NT])
    oh = sb(st, "oh", [P, NT, NG])
    pr = sb(st, "pr", [P, NT, EPG, NG])
    sel = sb(st, "sel", [P, NT, EPG])
    em = sb(st, "em", [P, NT, 8])
    ei = sb(st, "ei", [P, NT, 8], U32)
    ef = sb(st, "ef", [P, NT, 2])
    dd = sb(st, "dd", [P, NT])
    M = sb(st, "M", [P, 2, NT, NE])
    Ms = sb(st, "Ms", [P, NT, NE])
    pos = sb(st, "pos", [P, NT, NE])
    tot = sb(st, "tot", [P, NT, NE])
    cnt = sb(st, "cnt", [P, NE])
    cnt_i = sb(st, "cnt_i", [P, NE], I32)
    nt = sb(st, "nt", [P, NE])
    incl = sb(st, "incl", [P, NE])
    base = sb(st, "base", [P, NE])
    slot_f = sb(st, "slot_f", [P, 2, NT])
    cmp = sb(st, "cmp", [1, MAXT + 1, NE])
    te = sb(st, "te", [1, MAXT + 1])
    tok = sb(st, "tok", [P, NT], I32)
    psA = st.enter_context(nc.psum_tensor("psA", [P, 512], F32))
    psB = st.enter_context(nc.psum_tensor("psB", [P, 512], F32))
    g_sub, g_exp, d_sub, d_exp = (sem(st, n) for n in ("g_sub", "g_exp", "d_sub", "d_exp"))
    pairs_ready, counts_full, slots_ready, scattered = (sem(st, n) for n in ("pairs", "counts", "slots", "scattered"))
    dve_own = sem(st, "r_own")
    blk = st.enter_context(nc.Block())

    @blk.vector
    def _(dve):
        own = [0]

        def then(ins):
            own[0] += 1
            ins.then_inc(dve_own, 1)
            dve.wait_ge(dve_own, own[0])

        def bc(ap, shape, axis):
            return ap.unsqueeze(axis).to_broadcast(shape)

        V = nc.vector
        GL = g["logits"][:, :, 0:NG]
        EL = g["logits"][:, :, NG:].rearrange("p t (g e) -> p t e g", g=NG)
        then(V.memset(gpad[:, :, :], -3e38))
        then(V.tensor_copy(gpad[:, :, 0:NG], GL))
        for t in range(NT):
            last = V.max(gm[:, t, :], gpad[:, t, :])
        then(last)
        for t in range(NT):
            last = V.max_index(gi[:, t, :], gm[:, t, :], gpad[:, t, :])
        then(last)
        V.tensor_tensor(ge[:, :, :], GL, gm[:, :, 0:1].to_broadcast([P, NT, NG]), ALU.subtract).then_inc(g_sub, 1)
        then(V.tensor_copy(gf[:, :], gi[:, :, 0]))
        then(V.tensor_tensor(oh[:, :, :], bc(gf[:, :], [P, NT, NG], 2), bc(g["iota"][:, 0:NG], [P, NT, NG], 1),
                             ALU.is_equal))
        for t in range(NT):
            last = V.tensor_tensor(pr[:, t, :, :], EL[:, t, :, :], bc(oh[:, t, :], [P, EPG, NG], 1), ALU.mult)
        then(last)
        then(V.reduce_sum(sel[:, :, :], pr[:, :, :, :], AX_X))
        for t in range(NT):
            last = V.max(em[:, t, :], sel[:, t, :])
        then(last)
        for t in range(NT):
            last = V.max_index(ei[:, t, :], em[:, t, :], sel[:, t, :])
        then(last)
        V.tensor_tensor(dd[:, :], em[:, :, 1], em[:, :, 0], ALU.subtract).then_inc(d_sub, 1)
        then(V.tensor_copy(ef[:, :, :], ei[:, :, 0:2]))
        for n in range(2):
            last = V.scalar_tensor_tensor(ef[:, :, n], gf[:, :], float(EPG), ef[:, :, n], ALU.mult, ALU.add)
        then(last)
        for n in range(2):
            last = V.tensor_tensor(M[:, n], bc(ef[:, :, n], [P, NT, NE], 2), bc(g["iota"][:, 0:NE], [P, NT, NE], 1),
                                   ALU.is_equal)
        then(last)
        for n in range(2):
            last = V.tensor_tensor(M[:, n], M[:, n], bc(g["valid"], [P, NT, NE], 2), ALU.mult)
        then(last)
        V.tensor_tensor(Ms[:, :, :], M[:, 0], M[:, 1], ALU.add).then_inc(pairs_ready, 1)
        dve.wait_ge(g_exp, 1)
        then(V.reduce_sum(gw[:, :], ge[:, :, :], AX_X))
        then(V.reciprocal(gw[:, :], gw[:, :]))
        dve.wait_ge(d_exp, 1)
        then(V.tensor_scalar(gf[:, :], dd[:, :], 1.0, None, ALU.add))
        then(V.reciprocal(gf[:, :], gf[:, :]))
        then(V.tensor_tensor(g["gates"][:, :, 0], gf[:, :], gw[:, :], ALU.mult))
        then(V.tensor_tensor(g["gates"][:, :, 1], g["gates"][:, :, 0], dd[:, :], ALU.mult))
        dve.wait_ge(counts_full, 1)
        V.tensor_copy(tot[:, :, :], psB[:, 0:NT * NE].rearrange("p (t e) -> p t e", e=NE))
        then(V.tensor_copy(pos[:, :, :], psA[:, 0:NT * NE].rearrange("p (t e) -> p t e", e=NE)))
        then(V.tensor_copy(cnt[:, :], tot[:, 0, :]))
        for t in range(1, NT):
            then(V.tensor_tensor(pos[:, t, :], pos[:, t, :], cnt[:, :], ALU.add))
            then(V.tensor_tensor(cnt[:, :], cnt[:, :], tot[:, t, :], ALU.add))
        then(V.tensor_scalar(cnt_i[:, :], cnt[:, :], float(P - 1), None, ALU.add))
        then(V.tensor_scalar(cnt_i[:, :], cnt_i[:, :], 7, None, ALU.logical_shift_right))
        then(V.tensor_copy(nt[:, :], cnt_i[:, :]))
        then(V.tensor_tensor_scan(incl[:, :], nt[:, :], nt[:, :], 0.0, ALU.add, ALU.max))
        then(V.tensor_tensor(base[:, :], incl[:, :], nt[:, :], ALU.subtract))
        then(V.tensor_scalar(base[:, :], base[:, :], float(P), None, ALU.mult))
        then(V.tensor_tensor(pos[:, :, :], pos[:, :, :], bc(base[:, :], [P, NT, NE], 1), ALU.add))
        for n in range(2):
            last = V.tensor_tensor(M[:, n], M[:, n], pos[:, :, :], ALU.mult)
        then(last)
        then(V.reduce_sum(slot_f[:, :, :], M[:, :, :, :], AX_X))
        V.tensor_copy(tok[:, :], g["token"])
        V.tensor_copy(g["slot"][:, :, :], slot_f[:, :, :]).then_inc(slots_ready, 1)
        then(V.tensor_tensor(cmp[:, :, :], bc(incl[0:1, :], [1, MAXT + 1, NE], 1),
                             bc(g["iota"][0:1, :], [1, MAXT + 1, NE], 2), ALU.is_le))
        then(V.reduce_sum(te[:, :], cmp[:, :, :], AX_X))
        then(V.tensor_scalar(g["tile_expert"][:, :], te[:, :], float(NE - 1), None, ALU.min))
        then(V.tensor_copy(g["n_tiles"][:, 0:1], incl[0:1, NE - 1:NE]))
        then(V.tensor_scalar(g["n_tiles"][:, 1:2], incl[0:1, NE - 1:NE], -1.0, None, ALU.add))

    @blk.scalar
    def _(act):
        act.wait_ge(g_sub, 1)
        nc.scalar.activation(ge[:, :, :], ge[:, :, :], ACT.Exp).then_inc(g_exp, 1)
        act.wait_ge(d_sub, 1)
        nc.scalar.activation(dd[:, :], dd[:, :], ACT.Exp).then_inc(d_exp, 1)

    @blk.tensor
    def _(pe):
        pe.wait_ge(pairs_ready, 1)
        flat = Ms[:, :, :].rearrange("p t e -> p (t e)")
        nc.tensor.matmul(psA[:, 0:NT * NE], g["before"], flat, start=True, stop=True)
        nc.tensor.matmul(psB[:, 0:NT * NE], g["ones"], flat, start=True, stop=True).then_inc(counts_full, 1)

    @blk.gpsimd
    def _(pool):
        pool.wait_ge(slots_ready, 1)
        pool.wait_ge(g["stores"], 16 * n_stores[0])
        n = 0
        for t in range(NT):
            m = rows_of(t)
            for j in range(2):
                pool.indirect_dma_start(out=g["slotd"], out_offset=bass.IndirectOffsetOnAxis(
                    ap=g["slot"][0:m, j, t:t + 1], axis=0), in_=tok[0:m, t:t + 1], in_offset=None) \
                    .then_inc(scattered, 16)
                n += 1
        pool.wait_ge(scattered, 16 * n)


def experts(nc, A, g, st, sb, sem):
    w_gu = sb(st, "w_gu", [P, WRING * 2 * KC * DE])
    w_dn = sb(st, "w_dn", [P, WRING * EC * D])
    gu5 = w_gu[:, :].rearrange("p (s g c f) -> p s g c f", s=WRING, g=2, c=KC)
    dn4 = w_dn[:, :].rearrange("p (s c n) -> p s c n", s=WRING, c=EC)
    map_i = sb(st, "map_i", [MAXT + 1, P], I32)
    map_f = sb(st, "map_f", [MAXT + 1, P])
    idx = sb(st, "idx", [P, MAXT + 1], I32)
    idx1 = sb(st, "idx1", [P, 1], I32)
    xg = sb(st, "xg", [P, D])
    xgT = sb(st, "xgT", [P, KC, P])
    ex = sb(st, "ex", [P, DE])
    h = sb(st, "hid", [P, DE])
    hT = sb(st, "hT", [P, EC, P])
    y = sb(st, "y", [P, D])
    psX = st.enter_context(nc.psum_tensor("psXe", [P, 2, 512], F32))
    psG = st.enter_context(nc.psum_tensor("psG", [P, 512], F32))
    psH = st.enter_context(nc.psum_tensor("psH", [P, 512], F32))
    psY = st.enter_context(nc.psum_tensor("psYe", [P, 2, 512], F32))
    map_in, map_conv, map_full, idx_ready = (sem(st, n) for n in ("map_in", "map_conv", "map_full", "idx_ready"))
    gate_in, up_in, down_in = sem(st, "gate_in"), sem(st, "up_in"), sem(st, "down_in")
    idx_copied, x_in = sem(st, "idx_copied"), sem(st, "xg_in")
    xT_full, xT_act, xT_dve = sem(st, "e_xT_full"), sem(st, "e_xT_act"), sem(st, "e_xT_dve")
    gu_full, exp_done, h_ready = sem(st, "gu_full"), sem(st, "e_exp"), sem(st, "hid_ready")
    hT_full, hT_kept, y_full, y_kept, y_stored = (sem(st, n) for n in ("hT_full", "hT_kept", "e_y_full", "e_y_kept",
                                                                      "y_stored"))
    dve_own, turn = sem(st, "e_own"), sem(st, "turn")
    wg = A["w_gate"].rearrange("l e (p c) f -> (l e) p c f", c=KC)
    wu = A["w_up"].rearrange("l e (p c) f -> (l e) p c f", c=KC)
    wd = A["w_down"].rearrange("l e (c p) n -> (l e) p c n", p=P)

    blk = st.enter_context(nc.Block())

    def tiles(eng):
        return eng.value_load(g["n_tiles"][0:1, 0:1], min_val=2, max_val=MAXT)

    def last_tile(eng):
        return eng.value_load(g["n_tiles"][0:1, 1:2], min_val=1, max_val=MAXT - 1)

    @blk.sync
    def _(sp):
        sp.dma_start(map_i[:, :], g["slotd"].rearrange("(a b) o -> a (b o)", b=P)).then_inc(map_in, 16)

        def load(t, slot):
            e = sp.value_load(g["tile_expert"][0:1, ds(t, 1)], min_val=0, max_val=NE - 1)
            for sem_in, dst, src in ((gate_in, gu5[:, ds(slot, 1), 0], wg), (up_in, gu5[:, ds(slot, 1), 1], wu),
                                     (down_in, dn4[:, ds(slot, 1)], wd)):
                if not isinstance(t, int) or t >= 1:
                    sp.wait_ge(sem_in, t * 16)
                sp.dma_start(dst, src[ds(e, 1)].rearrange("o p c f -> p o c f")).then_inc(sem_in, 16)

        for t in range(WRING):
            load(t, t)
        with sp.Fori(WRING, tiles(sp)) as t:
            sp.wait_ge(y_full, t - (WRING - 1))
            load(t, t % WRING)

    @blk.gpsimd
    def _(pool):
        pool.wait_ge(idx_ready, 1)

        def gather(t):
            nc.gpsimd.tensor_copy(idx1[:, :], idx[:, ds(t, 1)]).then_inc(idx_copied, 1)
            pool.wait_ge(idx_copied, t + 1)
            pool.sem_inc(turn, 1)
            pool.indirect_dma_start(out=xg[:, :], out_offset=None, in_=g["xn2d"],
                                    in_offset=bass.IndirectOffsetOnAxis(ap=idx1[:, 0:1], axis=0)).then_inc(x_in, 16)

        gather(0)
        with pool.Fori(1, tiles(pool) + 1) as t:
            pool.wait_ge(x_in, t * 16)
            pool.wait_ge(xT_full, t)
            gather(t)
        pool.wait_ge(x_in, (tiles(pool) + 1) * 16)

    @blk.tensor
    def _(pe):
        pe.wait_ge(map_conv, 1)
        nc.tensor.transpose(psH[:, 0:MAXT + 1], map_f[:, :], g["ident"][0:MAXT + 1, 0:MAXT + 1]).then_inc(map_full, 1)

        def transpose_x(t):
            pe.wait_ge(x_in, (t + 1) * 16)
            if not isinstance(t, int) or t >= 1:
                pe.wait_ge(xT_act, t)
                pe.wait_ge(xT_dve, t)
            for c in range(KC):
                last = nc.tensor.transpose(psX[:, c // 4, P * (c % 4):P * (c % 4) + P], xg[:, P * c:P * c + P],
                                           g["ident"])
            last.then_inc(xT_full, 1)

        def gate_up(t, slot):
            pe.wait_ge(xT_act, t + 1)
            pe.wait_ge(xT_dve, t + 1)
            pe.wait_ge(gate_in, (t + 1) * 16)
            pe.wait_ge(up_in, (t + 1) * 16)
            if not isinstance(t, int) or t >= 1:
                pe.wait_ge(h_ready, t)
            for c in range(KC):
                last = nc.tensor.matmul(psG[:, :].rearrange("p (o g f) -> p o g f", o=1, g=2), xgT[:, c, :],
                                        gu5[:, ds(slot, 1), :, c, :], start=(c == 0), stop=(c == KC - 1))
            last.then_inc(gu_full, 1)

        def transpose_h(t):
            pe.wait_ge(h_ready, t + 1)
            for c in range(EC):
                last = nc.tensor.transpose(psH[:, P * c:P * c + P], h[:, P * c:P * c + P], g["ident"])
            last.then_inc(hT_full, 1)

        def down(t, slot):
            pe.wait_ge(hT_kept, t + 1)
            pe.wait_ge(down_in, (t + 1) * 16)
            if not isinstance(t, int) or t >= 1:
                pe.wait_ge(y_kept, t)
            for n in range(2):
                for c in range(EC):
                    last = nc.tensor.matmul(psY[:, n, :].rearrange("p (o f) -> p o f", o=1), hT[:, c, :],
                                            dn4[:, ds(slot, 1), c, 512 * n:512 * n + 512],
                                            start=(c == 0), stop=(c == EC - 1))
            last.then_inc(y_full, 1)

        transpose_x(0)
        gate_up(0, 0)
        transpose_x(1)
        gate_up(1, 1)
        pe.wait_ge(idx_ready, 1)
        transpose_h(0)
        transpose_x(2)
        down(0, 0)
        n_tiles = tiles(pe)
        with pe.Fori(2, n_tiles) as t:
            gate_up(t, t % WRING)
            transpose_h(t - 1)
            transpose_x(t + 1)
            down(t - 1, (t - 1) % WRING)
        last = last_tile(pe)
        transpose_h(last)
        down(last, last % WRING)

    @blk.scalar
    def _(act):
        def keep_xT(t):
            act.wait_ge(xT_full, t + 1)
            nc.scalar.activation(xgT[:, 0:4, :], psX[:, 0, :].rearrange("p (c m) -> p c m", c=4),
                                 ACT.Copy).then_inc(xT_act, 1)

        def exp_gate(t):
            act.wait_ge(gu_full, t + 1)
            nc.scalar.activation(ex[:, :], psG[:, 0:DE], ACT.Exp, scale=-1.0).then_inc(exp_done, 1)

        def keep_y(t):
            act.wait_ge(y_full, t + 1)
            if not isinstance(t, int) or t >= 1:
                act.wait_ge(y_stored, t * 16)
            nc.scalar.activation(y[:, :].rearrange("p (n f) -> p n f", n=2), psY[:, :, :], ACT.Copy).then_inc(y_kept, 1)
            act.wait_ge(y_kept, t + 1)
            act.dma_start(g["ysd"][ds(t * P, P), :], y[:, :]).then_inc(y_stored, 16)

        keep_xT(0)
        exp_gate(0)
        keep_xT(1)
        n_tiles = tiles(act)
        exp_gate(1)
        keep_xT(2)
        keep_y(0)
        with act.Fori(2, n_tiles) as t:
            exp_gate(t)
            keep_xT(t + 1)
            keep_y(t - 1)
        keep_y(last_tile(act))
        act.wait_ge(y_stored, n_tiles * 16)
        act.sem_inc(turn, 1)

    @blk.vector
    def _(dve):
        dve.wait_ge(map_in, 16)
        nc.vector.tensor_copy(map_f[:, :], map_i[:, :]).then_inc(map_conv, 1)
        dve.wait_ge(map_full, 1)
        nc.vector.tensor_copy(idx[:, :], psH[:, 0:MAXT + 1]).then_inc(idx_ready, 1)

        def keep_xT(t):
            dve.wait_ge(xT_full, t + 1)
            nc.vector.tensor_copy(xgT[:, 4:8, :], psX[:, 1, :].rearrange("p (c m) -> p c m", c=4)).then_inc(xT_dve, 1)

        def hidden(t):
            dve.wait_ge(exp_done, t + 1)
            nc.vector.tensor_scalar(ex[:, :], ex[:, :], 1.0, None, ALU.add).then_inc(dve_own, 1)
            dve.wait_ge(dve_own, 3 * t + 1)
            nc.vector.reciprocal(ex[:, :], ex[:, :]).then_inc(dve_own, 1)
            dve.wait_ge(dve_own, 3 * t + 2)
            nc.vector.tensor_tensor(ex[:, :], psG[:, 0:DE], ex[:, :], ALU.mult).then_inc(dve_own, 1)
            dve.wait_ge(dve_own, 3 * t + 3)
            nc.vector.tensor_tensor(h[:, :], psG[:, DE:2 * DE], ex[:, :], ALU.mult).then_inc(h_ready, 1)

        def keep_hT(t):
            dve.wait_ge(hT_full, t + 1)
            nc.vector.tensor_copy(hT[:, :, :], psH[:, 0:EC * P].rearrange("p (c m) -> p c m", c=EC)) \
                .then_inc(hT_kept, 1)

        keep_xT(0)
        hidden(0)
        keep_xT(1)
        keep_hT(0)
        keep_xT(2)
        hidden(1)
        n_tiles = tiles(dve)
        with dve.Fori(2, n_tiles) as t:
            keep_hT(t - 1)
            keep_xT(t + 1)
            hidden(t)
        keep_hT(last_tile(dve))


def combine(nc, A, g, st, sb, sem, n_stores):
    B = 3
    y1 = [sb(st, f"y1_{i}", [P, D]) for i in range(B)]
    y2 = [sb(st, f"y2_{i}", [P, D]) for i in range(B)]
    gfin = sb(st, "gfin", [P, D])
    o = [sb(st, f"o{i}", [P, D]) for i in range(2)]
    junk = sb(st, "junk3", [P, D], BF16)
    ss = sb(st, "ss3", [P, NT])
    rs = sb(st, "rs3", [P, NT])
    nh = sb(st, "nh3", [P, 1])
    g_in = sem(st, "gfin_in")
    y1_in = [sem(st, f"y1_in{i}") for i in range(B)]
    y2_in = [sem(st, f"y2_in{i}") for i in range(B)]
    added, summed, squared, rs_ready, o_ready = (sem(st, n) for n in ("c_add", "c_sum", "c_sq", "c_rs", "c_o"))
    ms_ready = sem(st, "c_ms")
    o_stored = [sem(st, f"o_stored{i}") for i in range(2)]
    blk = st.enter_context(nc.Block())
    y_rows = A["y_prompt"].rearrange("a s d -> (a s) d")
    ys_rows = A["y_sample"].rearrange("a s d -> (a s) d")

    @blk.sync
    def _(sp):
        sp.dma_start(gfin[:, :], A["final_norm_g"].rearrange("(o d) -> o d", o=1).broadcast_to([P, D])).then_inc(g_in, 16)
        for t in range(NT):
            sp.wait_ge(o_ready, t + 1)
            r = o[t % 2]
            if t == 0:
                sp.dma_start(y_rows[0:P - META, :], r[META:P, :]).then_inc(o_stored[0], 16)
            elif t < FULL:
                sp.dma_start(y_rows[P * t - META:P * t + P - META, :], r[:, :]).then_inc(o_stored[t % 2], 16)
            else:
                sp.dma_start(ys_rows, r[0:NS, :]).then_inc(o_stored[t % 2], 16)
                sp.dma_start(y_rows[SEQ - TAIL:SEQ, :], r[NS:LAST, :]).then_inc(o_stored[t % 2], 16)
        sp.wait_ge(o_stored[0], 16 * 6)
        sp.wait_ge(o_stored[1], 16 * 4)
        sp.wait_ge(g["stores"], 16 * n_stores[0])

    @blk.gpsimd
    def _(pool):
        nc.gpsimd.memset(nh[:, :], -0.5)
        n = [0]

        def gather(t):
            m = rows_of(t)
            if t >= B:
                pool.wait_ge(summed, t - B + 1)
            for j, (dst, done) in enumerate(((y1, y1_in), (y2, y2_in))):
                pool.indirect_dma_start(out=dst[t % B][0:m, :], out_offset=None, in_=g["ysd"],
                                        in_offset=bass.IndirectOffsetOnAxis(ap=g["slot"][0:m, j, t:t + 1], axis=0)) \
                    .then_inc(done[t % B], 16)

        for t in range(min(B, NT)):
            gather(t)
        for t in range(NT):
            m = rows_of(t)
            pool.wait_ge(squared, t + 1)
            nc.gpsimd.tensor_scalar(ss[0:m, t:t + 1], ss[0:m, t:t + 1], 1.0 / D, EPS, ALU.mult, ALU.add) \
                .then_inc(ms_ready, 1)
            pool.wait_ge(ms_ready, t + 1)
            nc.gpsimd.tensor_tensor(rs[0:m, t:t + 1], ss[0:m, t:t + 1], nh[0:m, :], ALU.pow).then_inc(rs_ready, 1)
            if t + B < NT:
                gather(t + B)

    @blk.vector
    def _(dve):
        dve.wait_ge(g_in, 16)

        def finish(t):
            m = rows_of(t)
            dve.wait_ge(rs_ready, t + 1)
            if t >= 2:
                dve.wait_ge(o_stored[t % 2], 16 * (t // 2))
            nc.vector.scalar_tensor_tensor(o[t % 2][0:m, :], g["h"][0:m, t, :], rs[0:m, t:t + 1], gfin[0:m, :],
                                           ALU.mult, ALU.mult).then_inc(o_ready, 1)

        for t in range(NT):
            m = rows_of(t)
            ht = g["h"][0:m, t, :]
            dve.wait_ge(y1_in[t % B], 16 * (t // B + 1))
            nc.vector.scalar_tensor_tensor(ht, y1[t % B][0:m, :], g["gates"][0:m, t, 0:1], ht, ALU.mult, ALU.add) \
                .then_inc(added, 1)
            dve.wait_ge(added, t + 1)
            dve.wait_ge(y2_in[t % B], 16 * (t // B + 1))
            nc.vector.scalar_tensor_tensor(ht, y2[t % B][0:m, :], g["gates"][0:m, t, 1:2], ht, ALU.mult, ALU.add) \
                .then_inc(summed, 1)
            if t >= 1:
                finish(t - 1)
        finish(NT - 1)

    @blk.scalar
    def _(act):
        for t in range(NT):
            m = rows_of(t)
            act.wait_ge(summed, t + 1)
            if t >= 1:
                act.wait_ge(squared, t)
            nc.scalar.activation(junk[0:m, :], g["h"][0:m, t, :], ACT.Square,
                                 accum_out=ss[0:m, t:t + 1]).then_inc(squared, 1)


INS = ["x_prompt", "x_sample", "cache_sb_k", "cache_sb_v", "cache_diff_k", "cache_diff_v", "meta_tokens",
       "norm_mix_g", "w_in", "lambda_q1", "lambda_k1", "lambda_q2", "lambda_k2", "subln_g", "w_out", "norm_ffn_g",
       "w_group", "b_group", "w_router", "b_router", "w_gate", "w_up", "w_down", "final_norm_g"]
OUTS = [("y_prompt", (1, SEQ, D)), ("y_sample", (1, NS, D)),
        ("sb_k_prompt", (1, 1, NPR, SBH, SBD)), ("sb_v_prompt", (1, 1, NPR, SBH, SBD)),
        ("diff_k_prompt", (1, 1, NPR, 2 * DFH, DFD)), ("diff_v_prompt", (1, 1, NPR, DFH, DFV)),
        ("sb_k_sample", (1, 1, NS, SBH, SBD)), ("sb_v_sample", (1, 1, NS, SBH, SBD)),
        ("diff_k_sample", (1, 1, NS, 2 * DFH, DFD)), ("diff_v_sample", (1, 1, NS, DFH, DFV))]


def kernel(**inputs):
    import concourse.bacc as bacc
    from concourse.bass_utils import run_bass_kernel_spmd

    nc = bacc.Bacc("TRN2", target_bir_lowering=False, num_devices=1)
    arrays, aps = {}, {}
    for name in INS:
        a = np.ascontiguousarray(inputs[name])
        arrays[f"in_{name}"] = a
        aps[name] = nc.dram_tensor(f"in_{name}", a.shape, mybir.dt.from_np(a.dtype), kind="ExternalInput").ap()
    const = np.concatenate(list(shape_constants().values()), axis=1)
    arrays["in_const"] = const
    aps["const"] = nc.dram_tensor("in_const", const.shape, F32, kind="ExternalInput").ap()
    for name, shape in OUTS:
        aps[name] = nc.dram_tensor(f"out_{name}", shape, F32, kind="ExternalOutput").ap()
    build(nc, aps)
    r = run_bass_kernel_spmd(nc, [arrays], core_ids=[0])
    return tuple(r.results[0][f"out_{name}"] for name, _ in OUTS)
```

```python
from contextlib import ExitStack

import numpy as np

import concourse.bass as bass
from concourse import mybir

P = 128
F32 = mybir.dt.float32
BF16 = mybir.dt.bfloat16
F32R = mybir.dt.float32r
I32 = mybir.dt.int32
U32 = mybir.dt.uint32
ALU = mybir.AluOpType
ACT = mybir.ActivationFunctionType
AX_X = mybir.AxisListType.X
ds = bass.ds

D = 1024
KC = D // P
SEQ = 1024
META = 16
CHUNK = 64
NS = 32
PAST = 2048
NPR = META + SEQ
FULL = NPR // P
TAIL = NPR - FULL * P
NT = FULL + 1
LAST = NS + TAIL
NTOK = FULL * P + LAST
SBH, SBD = 8, 64
DFH, DFD, DFV = 4, 64, 128
HP = 4
EPS = 1e-6
QSCALE = 0.125
LAM_INIT = 0.2
NEG = -1e30
LN_CAP = 44.0
NG, EPG, NE, DE = 4, 8, 32, 256
EC = DE // P
MAXT = NE + (2 * NTOK) // P
MAPT = MAXT + 1
WRING = 5
EARLY = 3
NOWHERE = float(1 << 20)


def rows_of(t):
    return P if t < FULL else LAST


def shape_constants():
    q = np.arange(P)[:, None]
    k = np.arange(P)[None, :]
    c = {}
    c["ident"] = (q == k).astype(np.float32)
    c["sb_mask"] = np.where(k < q, 0.0, NEG).astype(np.float32)
    reach = np.where(q < META, META, np.where(q < META + CHUNK, META + CHUNK, META + 2 * CHUNK))
    c["df_mask"] = np.where(np.arange(P + META)[None, :] < reach, 0.0, NEG).astype(np.float32)
    c["new_mask"] = np.where(np.arange(NS)[None, :] < q % NS, 0.0, NEG).astype(np.float32)
    c["before"] = (q < k).astype(np.float32)
    c["ones"] = np.ones((P, P), np.float32)
    half = DFD // 8
    inv = np.float32(500000.0) ** (-np.arange(half, dtype=np.float32) * np.float32(2.0) / np.float32(2 * half))
    pos = np.zeros((P, NT), np.float32)
    for t in range(FULL):
        pos[:, t] = P * t + np.arange(P)
    pos[:NS, FULL] = PAST + np.arange(NS)
    pos[NS:LAST, FULL] = FULL * P + np.arange(TAIL)
    ang = (pos[:, :, None] * inv.astype(np.float32)[None, None, :]).astype(np.float32)
    c["cos"] = np.concatenate([np.cos(ang)] * 2, 2).reshape(P, -1).astype(np.float32)
    c["sin"] = np.concatenate([np.sin(ang)] * 2, 2).reshape(P, -1).astype(np.float32)
    valid = np.ones((P, NT), np.float32)
    valid[LAST:, FULL] = 0
    c["valid"] = valid
    token = (P * np.arange(NT)[None, :] + q).astype(np.float32)
    c["pair"] = np.concatenate([(token + 1) * valid, (token + 1 + NTOK) * valid], 1).astype(np.float32)
    c["iota"] = np.broadcast_to(np.arange(P, dtype=np.float32), (P, P)).copy()
    c["fold"] = ((q // 64 == k[:, :64] // 32) & (q % 32 == k[:, :64] % 32)).astype(np.float32)
    c["first_map"] = ((q // 32) % 2 == 0).astype(np.float32)
    c["neg_half"] = np.full((P, 1), -0.5, np.float32)
    return c


CONST = {}
_at = 0
for _n, _a in shape_constants().items():
    CONST[_n] = (_at, _a.shape[1])
    _at += _a.shape[1]
NCONST = _at


def build(nc, A):
    with ExitStack() as keep:
        g = {}

        def sb(stack, name, shape, dt=F32):
            return stack.enter_context(nc.sbuf_tensor(name, shape, dt))

        def sem(stack, name):
            return stack.enter_context(nc.semaphore(name))

        g["const"] = sb(keep, "const", [P, NCONST])
        for n, (a, w) in CONST.items():
            g[n] = g["const"][:, a:a + w]
        g["lam"] = sb(keep, "lam", [P, 8])
        g["mixd"] = nc.dram_tensor("mix_scratch", [NTOK, D], F32).ap()
        g["xn2d"] = nc.dram_tensor("normed_scratch", [NTOK, D], F32).ap()
        g["ysd"] = nc.dram_tensor("expert_rows", [2 * NTOK, D], F32).ap()
        g["stores"] = sem(keep, "stores")
        w_out_stack = keep.enter_context(ExitStack())
        with ExitStack() as att:
            for n in ("sb", "df"):
                g["kT_" + n] = sb(att, "kT_" + n, [P, HP, NPR])
                g["kTnew_" + n] = sb(att, "kTnew_" + n, [P, HP, NS])
                g["vtail_" + n] = sb(att, "vtail_" + n, [P, 512])
                g["vnew_" + n] = sb(att, "vnew_" + n, [P, 512])
                for w in ("tail", "samp"):
                    g[f"qs_{n}_{w}"] = sb(att, f"qs_{n}_{w}", [P, HP, P])
            with ExitStack() as qs:
                for n in ("sb", "df"):
                    g["qT_" + n] = sb(qs, "qT_" + n, [P, HP, FULL * P])
                with ExitStack() as st:
                    n_stores = project(nc, A, g, st, sb, sem)
                g["w_out"] = w_out_stack.enter_context(nc.sbuf_tensor("w_out", [P, KC, 512], F32, side="right"))
                g["w_out_in"] = sem(w_out_stack, "w_out_in")
                for n in ("sb", "df"):
                    g["v_" + n] = att.enter_context(nc.sbuf_tensor("v_" + n, [P, FULL, 512], F32, side="right"))
                with ExitStack() as st:
                    attend(nc, A, g, st, sb, sem)
            with ExitStack() as st:
                stacked(nc, A, g, st, sb, sem)
        g["h"] = sb(keep, "h", [P, NT, D])
        g["gates"] = sb(keep, "gates", [P, NT, 2])
        g["slot_token"] = sb(keep, "slot_token", [P, MAPT], I32)
        g["slot_row"] = sb(keep, "slot_row", [P, MAPT], I32)
        g["tile_expert"] = sb(keep, "tile_expert", [1, MAPT], I32)
        g["n_tiles"] = sb(keep, "n_tiles", [1, 2], I32)
        g["logits"] = sb(keep, "logits", [P, NT, NG + NE])
        with ExitStack() as st:
            mix_out(nc, A, g, st, sb, sem)
        w_out_stack.close()
        with ExitStack() as ring:
            g["w_gu"] = sb(ring, "w_gu", [P, WRING * 2 * KC * DE])
            g["w_dn"] = sb(ring, "w_dn", [P, WRING * EC * D])
            for n in ("gate_in", "up_in", "down_in"):
                g[n] = sem(ring, n)
            g["xg"] = sb(ring, "xg", [P, D])
            g["token_idx"] = sb(ring, "token_idx", [P, 1], I32)
            g["xg_in"], g["idx_copied"] = sem(ring, "xg_in"), sem(ring, "idx_copied")
            g["turn"] = sem(ring, "turn")
            for part in (route, experts):
                with ExitStack() as st:
                    part(nc, A, g, st, sb, sem)
        with ExitStack() as st:
            combine(nc, A, g, st, sb, sem, n_stores)


def project(nc, A, g, st, sb, sem):
    KINDS = [("sb", "q"), ("sb", "k"), ("sb", "v"), ("df", "q"), ("df", "k"), ("df", "v")]
    BW = 256
    NB = 6 * 512 // BW

    def kind_of(b):
        return KINDS[b // 2]

    units = [(0, 0)]
    for t in range(1, NT):
        units += [(0, t), (1, t - 1)]
    units += [(1, NT - 1)] + [(b, t) for b in range(2, NB) for t in range(NT)]
    last_unit = {b: u for u, (b, t) in enumerate(units)}
    first_unit = {b: u for u, (b, t) in reversed(list(enumerate(units)))}
    split_at = {}
    for b in range(1, NB):
        u = 0 if b == 1 else last_unit[b - 2]
        split_at[u] = (b, 0)
        split_at[u + (1 if b <= 2 else 2)] = (b, 1)
    qk_units = [u for u, (b, t) in enumerate(units) if kind_of(b)[1] != "v"]
    qk_of = {u: n for n, u in enumerate(qk_units)}
    rope_of = {u: n for n, u in enumerate([u for u in qk_units if kind_of(units[u][0])[0] == "df"])}
    NAT = 4

    def uses_nat(u):
        return u in qk_of or units[u][1] < FULL

    def nat_stores(u):
        b, t = units[u]
        if kind_of(b)[1] == "q" or not uses_nat(u):
            return 0
        return 2 if t == FULL else 1

    xt = [sb(st, f"x{i}", [P, D]) for i in range(2)]
    gmix = sb(st, "gmix", [P, D])
    xh = sb(st, "xn_hi", [P, KC, NTOK], F32R)
    xl = sb(st, "xn_lo", [P, KC, NTOK], F32R)
    w = [sb(st, "w", [P, KC // 2, BW])[:, :, :]]
    w += [g["qT_df"][:, n, :].rearrange("p (c n) -> p c n", c=KC // 2) for n in range(1, HP)]

    def w_slot(i):
        return i % len(w) if i < 4 * 2 else 0
    wh = [st.enter_context(nc.sbuf_tensor(f"w_hi{i}", [P, KC, BW], F32R, side="right")) for i in range(2)]
    wl = [st.enter_context(nc.sbuf_tensor(f"w_lo{i}", [P, KC, BW], F32R, side="right")) for i in range(2)]
    nat = [sb(st, f"nat{i}", [P, BW]) for i in range(NAT)]
    rot = sb(st, "rot", [P, 2, 4, 16])
    ss = sb(st, "ss", [P, NT])
    rstd = sb(st, "rstd", [P, NT])
    lamv = sb(st, "lamv", [P, 4, DFD])
    psX = st.enter_context(nc.psum_tensor("psX", [P, 2, 512], F32))
    NPS = 4
    psP = st.enter_context(nc.psum_tensor("psP", [P, NPS, 512], F32))
    junk = g["qT_df"][:, 0, :]
    psQ = st.enter_context(nc.psum_tensor("psQ", [P, 2, 512], F32))

    const_in, gmix_in, lam_in = sem(st, "const_in"), sem(st, "gmix_in"), sem(st, "lam_in")
    x_in = [sem(st, f"x_in{i}") for i in range(2)]
    w_in = [sem(st, f"w_in{i}") for i in range(4)]
    w_hi_ready, w_lo_ready = sem(st, "w_hi_ready"), sem(st, "w_lo_ready")
    squared, rstd_ready, xn_ready = sem(st, "squared"), sem(st, "rstd_ready"), sem(st, "xn_ready")
    xT_full, xh_ready, xl_ready = sem(st, "xT_full"), sem(st, "xh_ready"), sem(st, "xl_ready")
    proj_full, proj_kept = sem(st, "proj_full"), sem(st, "proj_kept")
    rope_done, qT_full, qT_kept = sem(st, "rope_done"), sem(st, "qT_full"), sem(st, "qT_kept")
    nat_stored = [sem(st, f"nat_stored{i}") for i in range(NAT)]
    dve_own, pool_own, qs_zeroed = sem(st, "dve_own"), sem(st, "pool_own"), sem(st, "qs_zeroed")
    lam_sum, lam_exp = sem(st, "lam_sum"), sem(st, "lam_exp")
    n_stores = [0]

    x_rows = A["x_prompt"].rearrange("a s d -> (a s) d")
    xs_rows = A["x_sample"].rearrange("a s d -> (a s) d")
    w_dram = A["w_in"][0].rearrange("(c p) n -> p c n", p=P)

    def x_loads(t):
        return sum(2 if s in (0, FULL) else 1 for s in range(t % 2, t + 1, 2))

    def chunks(half):
        return slice(KC // 2 * half, KC // 2 * (half + 1))

    blk = st.enter_context(nc.Block())

    @blk.sync
    def _(sp):
        def load_x(t):
            if t >= 2:
                sp.wait_ge(xT_full, t - 1)
            if t == 0:
                sp.dma_start(xt[0][0:META, :], A["meta_tokens"]).then_inc(x_in[0], 16)
                sp.dma_start(xt[0][META:P, :], x_rows[0:P - META, :]).then_inc(x_in[0], 16)
            elif t < FULL:
                sp.dma_start(xt[t % 2][:, :], x_rows[P * t - META:P * t + P - META, :]).then_inc(x_in[t % 2], 16)
            else:
                sp.dma_start(xt[t % 2][0:NS, :], xs_rows).then_inc(x_in[t % 2], 16)
                sp.dma_start(xt[t % 2][NS:LAST, :], x_rows[SEQ - TAIL:SEQ, :]).then_inc(x_in[t % 2], 16)

        def load_w(b, half):
            i = 2 * b + half
            before = [j for j in range(i) if w_slot(j) == w_slot(i)]
            if before:
                sp.wait_ge(w_lo_ready, before[-1] + 1)
            sp.dma_start(w[w_slot(i)], w_dram[:, chunks(half), BW * b:BW * b + BW]).then_inc(w_in[i % 4], 16)

        load_x(0)
        sp.dma_start(g["const"][:, :], A["const"]).then_inc(const_in, 16)
        sp.dma_start(gmix[:, :], A["norm_mix_g"].broadcast_to([P, D])).then_inc(gmix_in, 16)
        load_w(0, 0)
        load_w(0, 1)
        load_x(1)
        load_w(1, 0)
        load_w(1, 1)
        load_x(2)
        for n, name in enumerate(("lambda_q1", "lambda_k1", "lambda_q2", "lambda_k2")):
            sp.dma_start(lamv[:, n, :], A[name].broadcast_to([P, DFD])).then_inc(lam_in, 16)
        for t in range(3, NT):
            load_x(t)
        for b in range(2, NB):
            for half in range(2):
                load_w(b, half)

    @blk.scalar
    def _(act):
        nc.scalar.preload_act_table_set("natural_log_exp_and_others")

        def square(t):
            m = rows_of(t)
            act.wait_ge(x_in[t % 2], 16 * x_loads(t))
            if t >= 1:
                act.wait_ge(squared, t)
            nc.scalar.activation(junk[0:m, :], xt[t % 2][0:m, :], ACT.Square,
                                 accum_out=ss[0:m, t:t + 1]).then_inc(squared, 1)

        def split_w(b, half):
            i = 2 * b + half
            act.wait_ge(w_in[i % 4], 16 * (i // 4 + 1))
            nc.scalar.activation(wh[b % 2][:, chunks(half), :], w[w_slot(i)], ACT.Copy).then_inc(w_hi_ready, 1)

        def keep_xT(t):
            m = rows_of(t)
            act.wait_ge(xT_full, t + 1)
            for n in range(2):
                nc.scalar.activation(xh[:, chunks(n), P * t:P * t + m],
                                     psX[:, n, 0:4 * m].rearrange("p (c m) -> p c m", c=4),
                                     ACT.Copy).then_inc(xh_ready, 1)

        def keep_proj(u):
            b, t = units[u]
            group, kind = kind_of(b)
            m = rows_of(t)
            act.wait_ge(proj_full, u + 1)
            ps = psP[:, u % NPS, 0:BW]
            if not uses_nat(u):
                cols = slice(BW * (b % 2), BW * (b % 2) + BW)
                nc.scalar.activation(g["vtail_" + group][0:TAIL, cols], ps[NS:LAST, :], ACT.Copy)
                nc.scalar.activation(g["vnew_" + group][0:NS, cols], ps[0:NS, :], ACT.Copy).then_inc(proj_kept, 1)
                return
            before = [s for s in range(u % NAT, u, NAT) if uses_nat(s)]
            if before and before[-1] in qk_of:
                act.wait_ge(qT_full, qk_of[before[-1]] + 1)
            if sum(map(nat_stores, before)):
                act.wait_ge(nat_stored[u % NAT], 16 * sum(map(nat_stores, before)))
            nc.scalar.activation(nat[u % NAT][0:m, :], ps[0:m, :], ACT.Copy,
                                 scale=QSCALE if kind == "q" else 1.0).then_inc(proj_kept, 1)

        square(0)
        split_w(0, 0)
        keep_xT(0)
        split_w(0, 1)
        square(1)
        for u, (b, t) in enumerate(units):
            if b == 0:
                if t + 1 < NT:
                    keep_xT(t + 1)
                if t + 2 < NT:
                    square(t + 2)
            keep_proj(u)
            if u in split_at:
                split_w(*split_at[u])
            if u == first_unit[2]:
                act.wait_ge(lam_sum, 1)
                nc.scalar.activation(g["lam"][:, 2:4], g["lam"][:, 0:2], ACT.Exp).then_inc(lam_exp, 1)

    @blk.gpsimd
    def _(pool):
        for group in ("sb", "df"):
            for who in ("samp", "tail"):
                nc.gpsimd.memset(g[f"qs_{group}_{who}"][:, :, :], 0.0).then_inc(qs_zeroed, 1)
        for t in range(NT):
            m = rows_of(t)
            pool.wait_ge(squared, t + 1)
            nc.gpsimd.tensor_scalar(ss[0:m, t:t + 1], ss[0:m, t:t + 1], 1.0 / D, EPS, ALU.mult, ALU.add) \
                .then_inc(pool_own, 1)
            if t == 0:
                pool.wait_ge(const_in, 16)
            pool.wait_ge(pool_own, t + 1)
            nc.gpsimd.tensor_tensor(rstd[0:m, t:t + 1], ss[0:m, t:t + 1], g["neg_half"][0:m, 0:1], ALU.pow) \
                .then_inc(rstd_ready, 1)
        k_out = {"sb": ("sb_k_prompt", "sb_k_sample"), "df": ("diff_k_prompt", "diff_k_sample")}
        v_out = {"sb": ("sb_v_prompt", "sb_v_sample"), "df": ("diff_v_prompt", "diff_v_sample")}
        for u, (b, t) in enumerate(units):
            group, kind = kind_of(b)
            if kind == "q":
                continue
            names = (k_out if kind == "k" else v_out)[group]
            cols = slice(BW * (b % 2), BW * (b % 2) + BW)
            prompt, samp = (A[n].rearrange("l b t h d -> (l b t) (h d)")[:, cols] for n in names)
            if u in rope_of:
                pool.wait_ge(rope_done, rope_of[u] + 1)
            else:
                pool.wait_ge(proj_kept, u + 1)
            if not uses_nat(u):
                pool.dma_start(samp, g["vnew_" + group][0:NS, cols]).then_inc(g["stores"], 16)
                pool.dma_start(prompt[FULL * P:NPR, :], g["vtail_" + group][0:TAIL, cols]).then_inc(g["stores"], 16)
                n_stores[0] += 2
                continue
            src, done = nat[u % NAT], nat_stored[u % NAT]
            if t < FULL:
                pool.dma_start(prompt[P * t:P * t + P, :], src[:, :]).then_inc(done, 16)
            else:
                pool.dma_start(samp, src[0:NS, :]).then_inc(done, 16)
                pool.dma_start(prompt[FULL * P:NPR, :], src[NS:LAST, :]).then_inc(done, 16)
        for n in range(NAT):
            pool.wait_ge(nat_stored[n], 16 * sum(nat_stores(u) for u in range(n, len(units), NAT)))

    @blk.vector
    def _(dve):
        own = [0]

        def then(ins):
            own[0] += 1
            ins.then_inc(dve_own, 1)
            dve.wait_ge(dve_own, own[0])

        def normalise(t):
            m = rows_of(t)
            dve.wait_ge(rstd_ready, t + 1)
            nc.vector.scalar_tensor_tensor(xt[t % 2][0:m, :], xt[t % 2][0:m, :], rstd[0:m, t:t + 1], gmix[0:m, :],
                                           ALU.mult, ALU.mult).then_inc(xn_ready, 1)

        def split_w(b, half):
            dve.wait_ge(w_hi_ready, 2 * b + half + 1)
            nc.vector.tensor_tensor(wl[b % 2][:, chunks(half), :], w[w_slot(2 * b + half)],
                                    wh[b % 2][:, chunks(half), :].bitcast(F32), ALU.subtract) \
                .then_inc(w_lo_ready, 1)

        def keep_xT(t):
            m = rows_of(t)
            for n in range(2):
                dve.wait_ge(xh_ready, 2 * t + n + 1)
                nc.vector.tensor_tensor(xl[:, chunks(n), P * t:P * t + m],
                                        psX[:, n, 0:4 * m].rearrange("p (c m) -> p c m", c=4),
                                        xh[:, chunks(n), P * t:P * t + m].bitcast(F32), ALU.subtract) \
                    .then_inc(xl_ready, 1)

        def rope(u):
            b, t = units[u]
            m = rows_of(t)
            dve.wait_ge(proj_kept, u + 1)
            v = nat[u % NAT][0:m, :].rearrange("p (h d) -> p h d", h=4)
            x = v[:, :, 0:16]
            if rope_of[u] >= 1:
                dve.wait_ge(rope_done, rope_of[u])
            cos = g["cos"][0:m, 16 * t:16 * t + 16].unsqueeze(1).to_broadcast([m, 4, 16])
            sin = g["sin"][0:m, 16 * t:16 * t + 16].unsqueeze(1).to_broadcast([m, 4, 16])
            nc.vector.tensor_tensor(rot[0:m, 0], x, cos, ALU.mult)
            then(nc.vector.tensor_tensor(rot[0:m, 1], x, sin, ALU.mult))
            nc.vector.tensor_tensor(v[:, :, 0:8], rot[0:m, 0, :, 0:8], rot[0:m, 1, :, 8:16], ALU.subtract)
            nc.vector.tensor_tensor(v[:, :, 8:16], rot[0:m, 0, :, 8:16], rot[0:m, 1, :, 0:8],
                                    ALU.add).then_inc(rope_done, 1)

        def keep_qT(u):
            b, t = units[u]
            group, kind = kind_of(b)
            n = qk_of[u]
            m = rows_of(t)
            dve.wait_ge(qT_full, n + 1)
            ps = psQ[:, n % 2, 0:2 * m].rearrange("p (c m) -> p c m", c=2)
            pairs = slice(2 * (b % 2), 2 * (b % 2) + 2)
            if t < FULL:
                last = nc.vector.tensor_copy(g[f"{kind}T_{group}"][:, pairs, P * t:P * t + P], ps)
            elif kind == "k":
                nc.vector.tensor_copy(g["kT_" + group][:, pairs, FULL * P:NPR], ps[:, :, NS:LAST])
                last = nc.vector.tensor_copy(g["kTnew_" + group][:, pairs, :], ps[:, :, 0:NS])
            else:
                dve.wait_ge(qs_zeroed, 4)
                for who, lo, hi in (("samp", 0, NS), ("tail", NS, LAST)):
                    for i in range(2):
                        p = 2 * (b % 2) + i
                        for half in range(2):
                            c = 32 * (2 * (p % 2) + half)
                            r = slice(64 * half, 64 * half + 64)
                            last = nc.vector.tensor_copy(g[f"qs_{group}_{who}"][r, p, c:c + hi - lo], ps[r, i, lo:hi])
            last.then_inc(qT_kept, 1)

        dve.wait_ge(gmix_in, 16)
        normalise(0)
        split_w(0, 0)
        keep_xT(0)
        split_w(0, 1)
        normalise(1)
        for u, (b, t) in enumerate(units):
            if b == 0:
                if t + 1 < NT:
                    keep_xT(t + 1)
                if t + 2 < NT:
                    normalise(t + 2)
            if u in rope_of:
                rope(u)
            if u >= 1 and u - 1 in qk_of:
                keep_qT(u - 1)
            if u in split_at:
                split_w(*split_at[u])
            if u == first_unit[2]:
                dve.wait_ge(lam_in, 64)
                for n in range(2):
                    then(nc.vector.tensor_tensor(lamv[:, 2 * n, :], lamv[:, 2 * n, :], lamv[:, 2 * n + 1, :],
                                                 ALU.mult))
                    red = nc.vector.reduce_sum(g["lam"][:, n:n + 1], lamv[:, 2 * n, :], AX_X)
                red.then_inc(lam_sum, 1)
        dve.wait_ge(lam_exp, 1)
        lam = g["lam"]
        then(nc.vector.tensor_tensor(lam[:, 5:6], lam[:, 3:4], lam[:, 2:3], ALU.subtract))
        then(nc.vector.tensor_scalar(lam[:, 4:5], lam[:, 5:6], -LAM_INIT, None, ALU.add))
        then(nc.vector.tensor_scalar(lam[:, 7:8], g["first_map"], -1.0, 1.0, ALU.mult, ALU.add))
        then(nc.vector.scalar_tensor_tensor(lam[:, 6:7], lam[:, 7:8], lam[:, 4:5], g["first_map"],
                                            ALU.mult, ALU.add))

    @blk.tensor
    def _(pe):
        ident = g["ident"]

        def transpose_x(t):
            m = rows_of(t)
            pe.wait_ge(xn_ready, t + 1)
            if t >= 1:
                pe.wait_ge(xl_ready, 2 * t)
            for c in range(KC):
                last = nc.tensor.transpose(psX[:, c // 4, (c % 4) * m:(c % 4) * m + m],
                                           xt[t % 2][0:m, P * c:P * c + P], ident[0:m, 0:m])
            last.then_inc(xT_full, 1)

        def products(u):
            b, t = units[u]
            m = rows_of(t)
            if b == 0:
                pe.wait_ge(xl_ready, 2 * (t + 1))
            if u >= NPS:
                pe.wait_ge(proj_kept, u - NPS + 1)
            for c in range(KC):
                if u == 0 and c == KC - 3:
                    transpose_x(1)
                if u == first_unit[b] and c in (0, KC // 2):
                    pe.wait_ge(w_lo_ready, 2 * b + c // (KC // 2) + 1)
                tok = slice(P * t, P * t + m)
                for x, y, first, final in ((xh, wh, c == 0, False), (xh, wl, False, False),
                                           (xl, wh, False, c == KC - 1)):
                    last = nc.tensor.matmul(psP[0:m, u % NPS, 0:BW], x[:, c, tok], y[b % 2][:, c, :],
                                            start=first, stop=final)
            last.then_inc(proj_full, 1)

        def transpose_qk(u):
            n = qk_of[u]
            m = rows_of(units[u][1])
            if u in rope_of:
                pe.wait_ge(rope_done, rope_of[u] + 1)
            else:
                pe.wait_ge(proj_kept, u + 1)
            if n >= 2:
                pe.wait_ge(qT_kept, n - 1)
            for c in range(2):
                last = nc.tensor.transpose(psQ[:, n % 2, c * m:c * m + m],
                                           nat[u % NAT][0:m, P * c:P * c + P], ident[0:m, 0:m])
            last.then_inc(qT_full, 1)

        pe.wait_ge(const_in, 16)
        transpose_x(0)
        for u, (b, t) in enumerate(units):
            if b == 0 and 0 < t < NT - 1:
                transpose_x(t + 1)
            products(u)
            if u >= 1 and u - 1 in qk_of:
                transpose_qk(u - 1)

    return n_stores


def attend(nc, A, g, st, sb, sem):
    jobs = []
    for i in range(FULL):
        for r in range(4):
            jobs += [("S", i, 2 * r), ("S", i, 2 * r + 1), ("Da", i, r), ("Db", i, r)]
    NJ = len(jobs)
    NKP = NPR + 0

    def place(k):
        return ("S1", "S2", "Da", "Db")[k % 4]

    def keys(j):
        kind, i, _ = jobs[j]
        return P * (i + 1) if kind == "S" else min(P * (i + 1) + META, NPR)

    def spill(j):
        return max(0, keys(j) - 1024)

    def key_tiles(j):
        n = keys(j)
        return [(a, min(P, n - a)) for a in range(0, n, P)]

    def groups(j):
        t = key_tiles(j)
        return [] if jobs[j][0] == "Da" else [t[a:a + 4] for a in range(0, len(t), 4)]

    uses, use_of = [], {}
    for k in range(-3, NJ):
        gr = groups(k) if k >= 0 else []
        if gr:
            use_of[("w", k, 0)] = len(uses)
            uses.append(("w", k, 0))
        if k + 3 < NJ and spill(k + 3):
            use_of[("z", k + 3, 0)] = len(uses)
            uses.append(("z", k + 3, 0))
        for n in range(1, len(gr)):
            use_of[("w", k, n)] = len(uses)
            uses.append(("w", k, n))
    wgroup_of = {u: n for n, u in enumerate([u for u in uses if u[0] == "w"])}
    s_of = {j: n for n, j in enumerate([j for j in range(NJ) if jobs[j][0] == "S"])}
    d_of = {j: n for n, j in enumerate([j for j in range(NJ) if jobs[j][0] != "S"])}
    a_of = {j: n for n, j in enumerate([j for j in range(NJ) if jobs[j][0] == "Db"])}
    pv_of = {j: n for n, j in enumerate([j for j in range(NJ) if groups(j)])}

    def count_to(table, j):
        return sum(1 for x in table if x <= j)

    E = [sb(st, f"E{i}", [P, 1024]) for i in range(3)]
    C = [sb(st, f"C{i}", [P, NKP]) for i in range(4)]
    zx = sb(st, "zx", [P, 4, META])
    wT = [sb(st, f"wT{i}", [P, 4, P]) for i in range(3)]
    mix = [sb(st, f"mix{i}", [P, D]) for i in range(2)]
    nm = sb(st, "nm", [P, 2, len(d_of)])
    Z = sb(st, "Z", [P, 2, len(d_of)])
    rZ = sb(st, "rZ", [P, len(d_of)])
    cf = sb(st, "cf", [P, len(a_of)])
    identb = sb(st, "identb", [P, P], BF16)
    maskb = {"S": sb(st, "sb_maskb", [P, P], BF16), "D": sb(st, "df_maskb", [P, P + META], BF16)}
    psZ = st.enter_context(nc.psum_tensor("psZ", [P, 3, 1024], F32))
    psT = st.enter_context(nc.psum_tensor("psT", [P, 512], F32))
    psO = st.enter_context(nc.psum_tensor("psO", [P, 512], F32))

    masks_ready = sem(st, "masks_ready")
    v_in = {grp: [sem(st, f"v_in_{grp}{n}") for n in range(FULL // 2)] for grp in ("sb", "df")}
    qk_full, exp_done, ln_done = sem(st, "qk_full"), sem(st, "exp_done"), sem(st, "ln_done")
    t_ready, w_ready = sem(st, "t_ready"), sem(st, "w_ready")
    max_ready, p_ready, a_ready = sem(st, "max_ready"), sem(st, "p_ready"), sem(st, "a_ready")
    T_full, T_kept, pv_done, o_kept = sem(st, "T_full"), sem(st, "T_kept"), sem(st, "pv_done"), sem(st, "o_kept")
    dve_own, mix_stored = sem(st, "att_dve_own"), [sem(st, f"mix_stored{i}") for i in range(2)]

    blk = st.enter_context(nc.Block())

    @blk.sync
    def _(sp):
        for n in range(FULL // 2):
            for grp, out in (("sb", "sb_v_prompt"), ("df", "diff_v_prompt")):
                rows = A[out].rearrange("l b t h d -> (l b t) (h d)")[2 * P * n:2 * P * (n + 1), :]
                sp.dma_start(g["v_" + grp][:, 2 * n:2 * n + 2, :], rows.rearrange("(t p) n -> p t n", p=P)) \
                    .then_inc(v_in[grp][n], 16)
        for i in range(FULL):
            sp.wait_ge(o_kept, 12 * (i + 1))
            sp.dma_start(g["mixd"][P * i:P * i + P, :], mix[i % 2][:, :]).then_inc(mix_stored[i % 2], 16)
        for b in range(2):
            sp.wait_ge(mix_stored[b], 16 * (FULL // 2))

    @blk.tensor
    def _(pe):
        def scores(j):
            kind, i, h = jobs[j]
            grp = "sb" if kind == "S" else "df"
            half = h % 2 if kind == "S" else (kind == "Db") * 1
            pair = h // 2 if kind == "S" else h
            r = slice(64 * half, 64 * half + 64)
            mask = maskb[kind[0]]
            n, m0 = keys(j), P * i
            if count_to(s_of, j - 3):
                pe.wait_ge(t_ready, count_to(s_of, j - 3))
            if count_to(d_of, j - 3):
                pe.wait_ge(p_ready, count_to(d_of, j - 3))
            for a in range(0, n, 512):
                b = min(a + 512, n)
                if a < 1024:
                    dst = psZ[:, j % 3, a:b]
                else:
                    u = use_of[("z", j, 0)]
                    if u:
                        pe.wait_ge(T_kept, u)
                    dst = psT[:, 0:b - a]
                lo = max(a, m0)
                last = nc.tensor.matmul(dst, g["qT_" + grp][r, pair, m0:m0 + P], g["kT_" + grp][r, pair, a:b],
                                        start=True, stop=(lo >= b))
                if lo < b:
                    last = nc.tensor.matmul(dst[:, lo - a:b - a], identb[:, :], mask[:, lo - m0:b - m0],
                                            start=False, stop=True)
                if a >= 1024:
                    last.then_inc(T_full, 1)
                    last = None
                elif b == min(n, 1024):
                    last.then_inc(qk_full, 1)

        def transposes(j, n):
            kind = jobs[j][0]
            u = use_of[("w", j, n)]
            if n == 0:
                if kind == "S":
                    pe.wait_ge(w_ready, s_of[j] + 1)
                else:
                    pe.wait_ge(a_ready, a_of[j] + 1)
            if u:
                pe.wait_ge(T_kept, u)
            for x, (a, m) in enumerate(groups(j)[n]):
                last = nc.tensor.transpose(psT[0:m, P * x:P * x + P], C[j % 4][:, a:a + m], g["ident"])
            last.then_inc(T_full, 1)

        def values(j, n):
            kind, i, h = jobs[j]
            grp, w = ("sb", SBD) if kind == "S" else ("df", DFV)
            gr = groups(j)
            pe.wait_ge(T_kept, use_of[("w", j, n)] + 1)
            if n == 0 and pv_of[j]:
                pe.wait_ge(o_kept, pv_of[j])
            for x, (a, m) in enumerate(gr[n]):
                if a < FULL * P and a // (2 * P) >= v_loads[grp]:
                    pe.wait_ge(v_in[grp][a // (2 * P)], 16)
                    v_loads[grp] += 1
                v = g["v_" + grp][0:m, a // P, w * h:w * h + w] if a < FULL * P else \
                    g["vtail_" + grp][0:m, w * h:w * h + w]
                last = nc.tensor.matmul(psO[:, 0:w], wT[wgroup_of[("w", j, n)] % 3][0:m, x, :], v,
                                        start=(n == 0 and x == 0), stop=(n == len(gr) - 1 and x == len(gr[n]) - 1))
            last.then_inc(pv_done, 1)

        v_loads = {"sb": 0, "df": 0}
        pe.wait_ge(masks_ready, 1)
        for k in range(-3, NJ):
            gr = groups(k) if k >= 0 else []
            if gr:
                transposes(k, 0)
            if k + 3 < NJ:
                scores(k + 3)
            for n in range(1, len(gr)):
                transposes(k, n)
                values(k, n - 1)
            if gr:
                values(k, len(gr) - 1)

    @blk.scalar
    def _(act):
        def keep_T(use):
            what, j, n = use
            u = use_of[use]
            act.wait_ge(T_full, u + 1)
            if what == "z":
                nc.scalar.activation(zx[:, j % 4, 0:spill(j)], psT[:, 0:spill(j)], ACT.Copy).then_inc(T_kept, 1)
                return
            w = wgroup_of[use]
            if w >= 3:
                act.wait_ge(pv_done, w - 2)
            tiles = groups(j)[n]
            full = [t for t in tiles if t[1] == P]
            last = None
            if full:
                last = nc.scalar.activation(wT[w % 3][:, 0:len(full), :],
                                            psT[:, 0:P * len(full)].rearrange("p (x q) -> p x q", q=P), ACT.Copy)
            if len(full) < len(tiles):
                m, x = tiles[-1][1], len(full)
                last = nc.scalar.activation(wT[w % 3][0:m, x, :], psT[0:m, P * x:P * x + P], ACT.Copy)
            last.then_inc(T_kept, 1)

        def exp_ln(j):
            s, n = s_of[j], keys(j)
            act.wait_ge(qk_full, j + 1)
            if s >= 3:
                act.wait_ge(t_ready, s - 2)
            nc.scalar.activation(E[s % 3][:, 0:n], psZ[:, j % 3, 0:n], ACT.Exp).then_inc(exp_done, 1)
            act.wait_ge(exp_done, s + 1)
            nc.scalar.activation(E[s % 3][:, 0:n], E[s % 3][:, 0:n], ACT.Ln, bias=1.0).then_inc(ln_done, 1)

        def weights(j):
            s, n = s_of[j], keys(j)
            act.wait_ge(t_ready, s + 1)
            nc.scalar.activation(C[j % 4][:, 0:n], C[j % 4][:, 0:n], ACT.Exp).then_inc(w_ready, 1)

        def softmax_exp(j):
            d, n = d_of[j], min(keys(j), 1024)
            act.wait_ge(max_ready, d + 1)
            if j >= 4:
                if jobs[j][0] == "Da":
                    act.wait_ge(a_ready, a_of[j - 3] + 1)
                else:
                    act.wait_ge(T_full, use_of[("w", j - 4, len(groups(j - 4)) - 1)] + 1)
            if spill(j):
                nc.scalar.activation(C[j % 4][:, n:n + spill(j)], zx[:, j % 4, 0:spill(j)], ACT.Exp,
                                     bias=nm[:, 0, d:d + 1], accum_out=Z[:, 1, d:d + 1])
            nc.scalar.activation(C[j % 4][:, 0:n], psZ[:, j % 3, 0:n], ACT.Exp, bias=nm[:, 0, d:d + 1],
                                 accum_out=Z[:, 0, d:d + 1]).then_inc(p_ready, 1)

        def keep_o(j):
            kind, i, h = jobs[j]
            act.wait_ge(pv_done, wgroup_of[("w", j, len(groups(j)) - 1)] + 1)
            if i >= 2 and h == 0 and kind == "S":
                act.wait_ge(mix_stored[i % 2], 16 * (i // 2))
            if kind == "S":
                nc.scalar.activation(mix[i % 2][:, SBD * h:SBD * h + SBD], psO[:, 0:SBD], ACT.Copy) \
                    .then_inc(o_kept, 1)
            else:
                d = d_of[j - 1]
                nc.scalar.activation(mix[i % 2][:, 512 + DFV * h:512 + DFV * h + DFV], psO[:, 0:DFV], ACT.Copy,
                                     scale=rZ[:, d:d + 1]).then_inc(o_kept, 1)

        for k in range(-3, NJ):
            gr = groups(k) if k >= 0 else []
            if gr:
                keep_T(("w", k, 0))
            if k + 3 < NJ and spill(k + 3):
                keep_T(("z", k + 3, 0))
            if k >= 0 and place(k) in ("S1", "S2"):
                softmax_exp(k + 2)
            for n in range(1, len(gr)):
                keep_T(("w", k, n))
            if place(k) in ("S2", "Da") and k + 3 < NJ:
                exp_ln(k + 3)
            if place(k) in ("Db", "S1") and k + 1 < NJ:
                weights(k + 1)
            if gr:
                keep_o(k)

    @blk.vector
    def _(dve):
        own = [0]

        def then(ins):
            own[0] += 1
            ins.then_inc(dve_own, 1)
            dve.wait_ge(dve_own, own[0])

        def row_max(j):
            d, n = d_of[j], min(keys(j), 1024)
            dve.wait_ge(qk_full, j + 1)
            if not spill(j):
                nc.vector.reduce_max(nm[:, 0, d:d + 1], psZ[:, j % 3, 0:n], AX_X, negate=True).then_inc(max_ready, 1)
                return
            dve.wait_ge(T_kept, use_of[("z", j, 0)] + 1)
            nc.vector.reduce_max(nm[:, 1, d:d + 1], zx[:, j % 4, 0:spill(j)], AX_X, negate=True)
            then(nc.vector.reduce_max(nm[:, 0, d:d + 1], psZ[:, j % 3, 0:n], AX_X, negate=True))
            nc.vector.tensor_tensor(nm[:, 0, d:d + 1], nm[:, 0, d:d + 1], nm[:, 1, d:d + 1],
                                    ALU.min).then_inc(max_ready, 1)

        def stick(j):
            s, n = s_of[j], keys(j)
            e, c, z = E[s % 3][:, 0:n], C[j % 4][:, 0:n], psZ[:, j % 3, 0:n]
            dve.wait_ge(ln_done, s + 1)
            then(nc.vector.scalar_tensor_tensor(e, e, LN_CAP, z, ALU.min, ALU.max))
            if j >= 4:
                dve.wait_ge(T_full, use_of[("w", j - 4, len(groups(j - 4)) - 1)] + 1)
            then(nc.vector.tensor_tensor_scan(c[:, ::-1], e[:, ::-1], e[:, ::-1], 0.0, ALU.add, ALU.max))
            nc.vector.tensor_tensor(c, z, c, ALU.subtract).then_inc(t_ready, 1)

        def mix_maps(j):
            d, n, a = d_of[j], keys(j), a_of[j]
            dve.wait_ge(p_ready, d + 1)
            if spill(j):
                then(nc.vector.tensor_tensor(Z[:, 0, d - 1:d + 1], Z[:, 0, d - 1:d + 1], Z[:, 1, d - 1:d + 1], ALU.add))
            then(nc.vector.reciprocal(rZ[:, d - 1:d + 1], Z[:, 0, d - 1:d + 1]))
            then(nc.vector.tensor_scalar(cf[:, a:a + 1], Z[:, 0, d - 1:d], rZ[:, d:d + 1], g["lam"][:, 4:5],
                                         ALU.mult, ALU.mult))
            nc.vector.scalar_tensor_tensor(C[j % 4][:, 0:n], C[j % 4][:, 0:n], cf[:, a:a + 1], C[(j - 1) % 4][:, 0:n],
                                           ALU.mult, ALU.add).then_inc(a_ready, 1)

        nc.vector.tensor_copy(identb[:, :], g["ident"])
        nc.vector.tensor_copy(maskb["S"][:, :], g["sb_mask"])
        nc.vector.tensor_copy(maskb["D"][:, :], g["df_mask"]).then_inc(masks_ready, 1)
        for k in range(-3, NJ):
            if place(k) == "S1":
                row_max(k + 2)
                row_max(k + 3)
            elif place(k) == "S2" and k >= 0:
                mix_maps(k + 2)
            elif place(k) in ("Da", "Db") and k + 2 < NJ:
                stick(k + 2)


def stacked(nc, A, g, st, sb, sem):
    jobs = [(who, grp, gi) for who in ("tail", "samp") for grp in ("sb", "df") for gi in range(2)]
    NJ = len(jobs)
    NK = PAST + NS

    def keys(j):
        return NPR if jobs[j][0] == "tail" else NK

    def old(j):
        return FULL * P if jobs[j][0] == "tail" else PAST

    def chunks(j):
        return [(a, min(a + 512, keys(j))) for a in range(0, keys(j), 512)]

    def groups(j):
        n = keys(j)
        t = [(a, min(P, n - a)) for a in range(0, n, P)]
        return [t[a:a + 4] for a in range(0, len(t), 4)]

    NKT = PAST // P
    KT_AT = {1: "sb", 5: "df"}
    uses, use_of = [], {}

    def use(x):
        use_of[x] = len(uses)
        uses.append(x)

    for n in range(NKT):
        use(("k", "sb", n))
    for k in range(NJ):
        for n in range(len(groups(k))):
            use(("w", k, n))
        if k + 2 == 5:
            for n in range(NKT):
                use(("k", "df", n))
    wgroup_of = {u: n for n, u in enumerate([u for u in uses if u[0] == "w"])}
    chunk_of = {}
    for j in range(NJ):
        for n in range(len(chunks(j))):
            chunk_of[(j, n)] = len(chunk_of)
    s_of = {j: n for n, j in enumerate([j for j in range(NJ) if jobs[j][1] == "sb"])}
    d_of = {j: n for n, j in enumerate([j for j in range(NJ) if jobs[j][1] == "df"])}
    vloads = [(j, n) for j in range(NJ) if jobs[j][0] == "samp" for n in range(NKT // 4)]
    vload_of = {x: n for n, x in enumerate(vloads)}
    kloads = [(grp, n) for grp in ("sb", "df") for n in range(NKT // 4)]
    kload_of = {x: n for n, x in enumerate(kloads)}

    kTc = sb(st, "kTc", [P, HP, PAST])
    Kc = [sb(st, f"Kc{i}", [P, 4, 512]) for i in range(2)]
    Vc = [sb(st, f"Vc{i}", [P, 4, 256]) for i in range(2)]
    zs = [sb(st, f"zs{i}", [P, NK]) for i in range(2)]
    E = sb(st, "Es", [P, NK])
    wT = [sb(st, f"wTs{i}", [P, 4, P]) for i in range(3)]
    mix8 = sb(st, "mix8", [LAST, D])
    nm = sb(st, "nms", [P, len(d_of)])
    Z = sb(st, "Zs", [P, len(d_of)])
    rZ = sb(st, "rZs", [P, len(d_of)])
    R = sb(st, "R", [P, 64])
    psZ = st.enter_context(nc.psum_tensor("psZs", [P, 3, 512], F32))
    psT = st.enter_context(nc.psum_tensor("psTs", [P, 2, 512], F32))
    psO = st.enter_context(nc.psum_tensor("psOs", [P, 2, 512], F32))

    k_in = [sem(st, f"k_in{i}") for i in range(2)]
    v_in = [sem(st, f"v_in{i}") for i in range(2)]
    qk_full, z_kept = sem(st, "s_qk_full"), sem(st, "s_z_kept")
    exp_done, ln_done, t_ready, w_ready = (sem(st, n) for n in ("s_exp", "s_ln", "s_t", "s_w"))
    max_ready, p_ready, r_ready = (sem(st, n) for n in ("s_max", "s_p", "s_r"))
    T_full, T_kept, pv_done, o_kept = (sem(st, n) for n in ("s_T_full", "s_T_kept", "s_pv", "s_o"))
    dve_own, mix_stored = sem(st, "s_own"), sem(st, "s_mix")

    blk = st.enter_context(nc.Block())

    @blk.sync
    def _(sp):
        cache_k = {"sb": A["cache_sb_k"], "df": A["cache_diff_k"]}
        cache_v = {"sb": A["cache_sb_v"], "df": A["cache_diff_v"]}

        def load_k(x):
            grp, n = x
            m = kload_of[x]
            if m >= 2:
                g2, n2 = kloads[m - 2]
                sp.wait_ge(T_full, use_of[("k", g2, 4 * n2 + 3)] + 1)
            src = cache_k[grp].rearrange("l b t h d -> (l b t) (h d)")[512 * n:512 * n + 512, :]
            sp.dma_start(Kc[m % 2][:, :, :], src.rearrange("(x p) f -> p x f", p=P)).then_inc(k_in[m % 2], 16)

        def load_v(x):
            j, n = x
            m = vload_of[x]
            if m >= 2:
                sp.wait_ge(pv_done, wgroup_of[("w", *vloads[m - 2])] + 1)
            _, grp, gi = jobs[j]
            src = cache_v[grp].rearrange("l b t h d -> (l b t) (h d)")[512 * n:512 * n + 512, 256 * gi:256 * gi + 256]
            sp.dma_start(Vc[m % 2][:, :, :], src.rearrange("(x p) f -> p x f", p=P)).then_inc(v_in[m % 2], 16)

        for n in range(NKT // 4):
            load_k(("sb", n))
        load_v(vloads[0])
        load_v(vloads[1])
        sp.dma_start(g["w_out"][:, :, :], A["w_out"][0].rearrange("(c p) n -> p c n", p=P)[:, :, 0:512]) \
            .then_inc(g["w_out_in"], 16)
        load_k(("df", 0))
        load_k(("df", 1))
        load_k(("df", 2))
        load_k(("df", 3))
        for x in vloads[2:]:
            load_v(x)
        sp.wait_ge(o_kept, NJ)
        sp.dma_start(g["mixd"][FULL * P:NTOK, :], mix8[:, :]).then_inc(mix_stored, 16)
        sp.wait_ge(mix_stored, 16)

    @blk.tensor
    def _(pe):
        def scores(j):
            who, grp, gi = jobs[j]
            q = g[f"qs_{grp}_{who}"]
            for n, (a, b) in enumerate(chunks(j)):
                c = chunk_of[(j, n)]
                if c >= 3:
                    pe.wait_ge(z_kept, c - 2)
                own = b - a < 512
                if who == "samp" and n == 0:
                    pe.wait_ge(T_kept, use_of[("k", grp, NKT - 1)] + 1)
                for pp in range(2):
                    if who == "tail":
                        k = g["kT_" + grp][:, 2 * gi + pp, a:b]
                    else:
                        k = g["kTnew_" + grp][:, 2 * gi + pp, :] if own else kTc[:, 2 * gi + pp, a:b]
                    masked = own and grp == "sb"
                    last = nc.tensor.matmul(psZ[:, c % 3, 0:b - a], q[:, 2 * gi + pp, :], k,
                                            start=(pp == 0), stop=(pp == 1 and not masked))
                if masked:
                    last = nc.tensor.matmul(psZ[:, c % 3, 0:b - a], g["ident"], g["new_mask"][:, 0:b - a],
                                            start=False, stop=True)
                last.then_inc(qk_full, 1)

        def cache_keys(grp):
            for n in range(NKT):
                u = use_of[("k", grp, n)]
                m = kload_of[(grp, n // 4)]
                if n % 4 == 0:
                    pe.wait_ge(k_in[m % 2], 16 * (m // 2 + 1))
                if u >= 2:
                    pe.wait_ge(T_kept, u - 1)
                for c in range(HP):
                    last = nc.tensor.transpose(psT[:, u % 2, P * c:P * c + P],
                                               Kc[m % 2][:, n % 4, P * c:P * c + P], g["ident"])
                last.then_inc(T_full, 1)

        def transposes(j, n):
            u = use_of[("w", j, n)]
            stick = jobs[j][1] == "sb"
            if n == 0:
                if stick:
                    pe.wait_ge(w_ready, s_of[j] + 1)
                else:
                    pe.wait_ge(r_ready, d_of[j] + 1)
            if u >= 2:
                pe.wait_ge(T_kept, u - 1)
            for x, (a, m) in enumerate(groups(j)[n]):
                if stick:
                    last = nc.tensor.transpose(psT[0:m, u % 2, P * x:P * x + P], zs[j % 2][:, a:a + m],
                                               g["ident"])
                else:
                    last = nc.tensor.matmul(psT[0:m, u % 2, P * x:P * x + 64], zs[j % 2][:, a:a + m], R[:, :],
                                            start=True, stop=True)
            last.then_inc(T_full, 1)

        def values(j, n):
            who, grp, gi = jobs[j]
            gr = groups(j)
            u = use_of[("w", j, n)]
            M = P if grp == "sb" else 64
            pe.wait_ge(T_kept, u + 1)
            if n == 0 and j >= 2:
                pe.wait_ge(o_kept, j - 1)
            if (j, n) in vload_of:
                v = vload_of[(j, n)]
                pe.wait_ge(v_in[v % 2], 16 * (v // 2 + 1))
            f = slice(256 * gi, 256 * gi + 256)
            for x, (a, m) in enumerate(gr[n]):
                if who == "tail":
                    val = g["v_" + grp][:, a // P, f] if m == P else g["vtail_" + grp][0:m, f]
                else:
                    val = Vc[v % 2][:, x, :] if m == P else g["vnew_" + grp][0:m, f]
                last = nc.tensor.matmul(psO[0:M, j % 2, 0:256], wT[wgroup_of[("w", j, n)] % 3][0:m, x, 0:M], val,
                                        start=(n == 0 and x == 0), stop=(n == len(gr) - 1 and x == len(gr[n]) - 1))
            last.then_inc(pv_done, 1)

        scores(0)
        cache_keys("sb")
        scores(1)
        for k in range(NJ):
            n_g = len(groups(k))
            transposes(k, 0)
            for n in range(1, n_g):
                transposes(k, n)
                values(k, n - 1)
            values(k, n_g - 1)
            if k + 2 < NJ:
                scores(k + 2)
            if k + 2 == 5:
                cache_keys("df")

    @blk.scalar
    def _(act):
        def keep_z(j, n):
            a, b = chunks(j)[n]
            c = chunk_of[(j, n)]
            act.wait_ge(qk_full, c + 1)
            if n == 0 and j >= 2:
                act.wait_ge(T_full, use_of[("w", j - 2, len(groups(j - 2)) - 1)] + 1)
            nc.scalar.activation(zs[j % 2][:, a:b], psZ[:, c % 3, 0:b - a], ACT.Copy).then_inc(z_kept, 1)

        def exp_ln(j):
            s, n = s_of[j], keys(j)
            act.wait_ge(z_kept, chunk_of[(j, len(chunks(j)) - 1)] + 1)
            if s >= 1:
                act.wait_ge(t_ready, s)
            nc.scalar.activation(E[:, 0:n], zs[j % 2][:, 0:n], ACT.Exp).then_inc(exp_done, 1)
            act.wait_ge(exp_done, s + 1)
            nc.scalar.activation(E[:, 0:n], E[:, 0:n], ACT.Ln, bias=1.0).then_inc(ln_done, 1)

        def last_exp(j):
            n = keys(j)
            if jobs[j][1] == "sb":
                act.wait_ge(t_ready, s_of[j] + 1)
                nc.scalar.activation(zs[j % 2][:, 0:n], zs[j % 2][:, 0:n], ACT.Exp).then_inc(w_ready, 1)
            else:
                d = d_of[j]
                act.wait_ge(max_ready, d + 1)
                nc.scalar.activation(zs[j % 2][:, 0:n], zs[j % 2][:, 0:n], ACT.Exp, bias=nm[:, d:d + 1],
                                     accum_out=Z[:, d:d + 1]).then_inc(p_ready, 1)

        def keep_o(j):
            who, grp, gi = jobs[j]
            act.wait_ge(pv_done, wgroup_of[("w", j, len(groups(j)) - 1)] + 1)
            r0, nq = (0, NS) if who == "samp" else (NS, TAIL)
            if grp == "sb":
                for s in range(4):
                    c = SBD * (4 * gi + s)
                    last = nc.scalar.activation(mix8[r0:r0 + nq, c:c + SBD],
                                                psO[32 * s:32 * s + nq, j % 2, SBD * s:SBD * s + SBD], ACT.Copy)
            else:
                for s in range(2):
                    c = 512 + DFV * (2 * gi + s)
                    last = nc.scalar.activation(mix8[r0:r0 + nq, c:c + DFV],
                                                psO[32 * s:32 * s + nq, j % 2, DFV * s:DFV * s + DFV], ACT.Copy)
            last.then_inc(o_kept, 1)

        for n in range(len(chunks(0))):
            keep_z(0, n)
        exp_ln(0)
        for n in range(len(chunks(1))):
            keep_z(1, n)
        last_exp(0)
        for k in range(NJ):
            if k + 1 < NJ and k + 1 in s_of:
                exp_ln(k + 1)
            if k + 1 < NJ:
                last_exp(k + 1)
            keep_o(k)
            if k + 2 < NJ:
                for n in range(len(chunks(k + 2))):
                    keep_z(k + 2, n)

    @blk.vector
    def _(dve):
        own = [0]

        def then(ins):
            own[0] += 1
            ins.then_inc(dve_own, 1)
            dve.wait_ge(dve_own, own[0])

        def keep_keys(grp):
            for n in range(NKT):
                u = use_of[("k", grp, n)]
                dve.wait_ge(T_full, u + 1)
                if grp == "df" and n == 0:
                    dve.wait_ge(qk_full, chunk_of[(5, len(chunks(5)) - 1)] + 1)
                nc.vector.tensor_copy(kTc[:, :, P * n:P * n + P],
                                      psT[:, u % 2, :].rearrange("p (c k) -> p c k", c=HP)).then_inc(T_kept, 1)

        def keep_w(j, n):
            u = use_of[("w", j, n)]
            w = wgroup_of[("w", j, n)]
            M = P if jobs[j][1] == "sb" else 64
            dve.wait_ge(T_full, u + 1)
            if w >= 3:
                dve.wait_ge(pv_done, w - 2)
            tiles = groups(j)[n]
            full = [t for t in tiles if t[1] == P]
            ps = psT[:, u % 2, :].rearrange("p (x q) -> p x q", q=P)
            last = None
            if full:
                last = nc.vector.tensor_copy(wT[w % 3][:, 0:len(full), 0:M], ps[:, 0:len(full), 0:M])
            if len(full) < len(tiles):
                m, x = tiles[-1][1], len(full)
                last = nc.vector.tensor_copy(wT[w % 3][0:m, x, 0:M], ps[0:m, x, 0:M])
            last.then_inc(T_kept, 1)

        def body(j, part):
            n, z = keys(j), zs[j % 2]
            if jobs[j][1] == "df":
                d = d_of[j]
                if part == 0:
                    dve.wait_ge(z_kept, chunk_of[(j, len(chunks(j)) - 1)] + 1)
                    nc.vector.reduce_max(nm[:, d:d + 1], z[:, 0:n], AX_X, negate=True).then_inc(max_ready, 1)
                elif part == 1:
                    dve.wait_ge(p_ready, d + 1)
                    then(nc.vector.reciprocal(rZ[:, d:d + 1], Z[:, d:d + 1]))
                    then(nc.vector.tensor_scalar(rZ[:, d:d + 1], rZ[:, d:d + 1], g["lam"][:, 6:7], None, ALU.mult))
                elif d >= 1:
                    before = [x for x in d_of if x < j][-1]
                    dve.wait_ge(T_full, use_of[("w", before, len(groups(before)) - 1)] + 1)
                if part == 2:
                    nc.vector.tensor_scalar(R[:, :], g["fold"], rZ[:, d:d + 1], None, ALU.mult).then_inc(r_ready, 1)
                return
            e = E[:, 0:n]
            if part == 0:
                dve.wait_ge(ln_done, s_of[j] + 1)
                then(nc.vector.scalar_tensor_tensor(e, e, LN_CAP, z[:, 0:n], ALU.min, ALU.max))
            elif part == 1:
                then(nc.vector.tensor_tensor_scan(e[:, ::-1], e[:, ::-1], e[:, ::-1], 0.0, ALU.add, ALU.max))
            else:
                nc.vector.tensor_tensor(z[:, 0:n], z[:, 0:n], e, ALU.subtract).then_inc(t_ready, 1)

        keep_keys("sb")
        for part in range(3):
            body(0, part)
        for k in range(NJ):
            for n in range(len(groups(k))):
                keep_w(k, n)
                if n < 3 and k + 1 < NJ:
                    body(k + 1, n)
            if k + 2 == 5:
                keep_keys("df")


def load_expert(sp, nc, A, g, e):
    gu = g["w_gu"][:, :].rearrange("p (s g c f) -> p s g c f", s=WRING, g=2, c=KC)
    dn = g["w_dn"][:, :].rearrange("p (s c n) -> p s c n", s=WRING, c=EC)
    if e >= 1:
        sp.wait_ge(g["up_in"], 16 * e)
    sp.dma_start(gu[:, e, 0], A["w_gate"][0, e].rearrange("(p c) f -> p c f", c=KC)).then_inc(g["gate_in"], 16)
    if e >= 1:
        sp.wait_ge(g["down_in"], 16 * e)
    sp.dma_start(gu[:, e, 1], A["w_up"][0, e].rearrange("(p c) f -> p c f", c=KC)).then_inc(g["up_in"], 16)
    sp.wait_ge(g["gate_in"], 16 * (e + 1))
    sp.dma_start(dn[:, e], A["w_down"][0, e].rearrange("(c p) n -> p c n", p=P)).then_inc(g["down_in"], 16)


def mix_out(nc, A, g, st, sb, sem):
    mixt = [sb(st, f"mixt{i}", [P, D]) for i in range(2)]
    xt = [sb(st, f"xr{i}", [P, D]) for i in range(2)]
    xn2 = [sb(st, f"xn2{i}", [P, D]) for i in range(2)]
    w = [g["w_out"], sb(st, "w_out_right", [P, KC, 512])]
    wh = [sb(st, f"wo_hi{n}", [P, KC, 512], F32R) for n in range(2)]
    wl = [sb(st, f"wo_lo{n}", [P, KC, 512], F32R) for n in range(2)]
    mh = [sb(st, f"mT_hi{i}", [P, KC, P], F32R) for i in range(2)]
    ml = [sb(st, f"mT_lo{i}", [P, KC, P], F32R) for i in range(2)]
    wr = sb(st, "wr", [P, KC, NG + NE])
    bias = sb(st, "bias", [P, NG + NE])
    gffn = sb(st, "gffn", [P, D])
    gsub = sb(st, "gsub", [P, DFV])
    xT = sb(st, "xT", [P, KC, P])
    junk = sb(st, "junk2", [P, D], BF16)
    junk4 = sb(st, "junk4", [P, 2, 512], BF16)
    ss = sb(st, "ss2", [P, NT, 5])
    rs = sb(st, "rs2", [P, NT, 5])
    nh = sb(st, "nh", [P, 4])
    psT = st.enter_context(nc.psum_tensor("psTm", [P, 2, 512], F32))
    psY = st.enter_context(nc.psum_tensor("psYm", [P, 2, 1024], F32))
    psR = st.enter_context(nc.psum_tensor("psR", [P, 512], F32))

    mix_in = [sem(st, f"mix_in{i}") for i in range(2)]
    x_in = [sem(st, f"xr_in{i}") for i in range(2)]
    small_in, w_hi_ready, w_lo_ready = sem(st, "small_in"), sem(st, "wo_hi_ready"), sem(st, "wo_lo_ready")
    gsub_in = sem(st, "gsub_in")
    sub_sq, sub_rs, sub_done = sem(st, "sub_sq"), sem(st, "sub_rs"), sem(st, "sub_done")
    T_full, T_act, T_dve = sem(st, "m_T_full"), sem(st, "m_T_act"), sem(st, "m_T_dve")
    y_full, h_ready, h_sq, h_rs, xn_ready = (sem(st, n) for n in ("y_full", "h_ready", "h_sq", "h_rs", "xn2_ready"))
    r_full, r_kept = sem(st, "r_full"), sem(st, "r_kept")
    xn_stored = [sem(st, f"xn_stored{i}") for i in range(2)]
    dve_own, pool_own = sem(st, "m_own"), sem(st, "m_pool_own")

    x_rows = A["x_prompt"].rearrange("a s d -> (a s) d")
    xs_rows = A["x_sample"].rearrange("a s d -> (a s) d")
    uses = [("m", 0)]
    for t in range(NT + 1):
        if t + 1 < NT:
            uses.append(("m", t + 1))
        if t >= 1:
            uses.append(("x", t - 1))
    use_of = {u: n for n, u in enumerate(uses)}

    def x_loads(t):
        return sum(2 if s in (0, FULL) else 1 for s in range(t % 2, t + 1, 2))

    blk = st.enter_context(nc.Block())

    @blk.sync
    def _(sp):
        def load_mix(t):
            m = rows_of(t)
            if t >= 2:
                sp.wait_ge(T_full, use_of[("m", t - 2)] + 1)
            sp.dma_start(mixt[t % 2][0:m, :], g["mixd"][P * t:P * t + m, :]).then_inc(mix_in[t % 2], 16)

        def load_x(t):
            if t >= 2:
                sp.wait_ge(h_ready, t - 1)
            if t == 0:
                sp.dma_start(xt[0][0:META, :], A["meta_tokens"]).then_inc(x_in[0], 16)
                sp.dma_start(xt[0][META:P, :], x_rows[0:P - META, :]).then_inc(x_in[0], 16)
            elif t < FULL:
                sp.dma_start(xt[t % 2][:, :], x_rows[P * t - META:P * t + P - META, :]).then_inc(x_in[t % 2], 16)
            else:
                sp.dma_start(xt[t % 2][0:NS, :], xs_rows).then_inc(x_in[t % 2], 16)
                sp.dma_start(xt[t % 2][NS:LAST, :], x_rows[SEQ - TAIL:SEQ, :]).then_inc(x_in[t % 2], 16)

        load_mix(0)
        sp.dma_start(gsub[:, :], A["subln_g"].broadcast_to([P, DFV])).then_inc(gsub_in, 16)
        sp.dma_start(w[1][:, :, :], A["w_out"][0].rearrange("(c p) n -> p c n", p=P)[:, :, 512:D]) \
            .then_inc(g["w_out_in"], 16)

        load_mix(1)
        load_x(0)
        load_x(1)
        sp.dma_start(gffn[:, :], A["norm_ffn_g"].broadcast_to([P, D])).then_inc(small_in, 16)
        sp.dma_start(wr[:, :, 0:NG], A["w_group"][0].rearrange("(p c) n -> p c n", c=KC)).then_inc(small_in, 16)
        sp.dma_start(wr[:, :, NG:], A["w_router"][0].rearrange("(p c) n -> p c n", c=KC)).then_inc(small_in, 16)
        sp.dma_start(bias[:, 0:NG], A["b_group"].broadcast_to([P, NG])).then_inc(small_in, 16)
        sp.dma_start(bias[:, NG:], A["b_router"].broadcast_to([P, NE])).then_inc(small_in, 16)
        for t in range(2, NT):
            load_mix(t)
            load_x(t)

    @blk.gpsimd
    def _(pool):
        own = [0]

        def then(ins):
            own[0] += 1
            ins.then_inc(pool_own, 1)
            pool.wait_ge(pool_own, own[0])

        then(nc.gpsimd.memset(nh[:, :], -0.5))

        def sub(t):
            m = rows_of(t)
            pool.wait_ge(sub_sq, t + 1)
            then(nc.gpsimd.tensor_scalar(ss[0:m, t, 0:4], ss[0:m, t, 0:4], 1.0 / DFV, EPS, ALU.mult, ALU.add))
            nc.gpsimd.tensor_tensor(rs[0:m, t, 0:4], ss[0:m, t, 0:4], nh[0:m, :], ALU.pow).then_inc(sub_rs, 1)

        def full(t):
            m = rows_of(t)
            pool.wait_ge(h_sq, t + 1)
            then(nc.gpsimd.tensor_scalar(ss[0:m, t, 4:5], ss[0:m, t, 4:5], 1.0 / D, EPS, ALU.mult, ALU.add))
            nc.gpsimd.tensor_tensor(rs[0:m, t, 4:5], ss[0:m, t, 4:5], nh[0:m, 0:1], ALU.pow).then_inc(h_rs, 1)

        def store(t):
            m = rows_of(t)
            pool.wait_ge(xn_ready, t + 1)
            pool.dma_start(g["xn2d"][P * t:P * t + m, :], xn2[t % 2][0:m, :]).then_inc(xn_stored[t % 2], 16)

        sub(0)
        sub(1)
        for t in range(NT):
            if t + 2 < NT:
                sub(t + 2)
            full(t)
            store(t)
        for b in range(2):
            pool.wait_ge(xn_stored[b], 16 * len(range(b, NT, 2)))

    @blk.scalar
    def _(act):
        def sub(t):
            m = rows_of(t)
            act.wait_ge(mix_in[t % 2], 16 * (t // 2 + 1))
            for h in range(DFH):
                last = nc.scalar.activation(junk4[0:m, t % 2, DFV * h:DFV * h + DFV], mixt[t % 2][0:m, 512 + DFV * h:512 + DFV * h + DFV],
                                            ACT.Square, accum_out=ss[0:m, t, h:h + 1])
            last.then_inc(sub_sq, 1)

        def split_w(i):
            n, c = i // 2, slice(4 * (i % 2), 4 * (i % 2) + 4)
            act.wait_ge(g["w_out_in"], 16 * (n + 1))
            nc.scalar.activation(wh[n][:, c, :], w[n][:, c, :], ACT.Copy).then_inc(w_hi_ready, 1)

        def keep_T(use):
            u = use_of[use]
            m = rows_of(use[1])
            act.wait_ge(T_full, u + 1)
            if use[0] == "m":
                hi = mh[use[1] % 2][:, :, 0:m].rearrange("p (n c) m -> p n c m", n=2)
                nc.scalar.activation(hi, psT[:, :, 0:4 * m].rearrange("p n (c m) -> p n c m", c=4),
                                     ACT.Copy).then_inc(T_act, 1)
            else:
                nc.scalar.activation(xT[:, 0:4, 0:m], psT[:, 0, 0:4 * m].rearrange("p (c m) -> p c m", c=4),
                                     ACT.Copy).then_inc(T_act, 1)

        def square(t):
            m = rows_of(t)
            act.wait_ge(h_ready, t + 1)
            if t >= 1:
                act.wait_ge(h_sq, t)
            nc.scalar.activation(junk[0:m, :], g["h"][0:m, t, :], ACT.Square,
                                 accum_out=ss[0:m, t, 4:5]).then_inc(h_sq, 1)

        split_w(0)
        split_w(1)
        sub(0)
        keep_T(("m", 0))
        split_w(2)
        sub(1)
        split_w(3)
        for t in range(NT + 1):
            if t + 1 < NT:
                if t >= 1:
                    act.wait_ge(y_full, t)
                keep_T(("m", t + 1))
            if t >= 1:
                keep_T(("x", t - 1))
            if t + 2 < NT:
                sub(t + 2)
            if t < NT:
                square(t)

    @blk.vector
    def _(dve):
        own = [0]

        def then(ins):
            own[0] += 1
            ins.then_inc(dve_own, 1)
            dve.wait_ge(dve_own, own[0])

        def sub(t):
            m = rows_of(t)
            dve.wait_ge(sub_rs, t + 1)
            for h in range(DFH):
                o = mixt[t % 2][0:m, 512 + DFV * h:512 + DFV * h + DFV]
                last = nc.vector.scalar_tensor_tensor(o, o, rs[0:m, t, h:h + 1], gsub[0:m, :], ALU.mult, ALU.mult)
            last.then_inc(sub_done, 1)

        def split_w(i):
            n, c = i // 2, slice(4 * (i % 2), 4 * (i % 2) + 4)
            dve.wait_ge(w_hi_ready, i + 1)
            nc.vector.tensor_tensor(wl[n][:, c, :], w[n][:, c, :], wh[n][:, c, :].bitcast(F32),
                                    ALU.subtract).then_inc(w_lo_ready, 1)

        def keep_T(use):
            u = use_of[use]
            m = rows_of(use[1])
            if use[0] == "m":
                dve.wait_ge(T_act, u + 1)
                for n in range(2):
                    c = slice(4 * n, 4 * n + 4)
                    last = nc.vector.tensor_tensor(ml[use[1] % 2][:, c, 0:m],
                                                   psT[:, n, 0:4 * m].rearrange("p (c m) -> p c m", c=4),
                                                   mh[use[1] % 2][:, c, 0:m].bitcast(F32), ALU.subtract)
                last.then_inc(T_dve, 1)
            else:
                dve.wait_ge(T_full, u + 1)
                nc.vector.tensor_copy(xT[:, 4:8, 0:m],
                                      psT[:, 1, 0:4 * m].rearrange("p (c m) -> p c m", c=4)).then_inc(T_dve, 1)

        def residual(t):
            m = rows_of(t)
            dve.wait_ge(y_full, t + 1)
            dve.wait_ge(x_in[t % 2], 16 * x_loads(t))
            nc.vector.tensor_tensor(g["h"][0:m, t, :], psY[0:m, t % 2, :], xt[t % 2][0:m, :],
                                    ALU.add).then_inc(h_ready, 1)

        def normalise(t):
            m = rows_of(t)
            dve.wait_ge(h_rs, t + 1)
            if t >= 2:
                dve.wait_ge(xn_stored[t % 2], 16 * (t // 2))
                dve.wait_ge(T_full, use_of[("x", t - 2)] + 1)
            swap = "p (f c) -> p c f"
            if t == 0:
                dve.wait_ge(small_in, 80)
            nc.vector.scalar_tensor_tensor(xn2[t % 2][0:m, :].rearrange("p (c f) -> p c f", c=KC),
                                           g["h"][0:m, t, :].rearrange(swap, c=KC), rs[0:m, t, 4:5],
                                           gffn[0:m, :].rearrange(swap, c=KC), ALU.mult, ALU.mult) \
                .then_inc(xn_ready, 1)

        def keep_logits(t):
            m = rows_of(t)
            dve.wait_ge(r_full, t + 1)
            if t == 0:
                dve.wait_ge(small_in, 80)
            nc.vector.tensor_tensor(g["logits"][0:m, t, :], psR[0:m, 0:NG + NE], bias[0:m, :],
                                    ALU.add).then_inc(r_kept, 1)

        then(nc.vector.memset(g["logits"][:, :, :], 0.0))
        split_w(0)
        split_w(1)
        dve.wait_ge(gsub_in, 16)
        then(nc.vector.tensor_scalar(gsub[:, :], gsub[:, :], 1.0 - LAM_INIT, None, ALU.mult))
        sub(0)
        keep_T(("m", 0))
        split_w(2)
        sub(1)
        split_w(3)
        for t in range(NT + 1):
            if t + 1 < NT:
                if t >= 1:
                    dve.wait_ge(y_full, t)
                keep_T(("m", t + 1))
            if t >= 1:
                keep_T(("x", t - 1))
            if t + 2 < NT:
                sub(t + 2)
            if t < NT:
                residual(t)
                normalise(t)
            if t >= 1:
                keep_logits(t - 1)

    @blk.tensor
    def _(pe):
        def transpose(use):
            u = use_of[use]
            t = use[1]
            m = rows_of(t)
            if use[0] == "m":
                pe.wait_ge(sub_done, t + 1)
            else:
                pe.wait_ge(xn_ready, t + 1)
            if u >= 1:
                pe.wait_ge(T_act, u)
                pe.wait_ge(T_dve, u)
            src = (mixt if use[0] == "m" else xn2)[t % 2]
            for c in range(KC):
                last = nc.tensor.transpose(psT[:, c // 4, (c % 4) * m:(c % 4) * m + m],
                                           src[0:m, P * c:P * c + P], g["ident"][0:m, 0:m])
            last.then_inc(T_full, 1)

        def outputs(t, n):
            m = rows_of(t)
            u = use_of[("m", t)]
            if n == 0:
                pe.wait_ge(T_act, u + 1)
                pe.wait_ge(T_dve, u + 1)
                if t >= 2:
                    pe.wait_ge(h_ready, t - 1)
            for c in range(KC):
                if t == 0 and c % 4 == 0:
                    pe.wait_ge(w_lo_ready, 2 * n + c // 4 + 1)
                for x, y, first, final in ((mh, wh, c == 0, False), (mh, wl, False, False),
                                           (ml, wh, False, c == KC - 1)):
                    last = nc.tensor.matmul(psY[0:m, t % 2, 512 * n:512 * n + 512], x[t % 2][:, c, 0:m],
                                            y[n][:, c, :], start=first, stop=final)
            if n == 1:
                last.then_inc(y_full, 1)

        def router(t):
            m = rows_of(t)
            u = use_of[("x", t)]
            pe.wait_ge(T_act, u + 1)
            pe.wait_ge(T_dve, u + 1)
            if t >= 1:
                pe.wait_ge(r_kept, t)
            else:
                pe.wait_ge(small_in, 80)
            for c in range(KC):
                last = nc.tensor.matmul(psR[0:m, 0:NG + NE], xT[:, c, 0:m], wr[:, c, :],
                                        start=(c == 0), stop=(c == KC - 1))
            last.then_inc(r_full, 1)

        transpose(("m", 0))
        for t in range(NT + 1):
            if 0 < t < NT - 1:
                transpose(("m", t + 1))
            if t < NT:
                outputs(t, 0)
            if t == 0:
                transpose(("m", 1))
            if t >= 1:
                transpose(("x", t - 1))
            if t < NT:
                outputs(t, 1)
            if t >= 1:
                router(t - 1)


def gather_tile(pool, nc, g, t):
    nc.gpsimd.tensor_copy(g["token_idx"][:, :], g["slot_token"][:, ds(t, 1)]).then_inc(g["idx_copied"], 1)
    pool.wait_ge(g["idx_copied"], t + 1)
    pool.sem_inc(g["turn"], 1)
    pool.indirect_dma_start(out=g["xg"][:, :], out_offset=None, in_=g["xn2d"],
                            in_offset=bass.IndirectOffsetOnAxis(ap=g["token_idx"][:, 0:1], axis=0),
                            bounds_check=NTOK - 1, oob_is_err=False).then_inc(g["xg_in"], 16)


def route(nc, A, g, st, sb, sem):
    gpad = sb(st, "gpad", [P, NT, 8])
    gm = sb(st, "gm", [P, NT, 8])
    gi = sb(st, "gi", [P, NT, 8], U32)
    gf = sb(st, "gf", [P, NT])
    ge = sb(st, "ge", [P, NT, NG])
    gw = sb(st, "gw", [P, NT])
    oh = sb(st, "oh", [P, NT, NG])
    pr = sb(st, "pr", [P, NT, EPG, NG])
    sel = sb(st, "sel", [P, NT, EPG])
    em = sb(st, "em", [P, NT, 8])
    ei = sb(st, "ei", [P, NT, 8], U32)
    ef = sb(st, "ef", [P, NT, 2])
    dd = sb(st, "dd", [P, NT])
    M = sb(st, "M", [P, 2, NT, NE])
    Ms = sb(st, "Ms", [P, NT, NE])
    pos = sb(st, "pos", [P, NT, NE])
    tot = sb(st, "tot", [P, NE, NT])
    upto = sb(st, "upto", [P, NE, NT])
    carry = sb(st, "carry", [P, NE, NT])
    cnt = sb(st, "cnt", [P, NE])
    cnt_i = sb(st, "cnt_i", [P, NE], I32)
    nt = sb(st, "nt", [P, NE])
    incl = sb(st, "incl", [P, NE])
    shift = sb(st, "shift", [P, NE])
    far = Ms
    place = sb(st, "place", [P, 2, NT])
    slot_i = sb(st, "slot_i", [P, 2, NT], I32)
    tile_i = sb(st, "tile_i", [P, 2, NT], I32)
    row_f = sb(st, "row_f", [P, 2 * NT])
    tile_f = sb(st, "tile_f", [P, 2 * NT])
    HOT = 4
    in_row = sb(st, "in_row", [P, HOT, P])
    in_tile = sb(st, "in_tile", [P, 2 * NT, MAPT])
    cmp = sb(st, "cmp", [1, MAPT - NE, NE])
    te = sb(st, "te", [1, MAPT])
    number = sb(st, "number", [P, MAPT])
    empty = sb(st, "empty", [P, MAPT])
    psA = st.enter_context(nc.psum_tensor("psA", [P, 512], F32))
    psB = st.enter_context(nc.psum_tensor("psB", [P, 512], F32))
    psMap = st.enter_context(nc.psum_tensor("psMap", [P, 512], F32))
    g_sub, g_exp, d_sub, d_exp = (sem(st, n) for n in ("g_sub", "g_exp", "d_sub", "d_exp"))
    pairs_ready, counts_full, one_hot_ready, map_parts = (sem(st, n) for n in ("pairs", "counts", "one_hot", "map_parts"))
    dve_own, map_ready, zeroed = sem(st, "r_own"), sem(st, "map_ready"), sem(st, "zeroed")
    blk = st.enter_context(nc.Block())

    @blk.gpsimd
    def _(pool):
        nc.gpsimd.memset(g["xg"][:, :], 0.0).then_inc(zeroed, 1)
        pool.wait_ge(zeroed, 1)
        pool.wait_ge(map_ready, 1)
        gather_tile(pool, nc, g, 0)

    @blk.sync
    def _(sp):
        for e in range(EARLY):
            load_expert(sp, nc, A, g, e)

    @blk.vector
    def _(dve):
        own = [0]

        def then(ins):
            own[0] += 1
            ins.then_inc(dve_own, 1)
            dve.wait_ge(dve_own, own[0])

        def bc(ap, shape, axis):
            return ap.unsqueeze(axis).to_broadcast(shape)

        V = nc.vector
        GL = g["logits"][:, :, 0:NG]
        EL = g["logits"][:, :, NG:].rearrange("p t (g e) -> p t e g", g=NG)
        then(V.memset(gpad[:, :, :], -3e38))
        then(V.tensor_copy(gpad[:, :, 0:NG], GL))
        for t in range(NT):
            last = V.max(gm[:, t, :], gpad[:, t, :])
        then(last)
        for t in range(NT):
            last = V.max_index(gi[:, t, :], gm[:, t, :], gpad[:, t, :])
        then(last)
        V.tensor_tensor(ge[:, :, :], GL, gm[:, :, 0:1].to_broadcast([P, NT, NG]), ALU.subtract).then_inc(g_sub, 1)
        then(V.tensor_copy(gf[:, :], gi[:, :, 0]))
        then(V.tensor_tensor(oh[:, :, :], bc(gf[:, :], [P, NT, NG], 2), bc(g["iota"][:, 0:NG], [P, NT, NG], 1),
                             ALU.is_equal))
        for t in range(NT):
            last = V.tensor_tensor(pr[:, t, :, :], EL[:, t, :, :], bc(oh[:, t, :], [P, EPG, NG], 1), ALU.mult)
        then(last)
        then(V.reduce_sum(sel[:, :, :], pr[:, :, :, :], AX_X))
        for t in range(NT):
            last = V.max(em[:, t, :], sel[:, t, :])
        then(last)
        for t in range(NT):
            last = V.max_index(ei[:, t, :], em[:, t, :], sel[:, t, :])
        then(last)
        V.tensor_tensor(dd[:, :], em[:, :, 1], em[:, :, 0], ALU.subtract).then_inc(d_sub, 1)
        then(V.tensor_copy(ef[:, :, :], ei[:, :, 0:2]))
        for n in range(2):
            last = V.scalar_tensor_tensor(ef[:, :, n], gf[:, :], float(EPG), ef[:, :, n], ALU.mult, ALU.add)
        then(last)
        for n in range(2):
            last = V.tensor_tensor(M[:, n], bc(ef[:, :, n], [P, NT, NE], 2), bc(g["iota"][:, 0:NE], [P, NT, NE], 1),
                                   ALU.is_equal)
        then(last)
        then(V.tensor_tensor(Ms[:, :, :], M[:, 0], M[:, 1], ALU.add))
        V.tensor_tensor(Ms[:, FULL, :], Ms[:, FULL, :], g["valid"][:, FULL:].to_broadcast([P, NE]), ALU.mult) \
            .then_inc(pairs_ready, 1)
        dve.wait_ge(g_exp, 1)
        then(V.reduce_sum(gw[:, :], ge[:, :, :], AX_X))
        then(V.reciprocal(gw[:, :], gw[:, :]))
        dve.wait_ge(d_exp, 1)
        then(V.tensor_scalar(gf[:, :], dd[:, :], 1.0, None, ALU.add))
        then(V.reciprocal(gf[:, :], gf[:, :]))
        then(V.tensor_tensor(g["gates"][:, :, 0], gf[:, :], gw[:, :], ALU.mult))
        then(V.tensor_tensor(g["gates"][:, :, 1], g["gates"][:, :, 0], dd[:, :], ALU.mult))
        then(V.memset(carry[:, :, :], 1.0))
        then(V.memset(carry[:, :, 0:1], 0.0))
        dve.wait_ge(counts_full, 1)
        then(V.tensor_copy(tot[:, :, :], psB[:, 0:NT * NE].rearrange("p (t e) -> p e t", e=NE)))
        then(V.tensor_tensor_scan(upto[:, :, :].rearrange("p e t -> p (e t)"),
                                  carry[:, :, :].rearrange("p e t -> p (e t)"),
                                  tot[:, :, :].rearrange("p e t -> p (e t)"), 0.0, ALU.mult, ALU.add))
        V.tensor_copy(cnt[:, :], upto[:, :, NT - 1])
        then(V.tensor_tensor(tot[:, :, :], upto[:, :, :], tot[:, :, :], ALU.subtract))
        then(V.tensor_tensor(pos[:, :, :], psA[:, 0:NT * NE].rearrange("p (t e) -> p t e", e=NE),
                             tot[:, :, :].rearrange("p e t -> p t e"), ALU.add))
        then(V.tensor_scalar(cnt_i[:, :], cnt[:, :], float(P - 1), None, ALU.add))
        then(V.tensor_scalar(cnt_i[:, :], cnt_i[:, :], 7, None, ALU.logical_shift_right))
        then(V.tensor_copy(nt[:, :], cnt_i[:, :]))
        then(V.tensor_scalar(nt[:, :], nt[:, :], -1.0, 0.0, ALU.add, ALU.max))
        then(V.tensor_tensor_scan(incl[:, :], nt[:, :], nt[:, :], 0.0, ALU.add, ALU.max))
        then(V.tensor_tensor(shift[:, :], incl[:, :], nt[:, :], ALU.subtract))
        then(V.tensor_tensor(shift[:, :], shift[:, :], g["iota"][:, 0:NE], ALU.subtract))
        then(V.tensor_scalar(shift[:, :], shift[:, :], float(NE - 1), float(P), ALU.add, ALU.mult))
        then(V.scalar_tensor_tensor(far[:, :, :], pos[:, :, :], float(P), bc(shift[:, :], [P, NT, NE], 1),
                                    ALU.is_ge, ALU.mult))
        then(V.tensor_tensor(pos[:, :, :], pos[:, :, :], far[:, :, :], ALU.add))
        for n in range(2):
            last = V.tensor_tensor(M[:, n], M[:, n], pos[:, :, :], ALU.mult)
        then(last)
        then(V.reduce_sum(place[:, :, :], M[:, :, :, :], AX_X))
        flat = "p n t -> p (n t)"
        then(V.scalar_tensor_tensor(slot_i[:, :, :], ef[:, :, :].rearrange("p t n -> p n t"), float(P),
                                    place[:, :, :], ALU.mult, ALU.add))
        then(V.tensor_scalar(tile_i[:, :, :], slot_i[:, :, :], 7, None, ALU.logical_shift_right))
        then(V.tensor_copy(tile_f[:, :], tile_i[:, :, :].rearrange(flat)))
        V.tensor_copy(row_f[:, :], slot_i[:, :, :].rearrange(flat))
        then(V.tensor_tensor(in_tile[:, :, :], bc(tile_f[:, :], [P, 2 * NT, MAPT], 2),
                             bc(g["iota"][:, 0:MAPT], [P, 2 * NT, MAPT], 1), ALU.is_equal))
        then(V.scalar_tensor_tensor(row_f[:, :], tile_f[:, :], -float(P), row_f[:, :], ALU.mult, ALU.add))
        for n in range(2 * NT):
            if n >= HOT:
                dve.wait_ge(map_parts, n - HOT + 1)
            V.tensor_scalar(in_row[:, n % HOT, :], g["iota"], row_f[:, n:n + 1], g["pair"][:, n:n + 1],
                            ALU.is_equal, ALU.mult).then_inc(one_hot_ready, 1)
        then(V.tensor_tensor(cmp[:, :, :], bc(incl[0:1, :], [1, MAPT - NE, NE], 1),
                             bc(g["iota"][0:1, 0:MAPT - NE], [1, MAPT - NE, NE], 2), ALU.is_le))
        then(V.reduce_sum(te[:, NE:], cmp[:, :, :], AX_X))
        V.tensor_scalar(g["tile_expert"][:, NE:], te[:, NE:], float(NE - 1), None, ALU.min)
        V.tensor_copy(g["tile_expert"][:, 0:NE], g["iota"][0:1, 0:NE])
        V.tensor_scalar(g["n_tiles"][:, 0:1], incl[0:1, NE - 1:NE], float(NE), None, ALU.add)
        V.tensor_scalar(g["n_tiles"][:, 1:2], incl[0:1, NE - 1:NE], float(NE - 2), None, ALU.add)
        dve.wait_ge(map_parts, 2 * NT)
        then(V.tensor_scalar(empty[:, :], psMap[:, 0:MAPT], 0.0, NOWHERE, ALU.is_equal, ALU.mult))
        then(V.scalar_tensor_tensor(number[:, :], psMap[:, 0:MAPT], -1.0, empty[:, :], ALU.add, ALU.add))
        V.tensor_copy(g["slot_row"][:, :], number[:, :])
        then(V.tensor_scalar(empty[:, :], number[:, :], float(NTOK), -float(NTOK), ALU.is_ge, ALU.mult))
        V.tensor_tensor(g["slot_token"][:, :], number[:, :], empty[:, :], ALU.add).then_inc(map_ready, 1)

    @blk.scalar
    def _(act):
        act.wait_ge(g_sub, 1)
        nc.scalar.activation(ge[:, :, :], ge[:, :, :], ACT.Exp).then_inc(g_exp, 1)
        act.wait_ge(d_sub, 1)
        nc.scalar.activation(dd[:, :], dd[:, :], ACT.Exp).then_inc(d_exp, 1)

    @blk.tensor
    def _(pe):
        pe.wait_ge(pairs_ready, 1)
        flat = Ms[:, :, :].rearrange("p t e -> p (t e)")
        nc.tensor.matmul(psA[:, 0:NT * NE], g["before"], flat, start=True, stop=True)
        nc.tensor.matmul(psB[:, 0:NT * NE], g["ones"], flat, start=True, stop=True).then_inc(counts_full, 1)
        for n in range(2 * NT):
            pe.wait_ge(one_hot_ready, n + 1)
            nc.tensor.matmul(psMap[:, 0:MAPT], in_row[:, n % HOT, :], in_tile[:, n, :],
                             start=(n == 0), stop=(n == 2 * NT - 1)).then_inc(map_parts, 1)


def experts(nc, A, g, st, sb, sem):
    gu5 = g["w_gu"][:, :].rearrange("p (s g c f) -> p s g c f", s=WRING, g=2, c=KC)
    dn4 = g["w_dn"][:, :].rearrange("p (s c n) -> p s c n", s=WRING, c=EC)
    idx2 = sb(st, "idx2", [P, 1], I32)
    xg = g["xg"]
    xgT = sb(st, "xgT", [P, KC, P])
    ex = sb(st, "ex", [P, DE])
    h = sb(st, "hid", [P, DE])
    gu = sb(st, "gate_up", [P, 2 * DE])
    hTh, hTl = sb(st, "hT_hi", [P, EC, P], F32R), sb(st, "hT_lo", [P, EC, P], F32R)
    dh, dl = sb(st, "down_hi", [P, EC, D], F32R), sb(st, "down_lo", [P, EC, D], F32R)
    y = sb(st, "y", [P, D])
    psX = st.enter_context(nc.psum_tensor("psXe", [P, 2, 512], F32))
    psG = st.enter_context(nc.psum_tensor("psG", [P, 512], F32))
    psH = st.enter_context(nc.psum_tensor("psH", [P, 512], F32))
    psY = st.enter_context(nc.psum_tensor("psYe", [P, 2, 512], F32))
    gate_in, up_in, down_in = g["gate_in"], g["up_in"], g["down_in"]
    x_in, row_copied = g["xg_in"], sem(st, "row_copied")
    xT_full, xT_kept = sem(st, "e_xT_full"), sem(st, "e_xT_kept")
    gu_full, exp_done, h_ready = sem(st, "gu_full"), sem(st, "e_exp"), sem(st, "hid_ready")
    hT_full, hT_kept, y_full, y_kept, y_stored = (sem(st, n) for n in ("hT_full", "hT_kept", "e_y_full", "e_y_kept",
                                                                      "y_stored"))
    gu_kept, hTh_ready, dh_ready, dl_ready = (sem(st, n) for n in ("gu_kept", "hTh_ready", "down_hi_ready",
                                                                   "down_lo_ready"))
    dve_own, turn = sem(st, "e_own"), g["turn"]
    wg = A["w_gate"].rearrange("l e (p c) f -> (l e) p c f", c=KC)
    wu = A["w_up"].rearrange("l e (p c) f -> (l e) p c f", c=KC)
    wd = A["w_down"].rearrange("l e (c p) n -> (l e) p c n", p=P)

    blk = st.enter_context(nc.Block())

    def tiles(eng):
        return eng.value_load(g["n_tiles"][0:1, 0:1], min_val=NE, max_val=MAXT)

    def last_but_one(eng):
        return eng.value_load(g["n_tiles"][0:1, 1:2], min_val=NE - 2, max_val=MAXT - 2)

    def last_tile(eng):
        return last_but_one(eng) + 1

    @blk.sync
    def _(sp):
        def load(t, slot):
            e = sp.value_load(g["tile_expert"][0:1, ds(t, 1)], min_val=0, max_val=NE - 1)
            for last_but_one, tiles_in, sem_in, dst, src in ((up_in, t, gate_in, gu5[:, ds(slot, 1), 0], wg),
                                                             (down_in, t, up_in, gu5[:, ds(slot, 1), 1], wu),
                                                             (gate_in, t + 1, down_in, dn4[:, ds(slot, 1)], wd)):
                sp.wait_ge(last_but_one, tiles_in * 16)
                sp.dma_start(dst, src[ds(e, 1)].rearrange("o p c f -> p o c f")).then_inc(sem_in, 16)

        for e in range(EARLY, WRING):
            load_expert(sp, nc, A, g, e)
        with sp.Fori(WRING, tiles(sp)) as t:
            sp.wait_ge(y_full, t - (WRING - 1))
            load(t, t % WRING)

    @blk.gpsimd
    def _(pool):
        def next_gather(t):
            pool.wait_ge(x_in, t * 16)
            pool.wait_ge(xT_full, t)
            gather_tile(pool, nc, g, t)

        def scatter(t):
            if not isinstance(t, int) or t >= 1:
                pool.wait_ge(y_stored, t * 16)
            nc.gpsimd.tensor_copy(idx2[:, :], g["slot_row"][:, ds(t, 1)]).then_inc(row_copied, 1)
            pool.wait_ge(row_copied, t + 1)
            pool.wait_ge(y_kept, t + 1)
            pool.sem_inc(turn, 1)
            pool.indirect_dma_start(out=g["ysd"], out_offset=bass.IndirectOffsetOnAxis(ap=idx2[:, 0:1], axis=0),
                                    in_=y[:, :], in_offset=None,
                                    bounds_check=2 * NTOK - 1, oob_is_err=False).then_inc(y_stored, 16)

        next_gather(1)
        next_gather(2)
        next_gather(3)
        scatter(0)
        n_tiles = tiles(pool)
        with pool.Fori(4, n_tiles + 1) as t:
            next_gather(t)
            scatter(t - 3)
        before_last = last_but_one(pool)
        scatter(before_last)
        scatter(before_last + 1)
        pool.wait_ge(x_in, (n_tiles + 1) * 16)
        pool.sem_inc(turn, 1)
        pool.wait_ge(y_stored, n_tiles * 16)
        pool.sem_inc(turn, 1)

    @blk.tensor
    def _(pe):
        def transpose_x(t):
            pe.wait_ge(x_in, (t + 1) * 16)
            if not isinstance(t, int) or t >= 1:
                pe.wait_ge(xT_kept, t)
            for c in range(KC):
                last = nc.tensor.transpose(psX[:, c // 4, P * (c % 4):P * (c % 4) + P], xg[:, P * c:P * c + P],
                                           g["ident"])
            last.then_inc(xT_full, 1)

        def transpose_h(t):
            pe.wait_ge(h_ready, t + 1)
            for c in range(EC):
                last = nc.tensor.transpose(psH[:, P * c:P * c + P], h[:, P * c:P * c + P], g["ident"])
            last.then_inc(hT_full, 1)

        def gate_up(t, slot, h_of=None):
            pe.wait_ge(xT_kept, t + 1)
            pe.wait_ge(gate_in, (t + 1) * 16)
            pe.wait_ge(up_in, (t + 1) * 16)
            if not isinstance(t, int) or t >= 1:
                pe.wait_ge(gu_kept, t)
            for c in range(KC):
                if c == KC // 2 and h_of is not None:
                    transpose_h(h_of)
                last = nc.tensor.matmul(psG[:, :].rearrange("p (o g f) -> p o g f", o=1, g=2), xgT[:, c, :],
                                        gu5[:, ds(slot, 1), :, c, :], start=(c == 0), stop=(c == KC - 1))
            last.then_inc(gu_full, 1)

        def down(t):
            pe.wait_ge(dl_ready, EC * t + EC)
            pe.wait_ge(hT_kept, t + 1)
            if not isinstance(t, int) or t >= 1:
                pe.wait_ge(y_kept, t)
            for n in range(2):
                for c in range(EC):
                    for x, w, first, final in ((hTh, dh, c == 0, False), (hTh, dl, False, False),
                                               (hTl, dh, False, c == EC - 1)):
                        last = nc.tensor.matmul(psY[:, n, :], x[:, c, :], w[:, c, 512 * n:512 * n + 512],
                                                start=first, stop=final)
            last.then_inc(y_full, 1)

        transpose_x(0)
        gate_up(0, 0)
        transpose_x(1)
        gate_up(1, 1, 0)
        transpose_x(2)
        down(0)
        n_tiles = tiles(pe)
        with pe.Fori(2, n_tiles) as t:
            gate_up(t, t % WRING, t - 1)
            transpose_x(t + 1)
            down(t - 1)
        last = last_tile(pe)
        transpose_h(last)
        down(last)

    @blk.scalar
    def _(act):
        def keep_xT(t):
            act.wait_ge(xT_full, t + 1)
            nc.scalar.activation(xgT[:, :, :].rearrange("p c m -> p (c m)"), psX[:, :, :].rearrange("p n f -> p (n f)"),
                                 ACT.Copy).then_inc(xT_kept, 1)

        def split_down(t, slot):
            act.wait_ge(down_in, (t + 1) * 16)
            if not isinstance(t, int) or t >= 1:
                act.wait_ge(y_full, t)
            for c in range(EC):
                nc.scalar.activation(dh[:, c:c + 1, :], dn4[:, ds(slot, 1), c, :], ACT.Copy).then_inc(dh_ready, 1)

        def exp_gate(t):
            act.wait_ge(gu_full, t + 1)
            if not isinstance(t, int) or t >= 1:
                act.wait_ge(h_ready, t)
            nc.scalar.activation(gu[:, :], psG[:, :], ACT.Copy).then_inc(gu_kept, 1)
            act.wait_ge(gu_kept, t + 1)
            nc.scalar.activation(ex[:, :], gu[:, 0:DE], ACT.Exp, scale=-1.0).then_inc(exp_done, 1)

        def keep_hT(t):
            act.wait_ge(hT_full, t + 1)
            nc.scalar.activation(hTh[:, :, :], psH[:, 0:EC * P].rearrange("p (c m) -> p c m", c=EC),
                                 ACT.Copy).then_inc(hTh_ready, 1)

        def keep_y(t):
            act.wait_ge(y_full, t + 1)
            if not isinstance(t, int) or t >= 1:
                act.wait_ge(y_stored, t * 16)
            nc.scalar.activation(y[:, :], psY[:, :, :].rearrange("p n f -> p (n f)"),
                                 ACT.Copy).then_inc(y_kept, 1)

        keep_xT(0)
        split_down(0, 0)
        exp_gate(0)
        keep_xT(1)
        n_tiles = tiles(act)
        keep_hT(0)
        exp_gate(1)
        keep_xT(2)
        keep_y(0)
        with act.Fori(2, n_tiles) as t:
            split_down(t - 1, (t - 1) % WRING)
            keep_hT(t - 1)
            exp_gate(t)
            keep_xT(t + 1)
            keep_y(t - 1)
        last = last_tile(act)
        split_down(last, last % WRING)
        keep_hT(last)
        keep_y(last)

    @blk.vector
    def _(dve):
        def hidden(t):
            dve.wait_ge(exp_done, t + 1)
            nc.vector.tensor_scalar(ex[:, :], ex[:, :], 1.0, None, ALU.add).then_inc(dve_own, 1)
            dve.wait_ge(dve_own, 3 * t + 1)
            nc.vector.reciprocal(ex[:, :], ex[:, :]).then_inc(dve_own, 1)
            dve.wait_ge(dve_own, 3 * t + 2)
            nc.vector.tensor_tensor(ex[:, :], gu[:, 0:DE], ex[:, :], ALU.mult).then_inc(dve_own, 1)
            dve.wait_ge(dve_own, 3 * t + 3)
            nc.vector.tensor_tensor(h[:, :], gu[:, DE:2 * DE], ex[:, :], ALU.mult).then_inc(h_ready, 1)

        def split_down(t, slot):
            for c in range(EC):
                dve.wait_ge(dh_ready, EC * t + c + 1)
                nc.vector.tensor_tensor(dl[:, c:c + 1, :], dn4[:, ds(slot, 1), c, :],
                                        dh[:, c:c + 1, :].bitcast(F32), ALU.subtract).then_inc(dl_ready, 1)

        def keep_hT(t):
            dve.wait_ge(hTh_ready, t + 1)
            nc.vector.tensor_tensor(hTl[:, :, :], psH[:, 0:EC * P].rearrange("p (c m) -> p c m", c=EC),
                                    hTh[:, :, :].bitcast(F32), ALU.subtract).then_inc(hT_kept, 1)

        split_down(0, 0)
        hidden(0)
        keep_hT(0)
        hidden(1)
        n_tiles = tiles(dve)
        with dve.Fori(2, n_tiles) as t:
            split_down(t - 1, (t - 1) % WRING)
            keep_hT(t - 1)
            hidden(t)
        last = last_tile(dve)
        split_down(last, last % WRING)
        keep_hT(last)


def combine(nc, A, g, st, sb, sem, n_stores):
    B = 3
    y1 = [sb(st, f"y1_{i}", [P, D]) for i in range(B)]
    y2 = [sb(st, f"y2_{i}", [P, D]) for i in range(B)]
    gfin = sb(st, "gfin", [P, D])
    o = [sb(st, f"o{i}", [P, D]) for i in range(2)]
    junk = sb(st, "junk3", [P, D], BF16)
    ss = sb(st, "ss3", [P, NT])
    rs = sb(st, "rs3", [P, NT])
    nh = sb(st, "nh3", [P, 1])
    g_in = sem(st, "gfin_in")
    y1_in = [sem(st, f"y1_in{i}") for i in range(B)]
    y2_in = [sem(st, f"y2_in{i}") for i in range(B)]
    added, summed, squared, rs_ready, o_ready = (sem(st, n) for n in ("c_add", "c_sum", "c_sq", "c_rs", "c_o"))
    ms_ready, nh_ready = sem(st, "c_ms"), sem(st, "c_nh")
    o_stored = [sem(st, f"o_stored{i}") for i in range(2)]
    blk = st.enter_context(nc.Block())
    y_rows = A["y_prompt"].rearrange("a s d -> (a s) d")
    ys_rows = A["y_sample"].rearrange("a s d -> (a s) d")

    @blk.sync
    def _(sp):
        for t in range(NT):
            m = rows_of(t)
            if t >= B:
                sp.wait_ge(summed, t - B + 1)
            for j, (dst, done) in enumerate(((y1, y1_in), (y2, y2_in))):
                sp.dma_start(dst[t % B][0:m, :], g["ysd"][NTOK * j + P * t:NTOK * j + P * t + m, :]) \
                    .then_inc(done[t % B], 16)
            if t == 0:
                sp.dma_start(gfin[:, :], A["final_norm_g"].rearrange("(o d) -> o d", o=1).broadcast_to([P, D])) \
                    .then_inc(g_in, 16)

    @blk.gpsimd
    def _(pool):
        nc.gpsimd.memset(nh[:, :], -0.5).then_inc(nh_ready, 1)
        pool.wait_ge(nh_ready, 1)

        def root(t):
            m = rows_of(t)
            pool.wait_ge(squared, t + 1)
            nc.gpsimd.tensor_scalar(ss[0:m, t:t + 1], ss[0:m, t:t + 1], 1.0 / D, EPS, ALU.mult, ALU.add) \
                .then_inc(ms_ready, 1)
            pool.wait_ge(ms_ready, t + 1)
            nc.gpsimd.tensor_tensor(rs[0:m, t:t + 1], ss[0:m, t:t + 1], nh[0:m, :], ALU.pow).then_inc(rs_ready, 1)

        def store(t):
            pool.wait_ge(o_ready, t + 1)
            r = o[t % 2]
            if t == 0:
                pool.dma_start(y_rows[0:P - META, :], r[META:P, :]).then_inc(o_stored[0], 16)
            elif t < FULL:
                pool.dma_start(y_rows[P * t - META:P * t + P - META, :], r[:, :]).then_inc(o_stored[t % 2], 16)
            else:
                pool.dma_start(ys_rows, r[0:NS, :]).then_inc(o_stored[t % 2], 16)
                pool.dma_start(y_rows[SEQ - TAIL:SEQ, :], r[NS:LAST, :]).then_inc(o_stored[t % 2], 16)

        for t in range(NT):
            root(t)
            if t >= 1:
                store(t - 1)
        store(NT - 1)
        pool.wait_ge(o_stored[0], 16 * 6)
        pool.wait_ge(o_stored[1], 16 * 4)
        pool.wait_ge(g["stores"], 16 * n_stores[0])

    @blk.vector
    def _(dve):
        def finish(t):
            m = rows_of(t)
            if t == 0:
                dve.wait_ge(g_in, 16)
            dve.wait_ge(rs_ready, t + 1)
            if t >= 2:
                dve.wait_ge(o_stored[t % 2], 16 * (t // 2))
            nc.vector.scalar_tensor_tensor(o[t % 2][0:m, :], g["h"][0:m, t, :], rs[0:m, t:t + 1], gfin[0:m, :],
                                           ALU.mult, ALU.mult).then_inc(o_ready, 1)

        for t in range(NT):
            m = rows_of(t)
            ht = g["h"][0:m, t, :]
            dve.wait_ge(y1_in[t % B], 16 * (t // B + 1))
            nc.vector.scalar_tensor_tensor(ht, y1[t % B][0:m, :], g["gates"][0:m, t, 0:1], ht, ALU.mult, ALU.add) \
                .then_inc(added, 1)
            dve.wait_ge(added, t + 1)
            dve.wait_ge(y2_in[t % B], 16 * (t // B + 1))
            nc.vector.scalar_tensor_tensor(ht, y2[t % B][0:m, :], g["gates"][0:m, t, 1:2], ht, ALU.mult, ALU.add) \
                .then_inc(summed, 1)
            if t >= 1:
                finish(t - 1)
        finish(NT - 1)

    @blk.scalar
    def _(act):
        for t in range(NT):
            m = rows_of(t)
            act.wait_ge(summed, t + 1)
            if t >= 1:
                act.wait_ge(squared, t)
            nc.scalar.activation(junk[0:m, :], g["h"][0:m, t, :], ACT.Square,
                                 accum_out=ss[0:m, t:t + 1]).then_inc(squared, 1)


INS = ["x_prompt", "x_sample", "cache_sb_k", "cache_sb_v", "cache_diff_k", "cache_diff_v", "meta_tokens",
       "norm_mix_g", "w_in", "lambda_q1", "lambda_k1", "lambda_q2", "lambda_k2", "subln_g", "w_out", "norm_ffn_g",
       "w_group", "b_group", "w_router", "b_router", "w_gate", "w_up", "w_down", "final_norm_g"]
OUTS = [("y_prompt", (1, SEQ, D)), ("y_sample", (1, NS, D)),
        ("sb_k_prompt", (1, 1, NPR, SBH, SBD)), ("sb_v_prompt", (1, 1, NPR, SBH, SBD)),
        ("diff_k_prompt", (1, 1, NPR, 2 * DFH, DFD)), ("diff_v_prompt", (1, 1, NPR, DFH, DFV)),
        ("sb_k_sample", (1, 1, NS, SBH, SBD)), ("sb_v_sample", (1, 1, NS, SBH, SBD)),
        ("diff_k_sample", (1, 1, NS, 2 * DFH, DFD)), ("diff_v_sample", (1, 1, NS, DFH, DFV))]


def kernel(**inputs):
    import concourse.bacc as bacc
    from concourse.bass_utils import run_bass_kernel_spmd

    nc = bacc.Bacc("TRN2", target_bir_lowering=False, num_devices=1)
    arrays, aps = {}, {}
    for name in INS:
        a = np.ascontiguousarray(inputs[name])
        arrays[f"in_{name}"] = a
        aps[name] = nc.dram_tensor(f"in_{name}", a.shape, mybir.dt.from_np(a.dtype), kind="ExternalInput").ap()
    const = np.concatenate(list(shape_constants().values()), axis=1)
    arrays["in_const"] = const
    aps["const"] = nc.dram_tensor("in_const", const.shape, F32, kind="ExternalInput").ap()
    for name, shape in OUTS:
        aps[name] = nc.dram_tensor(f"out_{name}", shape, F32, kind="ExternalOutput").ap()
    build(nc, aps)
    r = run_bass_kernel_spmd(nc, [arrays], core_ids=[0])
    return tuple(r.results[0][f"out_{name}"] for name, _ in OUTS)
```
